# Optimizing a Trainium2 kernel written in Bass

```python
import math
import jax, jax.numpy as jnp
from jax import lax
import numpy as np
import jax
import jax.numpy as jnp

D_MODEL = 1024
BATCH = 1
SEQ = 512
DEPTH = 2

GRID_W = 64
CTX_LEN = 256
N_EVEN = (DEPTH + 1) // 2
N_ODD = DEPTH // 2
EPS = 1e-6

ROPE_HEAD_DIM = 64
ROPE_FREQS = ROPE_HEAD_DIM // 4
ROPE_BASE = 10000.0

SC_WIDTH = D_MODEL // 2
DA_HEADS = 4
DA_HEAD_DIM = ROPE_HEAD_DIM
DA_V_DIM = 2 * DA_HEAD_DIM
DA_QK_WIDTH = DA_HEADS * 2 * DA_HEAD_DIM
DA_WIDTH = DA_HEADS * DA_V_DIM
Q_BLOCK = 128
EVEN_SPLITS = (SC_WIDTH, 2 * SC_WIDTH, 3 * SC_WIDTH, 3 * SC_WIDTH + DA_QK_WIDTH, 3 * SC_WIDTH + 2 * DA_QK_WIDTH)
EVEN_IN = 3 * SC_WIDTH + 2 * DA_QK_WIDTH + DA_WIDTH
EVEN_OUT = SC_WIDTH + DA_WIDTH

POOL_WINDOWS = (2, 4, 8, 16)
POOL_RADII = tuple(w // 2 for w in POOL_WINDOWS)
POOL_GROUPS = 4
POOL_WIDTH = D_MODEL // 2
POOL_GROUP_DIM = POOL_WIDTH // POOL_GROUPS
RET_HEADS = 4
RET_QK_DIM = ROPE_HEAD_DIM
RET_V_DIM = 2 * RET_QK_DIM
RET_QK_WIDTH = RET_HEADS * RET_QK_DIM
RET_WIDTH = RET_HEADS * RET_V_DIM
RET_CHUNK = 128
ODD_SPLITS = (POOL_WIDTH, POOL_WIDTH + RET_QK_WIDTH, POOL_WIDTH + 2 * RET_QK_WIDTH, POOL_WIDTH + 2 * RET_QK_WIDTH + RET_WIDTH)
ODD_IN = POOL_WIDTH + 2 * RET_QK_WIDTH + 2 * RET_WIDTH
ODD_OUT = POOL_WIDTH + RET_WIDTH

FFN_DIM = 2816


def rms_norm(x, g):
    xf = x.astype(jnp.float32)
    y = xf * lax.rsqrt(jnp.mean(xf * xf, axis=-1, keepdims=True) + EPS)
    return (y * g.astype(jnp.float32)).astype(x.dtype)

def modulate(h, shift, scale):
    return h * (1 + scale) + shift

def dwconv3(x, w):
    xp = jnp.pad(x, ((0, 0), (1, 1), (0, 0)))
    return xp[:, :-2] * w[0] + xp[:, 1:-1] * w[1] + xp[:, 2:] * w[2]

def rope_tables(rows):
    row = jnp.repeat(jnp.arange(rows, dtype=jnp.float32), GRID_W)
    col = jnp.tile(jnp.arange(GRID_W, dtype=jnp.float32), rows)
    inv = ROPE_BASE ** (-jnp.arange(ROPE_FREQS, dtype=jnp.float32) / ROPE_FREQS)
    ang = jnp.stack([row[:, None] * inv, col[:, None] * inv], axis=1)
    return jnp.cos(ang), jnp.sin(ang)

def apply_rope(x, cos, sin):
    shp = x.shape
    xr = x.reshape(*shp[:-1], 2, 2, ROPE_FREQS)
    bc = (shp[1],) + (1,) * (x.ndim - 3) + (2, ROPE_FREQS)
    c = cos.reshape(bc).astype(x.dtype)
    s = sin.reshape(bc).astype(x.dtype)
    x1, x2 = xr[..., 0, :], xr[..., 1, :]
    out = jnp.stack([x1 * c - x2 * s, x1 * s + x2 * c], axis=-2)
    return out.reshape(shp)

def conv_ffn(h, w_up, conv_w, conv_b, w_down):
    a, b = jnp.split(h @ w_up, 2, axis=-1)
    a = dwconv3(a, conv_w) + conv_b
    return (jax.nn.silu(a) * b) @ w_down

def diff_lambda_init(layer_idx):
    return 0.8 - 0.6 * math.exp(-0.3 * layer_idx)

def diff_attend(q, k, v, lam):
    s = jnp.einsum('bhmqd,bhmkd->bhmqk', q, k).astype(jnp.float32) * (DA_HEAD_DIM ** -0.5)
    p = jax.nn.softmax(s, axis=-1)
    p = p[:, :, 0] - lam * p[:, :, 1]
    return jnp.einsum('bhqk,bhkv->bhqv', p.astype(v.dtype), v)

def conv_diff_mixer(h_ctx, h_lat, w_in, w_out, sc_conv_w, q_g, k_g, lq1, lk1, lq2, lk2, subln_g, lam_init, cos, sin):
    f32 = jnp.float32
    lam = (jnp.exp(jnp.sum(lq1.astype(f32) * lk1.astype(f32)))
           - jnp.exp(jnp.sum(lq2.astype(f32) * lk2.astype(f32))) + lam_init)

    def project(h, rotate):
        b_g, c_g, xv, q, k, v = jnp.split(h @ w_in, EVEN_SPLITS, axis=-1)
        B_, N = h.shape[:2]
        q = rms_norm(q.reshape(B_, N, DA_HEADS, 2, DA_HEAD_DIM), q_g)
        k = rms_norm(k.reshape(B_, N, DA_HEADS, 2, DA_HEAD_DIM), k_g)
        if rotate:
            q = apply_rope(q, cos, sin)
            k = apply_rope(k, cos, sin)
        q = q.transpose(0, 2, 3, 1, 4)
        k = k.transpose(0, 2, 3, 1, 4)
        v = v.reshape(B_, N, DA_HEADS, DA_V_DIM).transpose(0, 2, 1, 3)
        return (b_g, c_g, xv), q, k, v

    def finish(gates, o):
        b_g, c_g, xv = gates
        y_conv = b_g * dwconv3(c_g * xv, sc_conv_w)
        B_, _, N, _ = o.shape
        o = rms_norm(o.transpose(0, 2, 1, 3), subln_g) * (1.0 - lam_init)
        return jnp.concatenate([y_conv, o.reshape(B_, N, DA_WIDTH).astype(y_conv.dtype)], axis=-1) @ w_out

    gates_c, qc, kc, vc = project(h_ctx, False)
    gates_l, ql, kl, vl = project(h_lat, True)
    k_all = jnp.concatenate([kl, kc], axis=3)
    v_all = jnp.concatenate([vl, vc], axis=2)
    B_, H, _, N, d = ql.shape
    nb = N // Q_BLOCK
    q_blocks = jnp.moveaxis(ql.reshape(B_, H, 2, nb, Q_BLOCK, d), 3, 0)
    o_blocks = lax.map(lambda qb: diff_attend(qb, k_all, v_all, lam), q_blocks)
    o_lat = jnp.moveaxis(o_blocks, 0, 2).reshape(B_, H, N, DA_V_DIM)
    y_lat = finish(gates_l, o_lat)
    y_ctx = finish(gates_c, diff_attend(qc, kc, vc, lam))
    return y_ctx, y_lat

def multiscale_pool(v, pool_w, pool_scale):
    B_, N, _ = v.shape
    vg = v.reshape(B_, N, POOL_GROUPS, POOL_GROUP_DIM).astype(jnp.float32)
    cs = jnp.concatenate([jnp.zeros_like(vg[:, :1]), jnp.cumsum(vg, axis=1)], axis=1)
    t = jnp.arange(N)[:, None]
    r = jnp.array(POOL_RADII)[None, :]
    lo = jnp.clip(t - r, 0, N)
    hi = jnp.clip(t + r + 1, 0, N)
    g = jnp.arange(POOL_GROUPS)[None, :]
    mean = (cs[:, hi, g] - cs[:, lo, g]) / (hi - lo).astype(jnp.float32)[:, :, None]
    y = (mean - vg).astype(v.dtype)
    y = jnp.einsum('bngc,gcd->bngd', y, pool_w)
    return y.reshape(B_, N, POOL_WIDTH) * pool_scale

def retention_scan(q, k, v, lg, s0):
    B_, H, N, _ = q.shape
    dv = v.shape[-1]
    nc = N // RET_CHUNK

    def chunks(t):
        return jnp.moveaxis(t.reshape(B_, H, nc, RET_CHUNK, t.shape[-1]), 2, 0)

    pos = jnp.arange(RET_CHUNK, dtype=jnp.float32)
    diff = pos[:, None] - pos[None, :]
    intra = jnp.where(diff >= 0, jnp.exp(lg[:, None, None] * jnp.maximum(diff, 0.0)), 0.0)
    q_dec = jnp.exp(lg[:, None] * (pos + 1.0))[None, :, :, None]
    k_dec = jnp.exp(lg[:, None] * (RET_CHUNK - 1.0 - pos))[None, :, :, None]
    c_dec = jnp.exp(lg * RET_CHUNK)[None, :, None, None]

    def step(s, qkv):
        qc, kc, vc = qkv
        att = jnp.einsum('bhid,bhjd->bhij', qc, kc) * intra
        o = jnp.einsum('bhij,bhjv->bhiv', att, vc) + jnp.einsum('bhid,bhdv->bhiv', qc * q_dec, s)
        s = s * c_dec + jnp.einsum('bhjd,bhjv->bhdv', kc * k_dec, vc)
        return s, o

    _, o = lax.scan(step, s0, (chunks(q), chunks(k), chunks(v)))
    return jnp.moveaxis(o, 0, 2).reshape(B_, H, N, dv)

def retention_bidir(q, k, v, lg_f, lg_b, s_f, s_b):
    o_f = retention_scan(q, k, v, lg_f, s_f)
    flip = lambda t: jnp.flip(t, axis=2)
    o_b = flip(retention_scan(flip(q), flip(k), flip(v), lg_b, s_b))
    return o_f + o_b

def context_states(k, v, lg_f, lg_b):
    L = k.shape[2]
    j = jnp.arange(L, dtype=jnp.float32)
    w_f = jnp.exp(lg_f[:, None] * (L - 1.0 - j))
    w_b = jnp.exp(lg_b[:, None] * j)
    s_f = jnp.einsum('bhjd,hj,bhjv->bhdv', k, w_f, v)
    s_b = jnp.einsum('bhjd,hj,bhjv->bhdv', k, w_b, v)
    return s_f, s_b

def pool_retention_mixer(h_ctx, h_lat, w_in, w_out, pool_w, pool_scale, dec_f, dec_b, gn_g, cos, sin, with_ctx):
    f32 = jnp.float32
    lg_f = -jnp.exp(dec_f.astype(f32))
    lg_b = -jnp.exp(dec_b.astype(f32))

    def heads(t, dh):
        B_, N = t.shape[:2]
        return t.reshape(B_, N, RET_HEADS, dh)

    def qkv_heads(q, k, v, rotate):
        q, k, v = heads(q, RET_QK_DIM), heads(k, RET_QK_DIM), heads(v, RET_V_DIM)
        if rotate:
            q = apply_rope(q, cos, sin)
            k = apply_rope(k, cos, sin)
        q = (q.astype(f32) * (RET_QK_DIM ** -0.5)).transpose(0, 2, 1, 3)
        k = k.astype(f32).transpose(0, 2, 1, 3)
        v = v.astype(f32).transpose(0, 2, 1, 3)
        return q, k, v

    def finish(pv, g, o):
        B_, _, N, _ = o.shape
        y_r = rms_norm(o.transpose(0, 2, 1, 3), gn_g).reshape(B_, N, RET_WIDTH).astype(g.dtype) * jax.nn.silu(g)
        y_p = multiscale_pool(pv, pool_w, pool_scale)
        return jnp.concatenate([y_p, y_r], axis=-1) @ w_out

    pv_l, q_l, k_l, v_l, g_l = jnp.split(h_lat @ w_in, ODD_SPLITS, axis=-1)
    ql, kl, vl = qkv_heads(q_l, k_l, v_l, True)
    if with_ctx:
        pv_c, q_c, k_c, v_c, g_c = jnp.split(h_ctx @ w_in, ODD_SPLITS, axis=-1)
        qc, kc, vc = qkv_heads(q_c, k_c, v_c, False)
    else:
        k_c, v_c = jnp.split(h_ctx @ w_in[:, ODD_SPLITS[1]:ODD_SPLITS[3]], [RET_QK_WIDTH], axis=-1)
        kc = heads(k_c, RET_QK_DIM).astype(f32).transpose(0, 2, 1, 3)
        vc = heads(v_c, RET_V_DIM).astype(f32).transpose(0, 2, 1, 3)
    s_f, s_b = context_states(kc, vc, lg_f, lg_b)
    y_lat = finish(pv_l, g_l, retention_bidir(ql, kl, vl, lg_f, lg_b, s_f, s_b))
    y_ctx = None
    if with_ctx:
        zero = jnp.zeros_like(s_f)
        y_ctx = finish(pv_c, g_c, retention_bidir(qc, kc, vc, lg_f, lg_b, zero, zero))
    return y_ctx, y_lat

def first_inputs(seed: int = 0) -> dict:
    key = jax.random.key(seed)
    ks = iter(jax.random.split(key, 40))

    def nrm(shape, scale=1.0):
        return scale * jax.random.normal(next(ks), shape, jnp.float32)

    def gain(shape):
        return 1.0 + nrm(shape, 0.05)

    base_decay = jnp.log(-jnp.log1p(-(2.0 ** (-5.0 - jnp.arange(RET_HEADS, dtype=jnp.float32)))))
    return {
        'x': nrm((BATCH, SEQ, D_MODEL)),
        'c': nrm((BATCH, D_MODEL)),
        'ctx': nrm((BATCH, CTX_LEN, D_MODEL)),
        'c_ctx': nrm((D_MODEL,)),
        'mod_w': nrm((DEPTH, D_MODEL, 6 * D_MODEL), 0.5 * D_MODEL ** -0.5),
        'mod_b': nrm((DEPTH, 6 * D_MODEL), 0.01),
        'norm1_g': gain((DEPTH, D_MODEL)),
        'norm2_g': gain((DEPTH, D_MODEL)),
        'ev_w_in': nrm((N_EVEN, D_MODEL, EVEN_IN), D_MODEL ** -0.5),
        'ev_w_out': nrm((N_EVEN, EVEN_OUT, D_MODEL), EVEN_OUT ** -0.5),
        'sc_conv_w': nrm((N_EVEN, 3, SC_WIDTH), 3 ** -0.5),
        'da_q_norm': gain((N_EVEN, DA_HEAD_DIM)),
        'da_k_norm': gain((N_EVEN, DA_HEAD_DIM)),
        'da_lq1': nrm((N_EVEN, DA_HEAD_DIM), 0.1),
        'da_lk1': nrm((N_EVEN, DA_HEAD_DIM), 0.1),
        'da_lq2': nrm((N_EVEN, DA_HEAD_DIM), 0.1),
        'da_lk2': nrm((N_EVEN, DA_HEAD_DIM), 0.1),
        'da_subln_g': gain((N_EVEN, DA_V_DIM)),
        'od_w_in': nrm((N_ODD, D_MODEL, ODD_IN), D_MODEL ** -0.5),
        'od_w_out': nrm((N_ODD, ODD_OUT, D_MODEL), ODD_OUT ** -0.5),
        'pool_w': nrm((N_ODD, POOL_GROUPS, POOL_GROUP_DIM, POOL_GROUP_DIM), POOL_GROUP_DIM ** -0.5),
        'pool_scale': gain((N_ODD, POOL_WIDTH)),
        'ret_decay_f': base_decay + nrm((N_ODD, RET_HEADS), 0.1),
        'ret_decay_b': base_decay + nrm((N_ODD, RET_HEADS), 0.1),
        'ret_gn_g': gain((N_ODD, RET_V_DIM)),
        'ffn_w_up': nrm((DEPTH, D_MODEL, 2 * FFN_DIM), D_MODEL ** -0.5),
        'ffn_conv_w': nrm((DEPTH, 3, FFN_DIM), 3 ** -0.5),
        'ffn_conv_b': nrm((DEPTH, FFN_DIM), 0.01),
        'ffn_w_down': nrm((DEPTH, FFN_DIM, D_MODEL), FFN_DIM ** -0.5),
    }

def first_block(x, c, ctx, c_ctx, mod_w, mod_b, norm1_g, norm2_g, ev_w_in, ev_w_out, sc_conv_w, da_q_norm, da_k_norm,
              da_lq1, da_lk1, da_lq2, da_lk2, da_subln_g, od_w_in, od_w_out, pool_w, pool_scale, ret_decay_f,
              ret_decay_b, ret_gn_g, ffn_w_up, ffn_conv_w, ffn_conv_b, ffn_w_down):
    ROWS = x.shape[1] // GRID_W
    cos, sin = rope_tables(ROWS)
    silu_c = jax.nn.silu(c)
    silu_cc = jax.nn.silu(c_ctx)
    for i in range(DEPTH):
        last = i == DEPTH - 1
        j = i // 2
        mod_l = (silu_c @ mod_w[i] + mod_b[i])[:, None, :]
        mod_c = silu_cc @ mod_w[i] + mod_b[i]
        sh1, sc1, g1, sh2, sc2, g2 = jnp.split(mod_l, 6, axis=-1)
        sh1c, sc1c, g1c, sh2c, sc2c, g2c = jnp.split(mod_c, 6, axis=-1)
        h_lat = modulate(rms_norm(x, norm1_g[i]), sh1, sc1)
        h_ctx = modulate(rms_norm(ctx, norm1_g[i]), sh1c, sc1c)
        if i % 2 == 0:
            y_ctx, y_lat = conv_diff_mixer(h_ctx, h_lat, ev_w_in[j], ev_w_out[j], sc_conv_w[j], da_q_norm[j],
                                           da_k_norm[j], da_lq1[j], da_lk1[j], da_lq2[j], da_lk2[j],
                                           da_subln_g[j], diff_lambda_init(i), cos, sin)
        else:
            y_ctx, y_lat = pool_retention_mixer(h_ctx, h_lat, od_w_in[j], od_w_out[j], pool_w[j], pool_scale[j],
                                                ret_decay_f[j], ret_decay_b[j], ret_gn_g[j], cos, sin, not last)
        x = x + g1 * y_lat
        x = x + g2 * conv_ffn(modulate(rms_norm(x, norm2_g[i]), sh2, sc2),
                              ffn_w_up[i], ffn_conv_w[i], ffn_conv_b[i], ffn_w_down[i])
        if not last:
            ctx = ctx + g1c * y_ctx
            ctx = ctx + g2c * conv_ffn(modulate(rms_norm(ctx, norm2_g[i]), sh2c, sc2c),
                                       ffn_w_up[i], ffn_conv_w[i], ffn_conv_b[i], ffn_w_down[i])
    return x


N_MIXERS = 2
N_META = 16
BLOCK = 128
NEG_INF = -1e30

FOX_HEADS = 16
FOX_HEAD_DIM = D_MODEL // FOX_HEADS
FOX_IN = 3 * D_MODEL + FOX_HEADS
FOX_FORGET_BIAS = 2.0

HG_HEADS = 8
HG_KEY_DIM = 128
HG_VAL_DIM = D_MODEL // HG_HEADS
HG_KEY_TOTAL = HG_HEADS * HG_KEY_DIM
HG_IN = 2 * HG_KEY_TOTAL + 2 * D_MODEL

N_GROUPS = 4
EXPERTS_PER_GROUP = 8
N_EXPERTS = N_GROUPS * EXPERTS_PER_GROUP
TOP_K = 2
D_EXPERT = D_MODEL // 2
EXPERT_ROW_BLOCK = 128


def rms_norm_2(x, gain):
    xf = x.astype(jnp.float32)
    y = xf * lax.rsqrt(jnp.mean(xf * xf, axis=-1, keepdims=True) + EPS)
    return (y * gain.astype(jnp.float32)).astype(x.dtype)

def front_pad(t, pad):
    widths = [(0, 0)] * t.ndim
    widths[1] = (pad, 0)
    return jnp.pad(t, widths)

def fox_attention(h, w_in, b_f, g_q, g_k, w_out):
    bsz, length, _ = h.shape
    q, k, v, f_logit = jnp.split(h @ w_in, [D_MODEL, 2 * D_MODEL, 3 * D_MODEL], axis=-1)
    q = rms_norm_2(q.reshape(bsz, length, FOX_HEADS, FOX_HEAD_DIM), g_q)
    k = rms_norm_2(k.reshape(bsz, length, FOX_HEADS, FOX_HEAD_DIM), g_k)
    v = v.reshape(bsz, length, FOX_HEADS, FOX_HEAD_DIM)
    log_f = jax.nn.log_sigmoid(f_logit.astype(jnp.float32) + b_f.astype(jnp.float32))
    pad = (-length) % BLOCK
    q, k, v, log_f = (front_pad(t, pad) for t in (q, k, v, log_f))
    lp = length + pad
    n_blk = lp // BLOCK
    cum = jnp.cumsum(log_f, axis=1).transpose(0, 2, 1)
    kh = k.transpose(0, 2, 1, 3)
    vh = v.transpose(0, 2, 1, 3)
    qb = q.reshape(bsz, n_blk, BLOCK, FOX_HEADS, FOX_HEAD_DIM).transpose(1, 0, 3, 2, 4)
    cb = cum.reshape(bsz, FOX_HEADS, n_blk, BLOCK).transpose(2, 0, 1, 3)
    key_pos = jnp.arange(lp)
    key_ok = key_pos >= pad
    scale = FOX_HEAD_DIM ** -0.5

    def attend(args):
        qi, ci, bi = args
        s = jnp.einsum('bhqd,bhkd->bhqk', qi, kh).astype(jnp.float32) * scale
        s = s + ci[..., :, None] - cum[:, :, None, :]
        q_pos = bi * BLOCK + jnp.arange(BLOCK)
        mask = (key_pos[None, :] <= q_pos[:, None]) & key_ok[None, :]
        p = jax.nn.softmax(jnp.where(mask, s, NEG_INF), axis=-1)
        return jnp.einsum('bhqk,bhkd->bhqd', p.astype(vh.dtype), vh)

    o = lax.map(attend, (qb, cb, jnp.arange(n_blk)))
    o = o.transpose(1, 0, 3, 2, 4).reshape(bsz, lp, D_MODEL)[:, pad:]
    return o @ w_out

def hgrn_lower_bounds(lb_logits):
    p = jax.nn.softmax(lb_logits.astype(jnp.float32), axis=0)
    cum = jnp.cumsum(p, axis=0)
    return cum - cum[:1]

def hgrn2_recurrence(h, w_in, b_f, lower_bound, g_o, w_out):
    bsz, length, _ = h.shape
    q, f_logit, v, g = jnp.split(
        h @ w_in, [HG_KEY_TOTAL, 2 * HG_KEY_TOTAL, 2 * HG_KEY_TOTAL + D_MODEL], axis=-1)
    f = lower_bound + (1.0 - lower_bound) * jax.nn.sigmoid(
        f_logit.astype(jnp.float32) + b_f.astype(jnp.float32))
    log_f = jnp.log(f)
    k = 1.0 - f
    q = jax.nn.silu(q.astype(jnp.float32))
    v = v.astype(jnp.float32)
    pad = (-length) % BLOCK
    lp = length + pad
    n_chk = lp // BLOCK

    def to_chunks(t, d):
        t = front_pad(t, pad).reshape(bsz, n_chk, BLOCK, HG_HEADS, d)
        return t.transpose(1, 0, 3, 2, 4)

    qc = to_chunks(q, HG_KEY_DIM)
    kc = to_chunks(k, HG_KEY_DIM)
    vc = to_chunks(v, HG_VAL_DIM)
    lc = to_chunks(log_f, HG_KEY_DIM)
    causal = jnp.tril(jnp.ones((BLOCK, BLOCK), dtype=bool))

    def step(state, args):
        qi, ki, vi, li = args
        b = jnp.cumsum(li, axis=2)
        o_inter = jnp.einsum('bhtk,bhkv->bhtv', qi * jnp.exp(b), state)
        diff = b[:, :, :, None, :] - b[:, :, None, :, :]
        decay = jnp.exp(jnp.where(causal[:, :, None], diff, -jnp.inf))
        scores = jnp.einsum('bhtk,bhsk,bhtsk->bhts', qi, ki, decay)
        o_intra = jnp.einsum('bhts,bhsv->bhtv', scores, vi)
        b_end = b[:, :, -1:, :]
        state = (jnp.exp(b_end[:, :, 0, :])[..., None] * state
                 + jnp.einsum('bhsk,bhsv->bhkv', ki * jnp.exp(b_end - b), vi))
        return state, o_inter + o_intra

    s0 = jnp.zeros((bsz, HG_HEADS, HG_KEY_DIM, HG_VAL_DIM), jnp.float32)
    _, o = lax.scan(step, s0, (qc, kc, vc, lc))
    o = o.transpose(1, 0, 3, 2, 4).reshape(bsz, lp, HG_HEADS, HG_VAL_DIM)[:, pad:]
    o = rms_norm_2(o, g_o).reshape(bsz, length, D_MODEL) * jax.nn.silu(g.astype(jnp.float32))
    return o.astype(h.dtype) @ w_out

def hier_moe(h, w_grp, b_grp, w_rt, b_rt, w_up, w_down):
    bsz, length, dm = h.shape
    n_tok = bsz * length
    n_asg = n_tok * TOP_K
    xt = h.reshape(n_tok, dm)
    g_prob = jax.nn.softmax((xt @ w_grp).astype(jnp.float32) + b_grp.astype(jnp.float32), axis=-1)
    g_gate, g_idx = lax.top_k(g_prob, 1)
    e_logit = ((xt @ w_rt).astype(jnp.float32) + b_rt.astype(jnp.float32)).reshape(
        n_tok, N_GROUPS, EXPERTS_PER_GROUP)
    e_logit = jnp.take_along_axis(e_logit, g_idx[:, :, None], axis=1)[:, 0]
    e_val, e_idx = lax.top_k(e_logit, TOP_K)
    gate = jax.nn.softmax(e_val, axis=-1) * g_gate
    expert = (g_idx * EXPERTS_PER_GROUP + e_idx).reshape(-1)
    order = jnp.argsort(expert)
    se = expert[order]
    tok = order // TOP_K
    w_sorted = gate.reshape(-1)[order]
    counts = jnp.bincount(expert, length=N_EXPERTS)
    padded = (counts + EXPERT_ROW_BLOCK - 1) // EXPERT_ROW_BLOCK * EXPERT_ROW_BLOCK
    start = jnp.cumsum(counts) - counts
    pend = jnp.cumsum(padded)
    pstart = pend - padded
    dest = pstart[se] + jnp.arange(n_asg) - start[se]
    n_blocks = (n_asg + N_EXPERTS * (EXPERT_ROW_BLOCK - 1) + EXPERT_ROW_BLOCK - 1) // EXPERT_ROW_BLOCK
    rows = n_blocks * EXPERT_ROW_BLOCK
    x_pad = jnp.zeros((rows, dm), h.dtype).at[dest].set(xt[tok])
    block_expert = jnp.minimum(
        jnp.searchsorted(pend, jnp.arange(n_blocks) * EXPERT_ROW_BLOCK, side='right'), N_EXPERTS - 1)

    def expert_block(args):
        xb, e = args
        gate_up = xb @ w_up[e]
        a, u = jnp.split(gate_up, 2, axis=-1)
        return (jax.nn.silu(a) * u) @ w_down[e]

    y_pad = lax.map(expert_block, (x_pad.reshape(n_blocks, EXPERT_ROW_BLOCK, dm), block_expert))
    y = y_pad.reshape(rows, dm)[dest] * w_sorted[:, None].astype(h.dtype)
    return jnp.zeros_like(xt).at[tok].add(y).reshape(bsz, length, dm)

def second_inputs(seed: int = 0) -> dict:
    key = jax.random.key(seed)
    ks = jax.random.split(key, 24)
    n_fox = (DEPTH + N_MIXERS - 1) // N_MIXERS
    n_hg = DEPTH // N_MIXERS
    out_scale = (2 * DEPTH) ** -0.5

    def nrm(k, shape, scale):
        return jax.random.normal(k, shape, jnp.float32) * scale

    def gain(k, shape):
        return 1.0 + nrm(k, shape, 0.02)

    return {
        'x': nrm(ks[0], (BATCH, SEQ, D_MODEL), 1.0),
        'meta_tokens': nrm(ks[1], (N_META, D_MODEL), 1.0),
        'fox_norm': gain(ks[2], (n_fox, D_MODEL)),
        'fox_w_in': nrm(ks[3], (n_fox, D_MODEL, FOX_IN), D_MODEL ** -0.5),
        'fox_b_f': FOX_FORGET_BIAS + nrm(ks[4], (n_fox, FOX_HEADS), 0.1),
        'fox_q_norm': gain(ks[5], (n_fox, FOX_HEAD_DIM)),
        'fox_k_norm': gain(ks[6], (n_fox, FOX_HEAD_DIM)),
        'fox_w_out': nrm(ks[7], (n_fox, D_MODEL, D_MODEL), D_MODEL ** -0.5 * out_scale),
        'hg_norm': gain(ks[8], (n_hg, D_MODEL)),
        'hg_w_in': nrm(ks[9], (n_hg, D_MODEL, HG_IN), D_MODEL ** -0.5),
        'hg_b_f': nrm(ks[10], (n_hg, HG_KEY_TOTAL), 0.02),
        'hg_lb_logits': nrm(ks[11], (DEPTH, HG_KEY_TOTAL), 0.5),
        'hg_o_norm': gain(ks[12], (n_hg, HG_VAL_DIM)),
        'hg_w_out': nrm(ks[13], (n_hg, D_MODEL, D_MODEL), D_MODEL ** -0.5 * out_scale),
        'moe_norm': gain(ks[14], (DEPTH, D_MODEL)),
        'moe_w_grp': nrm(ks[15], (DEPTH, D_MODEL, N_GROUPS), D_MODEL ** -0.5),
        'moe_b_grp': nrm(ks[16], (DEPTH, N_GROUPS), 0.01),
        'moe_w_rt': nrm(ks[17], (DEPTH, D_MODEL, N_EXPERTS), D_MODEL ** -0.5),
        'moe_b_rt': nrm(ks[18], (DEPTH, N_EXPERTS), 0.01),
        'moe_w_up': nrm(ks[19], (DEPTH, N_EXPERTS, D_MODEL, 2 * D_EXPERT), D_MODEL ** -0.5),
        'moe_w_down': nrm(ks[20], (DEPTH, N_EXPERTS, D_EXPERT, D_MODEL), D_EXPERT ** -0.5 * out_scale),
    }

def second_block(x, meta_tokens, fox_norm, fox_w_in, fox_b_f, fox_q_norm, fox_k_norm, fox_w_out,
              hg_norm, hg_w_in, hg_b_f, hg_lb_logits, hg_o_norm, hg_w_out,
              moe_norm, moe_w_grp, moe_b_grp, moe_w_rt, moe_b_rt, moe_w_up, moe_w_down):
    bsz = x.shape[0]
    meta = jnp.broadcast_to(meta_tokens[None].astype(x.dtype), (bsz, N_META, D_MODEL))
    h = jnp.concatenate([meta, x], axis=1)
    lower_bounds = hgrn_lower_bounds(hg_lb_logits)
    for i in range(DEPTH):
        j = i // N_MIXERS
        if i % N_MIXERS == 0:
            h = h + fox_attention(rms_norm_2(h, fox_norm[j]), fox_w_in[j], fox_b_f[j],
                                  fox_q_norm[j], fox_k_norm[j], fox_w_out[j])
        else:
            h = h + hgrn2_recurrence(rms_norm_2(h, hg_norm[j]), hg_w_in[j], hg_b_f[j],
                                     lower_bounds[i], hg_o_norm[j], hg_w_out[j])
        h = h + hier_moe(rms_norm_2(h, moe_norm[i]), moe_w_grp[i], moe_b_grp[i],
                         moe_w_rt[i], moe_b_rt[i], moe_w_up[i], moe_w_down[i])
    return h[:, N_META:]


def setup_inputs(seed=0):
    out = dict(first_inputs(seed))
    for name, value in second_inputs(seed + 1).items():
        if name != "x":
            out[name + "_2"] = value
    return out


def reference(
    x, c, ctx, c_ctx, mod_w, mod_b, norm1_g, norm2_g, ev_w_in, ev_w_out, sc_conv_w, da_q_norm,
    da_k_norm, da_lq1, da_lk1, da_lq2, da_lk2, da_subln_g, od_w_in, od_w_out, pool_w,
    pool_scale, ret_decay_f, ret_decay_b, ret_gn_g, ffn_w_up, ffn_conv_w, ffn_conv_b,
    ffn_w_down, meta_tokens_2, fox_norm_2, fox_w_in_2, fox_b_f_2, fox_q_norm_2, fox_k_norm_2,
    fox_w_out_2, hg_norm_2, hg_w_in_2, hg_b_f_2, hg_lb_logits_2, hg_o_norm_2, hg_w_out_2,
    moe_norm_2, moe_w_grp_2, moe_b_grp_2, moe_w_rt_2, moe_b_rt_2, moe_w_up_2, moe_w_down_2,
):
    x = first_block(
        x, c, ctx, c_ctx, mod_w, mod_b, norm1_g, norm2_g, ev_w_in, ev_w_out, sc_conv_w,
        da_q_norm, da_k_norm, da_lq1, da_lk1, da_lq2, da_lk2, da_subln_g, od_w_in, od_w_out,
        pool_w, pool_scale, ret_decay_f, ret_decay_b, ret_gn_g, ffn_w_up, ffn_conv_w,
        ffn_conv_b, ffn_w_down,
    )
    return second_block(
        x, meta_tokens_2, fox_norm_2, fox_w_in_2, fox_b_f_2, fox_q_norm_2, fox_k_norm_2,
        fox_w_out_2, hg_norm_2, hg_w_in_2, hg_b_f_2, hg_lb_logits_2, hg_o_norm_2, hg_w_out_2,
        moe_norm_2, moe_w_grp_2, moe_b_grp_2, moe_w_rt_2, moe_b_rt_2, moe_w_up_2, moe_w_down_2,
    )


_drawn_inputs = setup_inputs


def setup_inputs(seed=0):
    import zlib

    import numpy as np

    out = dict(_drawn_inputs(seed))
    spreads = {}
    factors = {'da_q_norm': 7.37,
     'da_k_norm': 7.248,
     'da_lq1': 5.478,
     'da_lk1': 6.824,
     'da_lq2': 5.458,
     'da_lk2': 6.705,
     'da_subln_g': 3.375,
     'pool_scale': 3.54,
     'ret_gn_g': 4.46,
     'ffn_conv_b': 5.423,
     'meta_tokens_2': 2.788,
     'fox_norm_2': 4.385,
     'fox_b_f_2': 3.406,
     'fox_q_norm_2': 6.446,
     'fox_k_norm_2': 8.0,
     'hg_norm_2': 4.839,
     'hg_b_f_2': 47.206,
     'hg_lb_logits_2': 3.447,
     'hg_o_norm_2': 6.663,
     'moe_norm_2': 2.681,
     'moe_b_grp_2': 8.0,
     'moe_b_rt_2': 5.105}
    for name, (base, spread) in spreads.items():
        noise = np.random.default_rng([zlib.crc32(name.encode()), seed]).standard_normal(out[name].shape)
        drawn = base * np.exp(spread * noise) if base else spread * noise
        out[name] = jnp.asarray(drawn.astype(out[name].dtype))
    for name, factor in factors.items():
        out[name] = (out[name] * factor).astype(out[name].dtype)
    return out
```

```python
import math
from contextlib import ExitStack
from collections import namedtuple

import numpy as np

import concourse.bass as bass
from concourse import mybir


def named(**fields):
    return namedtuple("Named", fields)(**fields)


ALU = mybir.AluOpType
ACT = mybir.ActivationFunctionType
F32 = mybir.dt.float32
I32 = mybir.dt.int32
U32 = mybir.dt.uint32
AX = mybir.AxisListType.X
ds = bass.ds

P = 128
D = 1024
KD = D // P
SEQ = 512
CTX = 256
TC = SEQ + CTX
META = 16
T2 = SEQ + META
HALF = T2 // 2
EPS = 1e-6
FFN = 2816
KF = FFN // P
DEPTH = 2
LAM_INIT = 0.8 - 0.6 * math.exp(0.0)
NEG = -1e30
HEADS_DA = 4
HD = 64
RET_HEADS = 4
POOL_RADII = (1, 2, 4, 8)
FOX_HEADS = 16
HG_HEADS = 8
LEVELS = 7
N_GROUPS, PER_GROUP = 4, 8
N_EXP = N_GROUPS * PER_GROUP
D_EXP = 512
CAP = 64
N_ASG = 2 * T2
MAX_OVER = (N_ASG - 1) // CAP
OVER_STEPS = (T2 - 1) // CAP
TOK = [(128 * t, 128) for t in range(4)] + [(512, META)]

RING = 4096
LAST = 99

CST = {}
_at = 0
for _n, _w in (("ident", 128), ("ones", 128), ("blk", 128), ("rot", 128), ("cmask", 128), ("upper", 128),
               ("cos", 512), ("sin", 512), ("hgmask", 1024), ("iota", 32), ("iotag", 32), ("valid", 5)):
    CST[_n] = (_at, _w)
    _at += _w
CST_W = _at

PRM = {}
PRM_ROWS = [[], [], []]


def shape_constants():
    p = np.arange(P)
    c = np.zeros((P, CST_W), np.float32)

    def put(name, a):
        at, w = CST[name]
        c[:, at:at + w] = a.reshape(P, w)

    put("ident", np.eye(P))
    put("ones", np.ones((P, P)))
    put("blk", (p[:, None] // HD == p[None, :] // HD).astype(float))
    rot = np.zeros((P, P))
    for m in range(P):
        if (m // 16) % 2 == 0:
            rot[m + 16, m] = -1.0
        else:
            rot[m - 16, m] = 1.0
    put("rot", rot)
    put("cmask", np.where(p[None, :] > p[:, None], NEG, 0.0))
    put("upper", (p[:, None] < p[None, :]).astype(float))
    d = p % HD
    inv = np.float32(10000.0) ** (-np.arange(16, dtype=np.float32) / np.float32(16))
    t = np.arange(SEQ)
    pos = np.where((d // 32 == 0)[:, None], (t // 64)[None, :], (t % 64)[None, :]).astype(np.float32)
    ang = pos * inv[d % 16][:, None]
    put("cos", np.cos(ang))
    put("sin", np.sin(ang))
    hg = np.zeros((P, 8, P))
    for lv in range(LEVELS):
        L = P >> lv
        hg[:, lv, :] = ((p[:, None] // L == p[None, :] // L) & (p[:, None] % L < L // 2) & (p[None, :] % L >= L // 2))
    hg[:, 7, :] = np.eye(P)
    put("hgmask", hg)
    put("iota", np.tile(np.arange(32), (P, 1)))
    put("iotag", np.tile(np.arange(32) // 8, (P, 1)))
    put("valid", np.stack([(p < w).astype(float) for _, w in TOK], axis=1))
    u = np.arange(896)[None, :] - 384 - p[:, None]
    i = np.arange(SEQ)[None, None, :]
    tt = np.arange(2)[None, :, None]
    pp = p[:, None, None]
    ret = np.concatenate([
        np.maximum(u, 0).reshape(P, -1), np.maximum(-u, 0).reshape(P, -1), (u >= 0).reshape(P, -1), (u <= 0).reshape(P, -1),
        (i + CTX - 128 * tt - pp).reshape(P, -1), (SEQ + 128 * tt + pp - i).reshape(P, -1)], axis=1).astype(np.float32)
    cnt = np.zeros((4, SEQ), np.float32)
    for g, r in enumerate(POOL_RADII):
        cnt[g] = 1.0 / (np.minimum(t + r + 1, SEQ) - np.maximum(t - r, 0))
    sel = np.zeros((FOX_HEADS, FOX_HEADS, P), np.float32)
    for h in range(FOX_HEADS):
        sel[h, h, :] = -1.0
    tokid = np.zeros((P, 5), np.int32)
    for n, (t0, w) in enumerate(TOK):
        tokid[:w, n] = t0 + np.arange(w)
    return {"cst": c, "ret_dist": ret, "pool_inv": np.ascontiguousarray(np.tile(cnt.reshape(1, -1), (P, 1))),
            "fox_sel": sel.reshape(FOX_HEADS, -1), "tokid": tokid, "zeros_i": np.zeros((CAP, N_EXP + MAX_OVER), np.int32),
            "zero_rows": np.zeros((CAP, D), np.float32)}


def param_rows(A):
    rows, at = [], [0, 0, 0]

    def add(stack, name, ap, n, width=P, col=0):
        if col == 0:
            PRM[name] = (stack, at[stack])
        rows.append((stack, at[stack], n, col, width, ap))
        if col + width == P:
            at[stack] += n

    add(0, "mod_b", A["mod_b"].rearrange("l (r p) -> (l r) p", p=P), 96)
    add(0, "norm1_g", A["norm1_g"].rearrange("l (r p) -> (l r) p", p=P), 16)
    add(0, "norm2_g", A["norm2_g"].rearrange("l (r p) -> (l r) p", p=P), 16)
    add(1, "conv_w0", A["ffn_conv_w"][0].rearrange("t (r p) -> (t r) p", p=P), 66)
    add(1, "conv_b", A["ffn_conv_b"].rearrange("l (r p) -> (l r) p", p=P), 44)
    add(1, "sc_w", A["sc_conv_w"][0].rearrange("t (r p) -> (t r) p", p=P), 12)
    add(1, "pool_scale", A["pool_scale"].rearrange("l (r p) -> (l r) p", p=P), 4)
    add(1, "ret_gn", A["ret_gn_g"], 1)
    add(1, "subln", A["da_subln_g"], 1)
    add(2, "conv_w1", A["ffn_conv_w"][1].rearrange("t (r p) -> (t r) p", p=P), 66)
    for name, key, n in (("fox_norm", "fox_norm_2", 8), ("hg_norm", "hg_norm_2", 8), ("hg_b", "hg_b_f_2", 8),
                         ("hg_lb", "hg_lb_logits_2", 16), ("moe_norm", "moe_norm_2", 16)):
        add(2, name, A[key].rearrange("l (r p) -> (l r) p", p=P), n)
    for name, key in (("q_g", "da_q_norm"), ("k_g", "da_k_norm"), ("fq_g", "fox_q_norm_2"), ("fk_g", "fox_k_norm_2")):
        add(2, name, A[key], 1, HD, 0)
        add(2, name, A[key], 1, HD, HD)
    add(2, "hg_o", A["hg_o_norm_2"], 1)
    add(2, "spare", A["hg_o_norm_2"], 1)
    assert at == [P, P, P], at
    return rows

STOP = 99


def build(nc, A, K, out, scratch, last=LAST):
    rows = param_rows(A)
    ctx = ExitStack()
    with ctx:
        def sb(name, cols, dt=F32, parts=P):
            return ctx.enter_context(nc.sbuf_tensor(name, [parts, cols], dt))

        def sem(name):
            return ctx.enter_context(nc.semaphore(name))

        def sems(prefix, names):
            return named(**{n: sem(f"{prefix}_{n}") for n in names.split()})

        ring_sb = sb("ring_sb", 3 * RING)
        x_sb = sb("x_sb", KD * TC)
        h_sb = sb("h_sb", KD * TC)
        big = sb("big", 17152)
        cst = sb("cst", CST_W)
        prm = sb("prm", 3 * P)
        small = sb("small", 380)
        dest = sb("dest", 10, U32)
        tokid = sb("tokid", 5, I32)
        ctl = sb("ctl", MAX_OVER + 1, I32, 1)
        scr = sb("scr", 7680)
        ps = ctx.enter_context(nc.psum_tensor("ps", [P, 8 * 512], F32))

        XT = x_sb[:, :].rearrange("p (k t) -> p k t", k=KD)
        HT = h_sb[:, :].rearrange("p (k t) -> p k t", k=KD)

        def cs(name, lo=0, n=None, parts=P):
            at, w = CST[name]
            return cst[0:parts, at + lo:at + lo + (w if n is None else n)]

        def pcol(name, i=0, n=1):
            stack, at = PRM[name]
            return prm[:, ds(P * stack + at + i, n)]

        def bank(b, n, lo=0, parts=P):
            return ps[0:parts, 512 * b + lo:512 * b + lo + n]


        def tick(eng, dst=None):
            one = cs("ident", 0, 1)
            if dst is not None:
                return nc.tensor.matmul(dst, one, one, start=True, stop=True)
            if eng.engine == mybir.EngineType.Activation:
                return nc.scalar.copy(ticks[:, 0:1], one)
            if eng.engine == mybir.EngineType.Pool:
                return nc.gpsimd.tensor_tensor(ticks[:, 1:2], one, one, ALU.mult)
            return nc.vector.tensor_tensor(ticks[:, 2:3], one, one, ALU.mult)

        def scr_at(lo, n, parts=P):
            return scr[0:parts, lo:lo + n]

        SM = {}
        at = [0]

        def small_at(name, n):
            SM[name] = small[:, at[0]:at[0] + n]
            at[0] += n
            assert at[0] <= 380
            return SM[name]

        ticks = small_at("ticks", 4)
        modT = small_at("mod", 2 * 48 * 2).rearrange("p (l c g) -> p l c g", l=2, g=2)
        cT = small_at("cT", 16).rearrange("p (k g) -> p k g", g=2)
        G1 = small_at("G1", 32).rearrange("p (l k g) -> p l k g", l=2, g=2)
        G2 = small_at("G2", 32).rearrange("p (l k g) -> p l k g", l=2, g=2)
        lam = small_at("lam", 4)
        gains = small_at("gains", 4)
        stats = small_at("stats", 16)
        decay = small_at("decay", 8)
        lbc = small_at("lbc", 32)
        fbias = small_at("fbias", 2)
        gate = small_at("gate", 10).rearrange("p (t s) -> p t s", s=2)

        ring = [ring_sb[:, RING * s:RING * (s + 1)] for s in range(3)] + [big[:, RING * s:RING * (s + 1)] for s in range(3)]
        w_full = [sem(f"w_full{s}") for s in range(6)]
        w_free = [sem(f"w_free{s}") for s in range(6)]
        filled, used = [0] * 6, [0] * 6

        def fill(sp, s, src, k, nth=None):
            n = filled[s] if nth is None else nth
            sp.wait_ge(w_free[s], n + 1)
            w = src.shape[-1]
            sp.dma_start(ring[s][:, 0:k * w].rearrange("p (k c) -> p k c", k=k), src).then_inc(w_full[s], 16)
            if nth is None:
                filled[s] += 1

        def await_tile(pe, s, nth):
            pe.wait_ge(w_full[s], 16 * (nth + 1))

        def leave_tile(pe, s):
            pe.drain().then_inc(w_free[s], 1)

        def in_turns(eng, n, slots, counts, step):
            with eng.Fori(0, n // 2) as i:
                for s in (0, 1):
                    step(slots[s], counts[slots[s]] + i, 2 * i + s, s)
            for s in (0, 1):
                counts[slots[s]] += n // 2
            if n % 2:
                step(slots[0], counts[slots[0]], n - 1, 0)
                counts[slots[0]] += 1

        def wview(s, k, c):
            return ring[s][:, 0:k * c].rearrange("p (k c) -> p k c", k=k)

        SEGS = {TC: [(0, 512), (512, 256)], SEQ: [(0, 512)], T2: [(0, HALF), (HALF, HALF)]}

        def pair(p, T):
            if T == T2:
                return ps[:, 1024 * p:1024 * p + 1024].rearrange("p (a b) -> p a b", a=2)[:, :, 0:HALF]
            return ps[:, 1024 * p:1024 * p + T]

        def tok(ap, T):
            return ap.rearrange("p (a b) -> p a b", a=2) if T == T2 else ap

        proj_s = sems("proj", "rdy free src")._asdict()
        proj_at = [0, 0, 0]

        def proj_use(chunks, out=False):
            use = named(r0=proj_at[0], f0=proj_at[0] + 2 * proj_at[1], src0=proj_at[2], **proj_s)
            proj_at[0] += chunks
            proj_at[1] += 1
            proj_at[2] += out
            return use

        def gemm_tile(pe, g, s, nth, n0, w, kt, rhs, T, chunks=4, col=0, par0=0, leave=True):
            await_tile(pe, s, nth)
            for c in range(chunks):
                p = (par0 + c) % 2
                pe.wait_ge(g.free, g.f0 + n0 + c + 1)
                for k in range(kt):
                    for b, (t0, n) in enumerate(SEGS[T]):
                        m = nc.tensor.matmul(bank(2 * p + b, n), w[:, k, col + P * c:col + P * (c + 1)],
                                             rhs(k)[:, t0:t0 + n], start=(k == 0), stop=(k == kt - 1))
                m.then_inc(g.rdy, 1)
            if leave:
                leave_tile(pe, s)

        def gemm_tokens(pe, g, s, nth, n0, w, tiles, par0=0):
            await_tile(pe, s, nth)
            for c, (t0, m) in enumerate(tiles):
                p = (par0 + c) % 2
                pe.wait_ge(g.free, g.f0 + n0 + c + 1)
                for k in range(KD):
                    mm = nc.tensor.matmul(bank(2 * p, 512, parts=m), HT[:, k, t0:t0 + m], w[:, k, :],
                                          start=(k == 0), stop=(k == KD - 1))
                mm.then_inc(g.rdy, 1)
            leave_tile(pe, s)

        def hrhs(k):
            return HT[:, k, :]

        SQ = [scr_at(0, 768), scr_at(768, 768)]
        RR = scr_at(1536, 768)

        def norm_scalar(act, n, T, groups, scale, shift):
            act.wait_ge(n.go, n.q + 1)
            for k in range(KD):
                if k >= 2:
                    act.wait_ge(n.ssk, KD * n.q + k - 1)
                nc.scalar.activation(SQ[k % 2][:, 0:T], XT[:, k, 0:T], ACT.Square).then_inc(n.sq, 1)
            act.wait_ge(n.ms, n.q + 1)
            nc.scalar.activation(RR[:, 0:T], RR[:, 0:T], ACT.Sqrt).then_inc(n.root, 1)
            for k in range(KD):
                act.wait_ge(n.mul, KD * n.q + k + 1)
                for gi, (t0, t1) in enumerate(groups):
                    bias = 0.0 if shift is None else shift(k, gi)
                    a = nc.scalar.activation(HT[:, k, t0:t1], HT[:, k, t0:t1], ACT.Identity, bias=bias, scale=scale(k, gi))
                a.then_inc(n.h, 1)

        def norm_tensor(pe, n, T):
            for k in range(KD):
                pe.wait_ge(n.sq, KD * n.q + k + 1)
                for b, (t0, w) in enumerate(SEGS[T]):
                    m = nc.tensor.matmul(bank(6 + b, w), cs("ones"), SQ[k % 2][:, t0:t0 + w], start=(k == 0), stop=(k == KD - 1))
                m.then_inc(n.ssk, 1)
            pe.wait_ge(n.h, KD * (n.q + 1))

        def norm_vector(v, n, T):
            v.drain().then_inc(n.go, 1)
            v.wait_ge(n.ssk, KD * (n.q + 1))
            nc.vector.tensor_scalar(tok(RR[:, 0:T], T), pair(3, T), 1.0 / D, EPS, ALU.mult, ALU.add).then_inc(n.ms, 1)
            v.wait_ge(n.root, n.q + 1)
            nc.vector.reciprocal(RR[:, 0:T], RR[:, 0:T])
            v.drain()
            for k in range(KD):
                nc.vector.tensor_tensor(HT[:, k, 0:T], XT[:, k, 0:T], RR[:, 0:T], ALU.mult).then_inc(n.mul, 1)

        norm_s = sems("norm", "go sq ssk ms root mul h")._asdict()

        def norm_use(q):
            return named(q=q, **norm_s)

        HSQ, HRR, HQN, HTT = scr_at(0, 768), scr_at(768, 768), scr_at(1536, 768), scr_at(2304, 768)

        def heads_scalar(act, h, runs, T):
            n0, f0 = h.norm0, h.fin0
            for cnt, src, _, _, normed, _ in runs:
                if normed:
                    with act.Fori(0, cnt) as i:
                        act.wait_ge(h.fin, f0 + i + 1)
                        nc.scalar.activation(HSQ[:, 0:T], src(i), ACT.Square).then_inc(h.sq, 1)
                        act.wait_ge(h.ms, n0 + i + 1)
                        nc.scalar.activation(HRR[:, 0:T], HRR[:, 0:T], ACT.Sqrt).then_inc(h.root, 1)
                    n0 += cnt
                f0 += cnt

        def heads_tensor(pe, h, runs, T, mat):
            n0, r0 = h.norm0, h.rot0
            for cnt, src, _, _, normed, rotated in runs:
                with pe.Fori(0, cnt) as i:
                    if normed:
                        pe.wait_ge(h.sq, n0 + i + 1)
                        for b, (t0, w) in enumerate(SEGS[T]):
                            m = nc.tensor.matmul(bank(4 + b, w), mat, HSQ[:, t0:t0 + w], start=True, stop=True)
                        m.then_inc(h.ss, 1)
                    if rotated:
                        pe.wait_ge(h.qn, r0 + i + 1)
                        nc.tensor.matmul(bank(6, SEQ), cs("rot"), HQN[:, 0:SEQ], start=True, stop=True).then_inc(h.rot, 1)
                if normed:
                    n0 += cnt
                if rotated:
                    r0 += cnt

        def heads_vector(v, h, runs, T, width):
            n0, r0 = h.norm0, h.rot0
            v.drain().then_inc(h.fin, 1)
            for cnt, src, dst, gain, normed, rotated in runs:
                with v.Fori(0, cnt) as i:
                    out_ap = HQN[:, 0:T] if rotated else dst(i)
                    if normed:
                        v.wait_ge(h.ss, n0 + i + 1)
                        nc.vector.tensor_scalar(tok(HRR[:, 0:T], T), pair(2, T), 1.0 / width, EPS, ALU.mult, ALU.add).then_inc(h.ms, 1)
                        v.wait_ge(h.root, n0 + i + 1)
                        nc.vector.reciprocal(HRR[:, 0:T], HRR[:, 0:T])
                        v.drain()
                        a = nc.vector.scalar_tensor_tensor(out_ap, src(i), gain, HRR[:, 0:T], ALU.mult, ALU.mult)
                    else:
                        a = nc.vector.tensor_scalar(out_ap, src(i), gain, None, ALU.mult)
                    if rotated:
                        a.then_inc(h.qn, 1)
                        v.drain()
                        q = dst(i)
                        nc.vector.tensor_tensor(q[:, 0:SEQ], HQN[:, 0:SEQ], cs("cos"), ALU.mult)
                        if T > SEQ:
                            nc.vector.tensor_copy(q[:, SEQ:T], HQN[:, SEQ:T])
                        v.wait_ge(h.rot, r0 + i + 1)
                        nc.vector.tensor_tensor(HTT[:, 0:SEQ], bank(6, SEQ), cs("sin"), ALU.mult)
                        v.drain()
                        nc.vector.tensor_tensor(q[:, 0:SEQ], q[:, 0:SEQ], HTT[:, 0:SEQ], ALU.add)
                    v.drain().then_inc(h.fin, 1)
                if normed:
                    n0 += cnt
                if rotated:
                    r0 += cnt

        heads_s = sems("heads", "fin sq ss ms root qn rot")._asdict()
        heads_at = [0, 0, 0]

        def heads_use(runs):
            use = named(fin0=heads_at[0], norm0=heads_at[1], rot0=heads_at[2], **heads_s)
            heads_at[0] += 1 + sum(r[0] for r in runs)
            heads_at[1] += sum(r[0] for r in runs if r[4])
            heads_at[2] += sum(r[0] for r in runs if r[5])
            return use

        def outproj_sync(sp, w):
            for t, s in enumerate((1, 2)):
                fill(sp, s, w.rearrange("(k p) c -> p k c", p=P)[:, :, 512 * t:512 * t + 512], KD)

        def outproj_tensor(pe, g, T, rhs):
            pe.wait_ge(g.src, g.src0 + 1)
            for t, s in enumerate((1, 2)):
                gemm_tile(pe, g, s, used[s], 4 * t, wview(s, KD, 512), KD, rhs, T)
                used[s] += 1

        def add_vector(v, p, T, m, groups, gate):
            if gate is None:
                return nc.vector.tensor_tensor(tok(XT[:, m, 0:T], T), tok(XT[:, m, 0:T], T), pair(p, T), ALU.add)
            for gi, (t0, t1) in enumerate(groups):
                a = nc.vector.scalar_tensor_tensor(XT[:, m, t0:t1], ps[:, 1024 * p + t0:1024 * p + t1], gate(m, gi),
                                                   XT[:, m, t0:t1], ALU.mult, ALU.add)
            return a

        def outproj_vector(v, g, T, groups, gate):
            v.drain().then_inc(g.src, 1)
            v.drain().then_inc(g.free, 2)
            for m in range(KD):
                v.wait_ge(g.rdy, g.r0 + m + 1)
                add_vector(v, m % 2, T, m, groups, gate).then_inc(g.free, 1)

        pr = sems("prep", "row tr col c lamd lame misc cdma")
        md = sems("mod", "rdy free")

        def prep_gpsimd(pool):
            pool.dma_start(cst[:, :], K["cst"]).then_inc(pr.row, 16)
            for stack, at_, n, col, width, ap in rows:
                pool.dma_start(scr[at_:at_ + n, P * stack + col:P * stack + col + width], ap).then_inc(pr.row, 16)

        def prep_scalar(act):
            act.dma_start(scr[0:8, 512:640], A["c"].rearrange("a (k p) -> (a k) p", p=P)).then_inc(pr.cdma, 16)
            act.dma_start(scr[8:16, 512:640], A["c_ctx"].rearrange("(k p) -> k p", p=P)).then_inc(pr.cdma, 16)
            for n, key in enumerate(("da_lq1", "da_lk1", "da_lq2", "da_lk2")):
                act.dma_start(scr[:, 640 + HD * n:640 + HD * (n + 1)], A[key].partition_broadcast(P).rearrange("p a b -> p (a b)") if len(A[key].partition_broadcast(P).shape) == 3 else A[key].partition_broadcast(P)).then_inc(pr.misc, 16)
            for n, key in enumerate(("ret_decay_f", "ret_decay_b")):
                b = A[key].partition_broadcast(P)
                act.dma_start(decay[:, 4 * n:4 * n + 4], b.rearrange("p a b -> p (a b)") if len(b.shape) == 3 else b).then_inc(pr.misc, 16)
            act.dma_start(fbias[0:FOX_HEADS, 0:1], A["fox_b_f_2"].rearrange("a h -> h a")).then_inc(pr.misc, 16)
            act.wait_ge(pr.tr, 4)
            for n in range(3):
                nc.scalar.copy(prm[:, P * n:P * (n + 1)], bank(n, P))
            act.drain().then_inc(pr.col, 1)
            nc.scalar.activation(cT, bank(3, 16).rearrange("p (g k) -> p k g", g=2), ACT.Silu).then_inc(pr.c, 1)
            act.wait_ge(pr.lamd, 1)
            nc.scalar.activation(lam[:, 0:2], lam[:, 0:2], ACT.Exp)
            act.wait_ge(pr.misc, 16 * 7)
            nc.scalar.activation(decay[:, :], decay[:, :], ACT.Exp)
            act.drain().then_inc(pr.lame, 1)

        def prep_tensor(pe):
            for s in range(6):
                pe.drain().then_inc(w_free[s], 1)
            pe.wait_ge(pr.row, 16 * (1 + len(rows)))
            for n in range(3):
                nc.tensor.transpose(bank(n, P), scr_at(P * n, P), cs("ident")).then_inc(pr.tr, 1)
            pe.wait_ge(pr.cdma, 32)
            nc.tensor.transpose(bank(3, 16), scr_at(512, P, 16), cs("ident", 0, 16, 16)).then_inc(pr.tr, 1)

        def prep_vector(v):
            v.wait_ge(pr.misc, 16 * 7)
            nc.vector.tensor_tensor(scr_at(896, HD), scr_at(640, HD), scr_at(640 + HD, HD), ALU.mult)
            nc.vector.tensor_tensor(scr_at(896 + HD, HD), scr_at(640 + 2 * HD, HD), scr_at(640 + 3 * HD, HD), ALU.mult)
            v.drain()
            nc.vector.tensor_reduce(lam[:, 0:2], scr_at(896, 2 * HD).rearrange("p (a b) -> p a b", a=2), AX, ALU.add).then_inc(pr.lamd, 1)
            v.wait_ge(pr.lame, 1)
            nc.vector.tensor_tensor(lam[:, 2:3], lam[:, 0:1], lam[:, 1:2], ALU.subtract)
            nc.vector.tensor_scalar(decay[:, :], decay[:, :], -1.0, None, ALU.mult)
            v.drain()
            nc.vector.tensor_scalar(lam[:, 3:4], lam[:, 2:3], LAM_INIT, None, ALU.add)
            v.wait_ge(pr.col, 1)
            for n, (name, f) in enumerate((("q_g", HD ** -0.5), ("fq_g", HD ** -0.5), ("subln", 1.0 - LAM_INIT))):
                nc.vector.tensor_scalar(gains[:, n:n + 1], pcol(name), f, None, ALU.mult)
            nc.vector.memset(gains[:, 3:4], HD ** -0.5)
            v.drain()

        def mod_sync(sp):
            for l in range(DEPTH):
                w = A["mod_w"][l].rearrange("(k p) c -> p k c", p=P)
                in_turns(sp, 12, (0, 1), filled, lambda s, nth, t, par: fill(sp, s, w[:, :, ds(512 * t, 512)], KD, nth))

        def mod_tensor(pe):
            pe.wait_ge(pr.c, 1)
            for l in range(DEPTH):
                def step(s, nth, t, par):
                    await_tile(pe, s, nth)
                    pe.wait_ge(md.free, 12 * l + t + 1)
                    for c in range(4):
                        for k in range(KD):
                            m = nc.tensor.matmul(bank(par, 2, 2 * c), wview(s, KD, 512)[:, k, P * c:P * (c + 1)], cT[:, k, :],
                                                 start=(k == 0), stop=(k == KD - 1))
                    m.then_inc(md.rdy, 1)
                    leave_tile(pe, s)
                in_turns(pe, 12, (0, 1), used, step)

        def mod_vector(v):
            v.drain().then_inc(md.free, 2)
            for l in range(DEPTH):
                def step(s, nth, t, par):
                    v.wait_ge(md.rdy, 12 * l + t + 1)
                    nc.vector.tensor_tensor(modT[:, l, ds(4 * t, 4), :], bank(par, 8).rearrange("p (c g) -> p c g", g=2),
                                            pcol("mod_b", 48 * l + 4 * t, 4).unsqueeze(2).to_broadcast([P, 4, 2]),
                                            ALU.add).then_inc(md.free, 1)
                in_turns(v, 12, (0, 1), [0] * 6, step)
            v.drain()
            for l in range(DEPTH):
                for G, name, part in ((G1, "norm1_g", 1), (G2, "norm2_g", 4)):
                    nc.vector.tensor_scalar(G[:, l, :, :], modT[:, l, 8 * part:8 * part + 8, :], 1.0, None, ALU.add)
                    v.drain()
                    nc.vector.tensor_tensor(G[:, l, :, :], G[:, l, :, :],
                                            pcol(name, 8 * l, 8).unsqueeze(2).to_broadcast([P, 8, 2]), ALU.mult)
            v.drain()

        ti = sems("tokin", "x tr cp")

        def tokin_gpsimd(pool):
            for t in range(6):
                src = A["x"][0][P * t:P * (t + 1), :] if t < 4 else A["ctx"][0][P * (t - 4):P * (t - 3), :]
                pool.dma_start(big[:, D * t:D * (t + 1)], src).then_inc(ti.x, 16)

        def tokin_tensor(pe):
            pe.wait_ge(ti.x, 16 * 6)
            for t in range(6):
                for hf in range(2):
                    n = 2 * t + hf
                    if n >= 2:
                        pe.wait_ge(ti.cp, n - 1)
                    for c in range(4):
                        m = nc.tensor.transpose(bank(4 + n % 2, P, P * c), big[:, D * t + 512 * hf + P * c:D * t + 512 * hf + P * (c + 1)], cs("ident"))
                    m.then_inc(ti.tr, 1)

        def tokin_vector(v):
            for t in range(6):
                for hf in range(2):
                    n = 2 * t + hf
                    v.wait_ge(ti.tr, n + 1)
                    nc.vector.tensor_copy(XT[:, 4 * hf:4 * hf + 4, P * t:P * (t + 1)],
                                          bank(4 + n % 2, 512).rearrange("p (c t) -> p c t", c=4)).then_inc(ti.cp, 1)
            v.drain()

        GU = big[:, 0:KF * TC].rearrange("p (j t) -> p j t", j=KF)
        CA = [scr_at(0, 768), scr_at(768, 768)]
        CS = [scr_at(1536, 768), scr_at(2304, 768)]

        def ffn_sync(sp, l):
            up = A["ffn_w_up"][l].rearrange("(k p) (h c) -> h p k c", p=P, h=2)
            with sp.Fori(0, KF // 2) as i:
                for h in range(2):
                    fill(sp, h, up[h][:, :, ds(256 * i, 256)], KD, filled[h] + i)
            for h in range(2):
                filled[h] += KF // 2

        def conv_ops(v, out_ap, src, w, j, T):
            spans = [(0, SEQ)] + ([(SEQ, TC)] if T == TC else [])
            for tap in (0, 2):
                for t0, t1 in spans:
                    o = out_ap[:, t0 + 1:t1] if tap == 0 else out_ap[:, t0:t1 - 1]
                    i = src[:, t0:t1 - 1] if tap == 0 else src[:, t0 + 1:t1]
                    a = nc.vector.scalar_tensor_tensor(o, i, w(tap, j), o, ALU.mult, ALU.add)
                if tap == 0:
                    v.drain()
            return a

        def ffn_tensor(pe, f, T):
            with pe.Fori(0, KF // 2) as i:
                for jj in range(2):
                    pe.wait_ge(f.free, f.o.free + 2 * i + jj + 1)
                    for h in range(2):
                        w = wview(h, KD, 256)
                        if jj == 0:
                            await_tile(pe, h, used[h] + i)
                        for k in range(KD):
                            for b, (t0, n) in enumerate(SEGS[T]):
                                m = nc.tensor.matmul(bank(4 * jj + 2 * h + b, n), w[:, k, P * jj:P * (jj + 1)],
                                                     HT[:, k, t0:t0 + n], start=(k == 0), stop=(k == KD - 1))
                        if h == 1:
                            m.then_inc(f.rdy, 1)
                        if jj == 1:
                            leave_tile(pe, h)
            for h in range(2):
                used[h] += KF // 2
        def ffn_scalar(act, f, l, T):
            with act.Fori(0, KF // 2) as i:
                for jj in range(2):
                    n = 2 * i + jj
                    act.wait_ge(f.rdy, f.o.rdy + n + 1)
                    nc.scalar.activation(CA[jj][:, 0:T], ps[:, 2048 * jj:2048 * jj + T], ACT.Identity,
                                         bias=pcol("conv_b", KF * l + n), scale=pcol(f"conv_w{l}", KF + n)).then_inc(f.mid, 1)
                    act.wait_ge(f.conv, f.o.conv + n + 1)
                    nc.scalar.activation(CS[jj][:, 0:T], CA[jj][:, 0:T], ACT.Silu).then_inc(f.silu, 1)

        def ffn_vector(v, f, l, T, groups):
            v.drain().then_inc(f.free, 2)

            with v.Fori(0, KF // 2) as i:
                for jj in range(2):
                    n = 2 * i + jj
                    v.wait_ge(f.mid, f.o.mid + n + 1)
                    conv_ops(v, CA[jj], ps[:, 2048 * jj:2048 * jj + T], lambda tap, j: pcol(f"conv_w{l}", KF * tap + j), n, T).then_inc(f.conv, 1)
                    v.wait_ge(f.silu, f.o.silu + n + 1)
                    nc.vector.tensor_tensor(GU[:, n, 0:T], CS[jj][:, 0:T], ps[:, 2048 * jj + 1024:2048 * jj + 1024 + T], ALU.mult).then_inc(f.free, 1)

        def down_sync(sp, l):
            w = A["ffn_w_down"][l].rearrange("(k p) c -> p k c", p=P)
            in_turns(sp, KD, (2, 0), filled, lambda s, nth, t, par: fill(sp, s, w[:, :, ds(P * t, P)], KF, nth))

        def down_tensor(pe, f, g, T):
            pe.wait_ge(f.free, f.o.free + KF + 2)
            in_turns(pe, KD, (2, 0), used, lambda s, nth, t, par: gemm_tile(
                pe, g, s, nth, t, wview(s, KF, P), KF, lambda k: GU[:, k, :], T, chunks=1, par0=par))

        def down_vector(v, g, l, T, groups):
            v.drain().then_inc(g.free, 2)

            def step(s, nth, t, par):
                v.wait_ge(g.rdy, g.r0 + t + 1)
                add_vector(v, par, T, t, groups, lambda m, gi: modT[:, l, ds(40 + m, 1), gi]).then_inc(g.free, 1)
            in_turns(v, KD, (2, 0), [0] * 6, step)
            v.drain()

        ffn_s = sems("ffn", "rdy free mid conv silu")._asdict()

        def ffn_use(q):
            return named(o=named(rdy=KF * q, free=(KF + 2) * q, mid=KF * q, conv=KF * q, silu=KF * q), **ffn_s)

        Z = big[:, 0:12 * TC].rearrange("p (j t) -> p j t", j=12)
        VT = big[:, 12 * TC:12 * TC + 6 * 512].rearrange("p (t c) -> p t c", t=6)
        QH, KH = scr_at(3072, 768), scr_at(3840, 768)
        VH = scr_at(4608, 768).rearrange("p (t c) -> p t c", t=6)
        PR = scr_at(5376, 1536).rearrange("p (m t) -> p m t", m=2)
        PTR = scr_at(6912, 768)
        G_ALL = [(0, SEQ), (SEQ, TC)]
        G_LAT = [(0, SEQ)]
        TILES6 = [(P * t, P) for t in range(6)]

        def l0_sync(sp):
            w = A["ev_w_in"][0].rearrange("(k p) c -> p k c", p=P)
            for t, part in enumerate((1, 2, 0, 3, 4, 5)):
                fill(sp, t % 3, w[:, :, 512 * part:512 * part + 512], KD)

        def l0_tensor(pe, g):
            for t in range(5):
                gemm_tile(pe, g, t % 3, used[t % 3], 4 * t, wview(t % 3, KD, 512), KD, hrhs, TC)
                used[t % 3] += 1
            gemm_tokens(pe, g, 2, used[2], 20, wview(2, KD, 512), TILES6)
            used[2] += 1

        def l0_vector(v, g):
            v.drain().then_inc(g.free, 2)
            for c in range(4):
                v.wait_ge(g.rdy, g.r0 + c + 1)
                nc.vector.tensor_copy(Z[:, c, :], pair(c % 2, TC)).then_inc(g.free, 1)
            v.drain()
            for c in range(4):
                v.wait_ge(g.rdy, g.r0 + 4 + c + 1)
                nc.vector.tensor_tensor(Z[:, c, :], Z[:, c, :], pair(c % 2, TC), ALU.mult).then_inc(g.free, 1)
            v.drain()
            for c in range(4):
                nc.vector.tensor_scalar(HQN, Z[:, c, :], pcol("sc_w", 4 + c), None, ALU.mult)
                v.drain()
                conv_ops(v, HQN, Z[:, c, :], lambda tap, j: pcol("sc_w", 4 * tap + j), c, TC)
                v.drain()
                v.wait_ge(g.rdy, g.r0 + 8 + c + 1)
                nc.vector.tensor_tensor(Z[:, c, :], HQN, pair(c % 2, TC), ALU.mult).then_inc(g.free, 1)
                v.drain()
            for c in range(8):
                v.wait_ge(g.rdy, g.r0 + 12 + c + 1)
                nc.vector.tensor_copy(Z[:, 4 + c, :], pair(c % 2, TC)).then_inc(g.free, 1)
            for t in range(6):
                v.wait_ge(g.rdy, g.r0 + 20 + t + 1)
                nc.vector.tensor_copy(VT[:, t, :], bank(2 * (t % 2), 512)).then_inc(g.free, 1)

        def l0_runs():
            return [(4, lambda i: Z[:, 4 + i, :], None, gains[:, 0:1], True, True),
                    (4, lambda i: Z[:, 8 + i, :], None, pcol("k_g"), True, True)]

        def with_dst(runs, dsts):
            return [(c, s, d, g_, n, r) for (c, s, _, g_, n, r), d in zip(runs, dsts)]

        L0_Q = [(j, 0, 768) for j in range(4)] + [(j, 512, 256) for j in (4, 5)]

        att_s = sems("att", "qkv s nm p pd pt ptc o oc")._asdict()
        ATT_ADDS = dict(qkv=4, s=24, nm=24, p=25, pd=24, pt=25, ptc=24, o=25, oc=25)

        def att_use(q):
            return named(b=named(**{n: q * c for n, c in ATT_ADDS.items()}), **att_s)

        def l0_att_scalar(act, a):
            act.drain().then_inc(a.p, 1)
            with act.Fori(0, HEADS_DA) as h:
                act.wait_ge(a.o, a.b.o + 6 * h + 1)
                nc.scalar.copy(QH, Z[:, 4 + h, :])
                nc.scalar.copy(KH, Z[:, 8 + h, :])
                nc.scalar.copy(VH, VT[:, :, ds(P * h, P)]).then_inc(a.qkv, 1)
                for j, (qt, k0, nk) in enumerate(L0_Q):
                    n = 6 * h + j
                    act.wait_ge(a.nm, a.b.nm + n + 1)
                    act.wait_ge(a.pt, a.b.pt + n + 1)
                    for m in range(2):
                        e = nc.scalar.activation(PR[:, m, 0:nk], ps[:, 1024 * m:1024 * m + nk], ACT.Exp,
                                                 bias=stats[:, 2 + m:3 + m], accum_out=stats[:, 4 + m:5 + m])
                    e.then_inc(a.p, 1)
                    act.wait_ge(a.pt, a.b.pt + n + 2)
                    act.wait_ge(a.o, a.b.o + n + 1)
                    nc.scalar.copy(PTR[:, 0:nk], ps[:, 2048:2048 + nk]).then_inc(a.ptc, 1)

        def l0_att_tensor(pe, a):
            pe.drain().then_inc(a.pt, 1)
            pe.drain().then_inc(a.o, 1)
            with pe.Fori(0, HEADS_DA) as h:
                pe.wait_ge(a.qkv, a.b.qkv + h + 1)
                for j, (qt, k0, nk) in enumerate(L0_Q):
                    n = 6 * h + j
                    pe.wait_ge(a.p, a.b.p + n + 1)
                    for m in range(2):
                        r = slice(HD * m, HD * (m + 1))
                        for c0 in range(0, nk, 512):
                            w = min(512, nk - c0)
                            mm = nc.tensor.matmul(bank(2 * m + c0 // 512, w), QH[r, P * qt:P * (qt + 1)],
                                                  KH[r, k0 + c0:k0 + c0 + w], start=True, stop=True)
                    mm.then_inc(a.s, 1)
                    pe.wait_ge(a.pd, a.b.pd + n + 1)
                    for b in range(nk // P):
                        mm = nc.tensor.transpose(ps[:, 2048 + P * b:2048 + P * (b + 1)], PR[:, 0, P * b:P * (b + 1)], cs("ident"))
                    mm.then_inc(a.pt, 1)
                    pe.wait_ge(a.ptc, a.b.ptc + n + 1)
                    pe.wait_ge(a.oc, a.b.oc + n + 1)
                    for b in range(nk // P):
                        mm = nc.tensor.matmul(bank(6, P), VH[:, k0 // P + b, :], PTR[:, P * b:P * (b + 1)],
                                              start=(b == 0), stop=(b == nk // P - 1))
                    mm.then_inc(a.o, 1)

        def l0_att_vector(v, a):
            v.drain().then_inc(a.oc, 1)
            with v.Fori(0, HEADS_DA) as h:
                for j, (qt, k0, nk) in enumerate(L0_Q):
                    n = 6 * h + j
                    v.wait_ge(a.s, a.b.s + n + 1)
                    for m in range(2):
                        nc.vector.tensor_reduce(stats[:, m:m + 1], ps[:, 1024 * m:1024 * m + nk], AX, ALU.max)
                    v.drain()
                    nc.vector.tensor_scalar(stats[:, 2:4], stats[:, 0:2], -1.0, None, ALU.mult).then_inc(a.nm, 1)
                    v.wait_ge(a.p, a.b.p + n + 2)
                    nc.vector.reciprocal(stats[:, 6:8], stats[:, 4:6])
                    v.drain()
                    nc.vector.tensor_tensor(stats[:, 7:8], stats[:, 7:8], lam[:, 3:4], ALU.mult)
                    v.drain()
                    nc.vector.tensor_scalar(PR[:, 1, 0:nk], PR[:, 1, 0:nk], stats[:, 7:8], None, ALU.mult)
                    v.drain()
                    nc.vector.scalar_tensor_tensor(PR[:, 0, 0:nk], PR[:, 0, 0:nk], stats[:, 6:7], PR[:, 1, 0:nk],
                                                   ALU.mult, ALU.subtract).then_inc(a.pd, 1)
                    v.wait_ge(a.o, a.b.o + n + 2)
                    nc.vector.tensor_copy(HT[:, 4 + h, P * qt:P * (qt + 1)], bank(6, P)).then_inc(a.oc, 1)

        PV_ = big[:, 0:4 * SEQ].rearrange("p (j t) -> p j t", j=4)
        RQ = big[:, 2048:2048 + 2 * SEQ].rearrange("p (j t) -> p j t", j=2)
        RK = big[:, 3072:3072 + 2 * TC].rearrange("p (j t) -> p j t", j=2)
        RG = big[:, 4608:4608 + 4 * SEQ].rearrange("p (j t) -> p j t", j=4)
        RV = big[:, 6656:6656 + 6 * 512].rearrange("p (t c) -> p t c", t=6)
        RD = big[:, 9728:9728 + 3584 + 2048]
        RDEC = scr_at(3072, 1920)
        RTMP = scr_at(4992, 1024)
        RATT = [scr_at(6016, 512), scr_at(6528, 512)]
        PI = big[:, 15360:15360 + 4 * 128]
        l1s = sems("l1", "dma")

        def l1_gpsimd(pool, gate):
            pool.wait_ge(gate, 1)
            pool.dma_start(RD, K["ret_dist"]).then_inc(l1s.dma, 16)
            pool.dma_start(scr_at(3072, 2048), K["pool_inv"]).then_inc(l1s.dma, 16)
            pool.dma_start(scr_at(5120, 512).rearrange("p (g c) -> p g c", g=4), A["pool_w"][0].rearrange("g p c -> p g c")).then_inc(l1s.dma, 16)

        def l1_sync(sp):
            w = A["od_w_in"][0].rearrange("(k p) c -> p k c", p=P)
            for t in range(4):
                fill(sp, (1, 2, 0, 1)[t], w[:, :, 512 * t:512 * t + 512], KD)

        def l1_tensor(pe, g):
            W = lambda s: wview(s, KD, 512)
            gemm_tile(pe, g, 1, used[1], 0, W(1), KD, hrhs, SEQ)
            used[1] += 1
            gemm_tile(pe, g, 2, used[2], 4, W(2), KD, hrhs, SEQ, chunks=2, leave=False)
            gemm_tile(pe, g, 2, used[2], 6, W(2), KD, hrhs, TC, chunks=2, col=256)
            used[2] += 1
            gemm_tokens(pe, g, 0, used[0], 8, W(0), TILES6)
            used[0] += 1
            gemm_tile(pe, g, 1, used[1], 14, W(1), KD, hrhs, SEQ)
            used[1] += 1

        def l1_vector(v, g):
            v.drain().then_inc(g.free, 2)
            for c in range(18):
                v.wait_ge(g.rdy, g.r0 + c + 1)
                src = ps[:, 1024 * (c % 2):1024 * (c % 2) + SEQ]
                if c < 4:
                    nc.vector.tensor_copy(PV_[:, c, :], src).then_inc(g.free, 1)
                elif c < 6:
                    nc.vector.tensor_copy(RQ[:, c - 4, :], src).then_inc(g.free, 1)
                elif c < 8:
                    nc.vector.tensor_copy(RK[:, c - 6, :], pair(c % 2, TC)).then_inc(g.free, 1)
                elif c < 14:
                    nc.vector.tensor_copy(RV[:, c - 8, :], src).then_inc(g.free, 1)
                else:
                    nc.vector.tensor_copy(RG[:, c - 14, :], src).then_inc(g.free, 1)

        def pool_vector(v, b):
            v.wait_ge(l1s.dma, 48)
            v.drain()
            R = max(POOL_RADII)
            run = scr_at(0, SEQ + 2 * R + 1)
            nc.vector.memset(scr_at(768, SEQ), 0.0)
            nc.vector.memset(run[:, 0:R + 1], 0.0)
            for g_, r in enumerate(POOL_RADII):
                v.drain()
                nc.vector.tensor_tensor_scan(run[:, R + 1:R + 1 + SEQ], scr_at(768, SEQ), PV_[:, g_, :], 0.0, ALU.add, ALU.add)
                v.drain()
                nc.vector.tensor_copy(run[:, R + 1 + SEQ:], run[:, R + SEQ:R + SEQ + 1].to_broadcast([P, R]))
                v.drain()
                nc.vector.tensor_tensor(scr_at(1536, SEQ), run[:, R + 1 + r:R + 1 + r + SEQ], run[:, R - r:R - r + SEQ], ALU.subtract)
                v.drain()
                nc.vector.tensor_tensor(scr_at(1536, SEQ), scr_at(1536, SEQ), scr_at(3072 + SEQ * g_, SEQ), ALU.mult)
                v.drain()
                nc.vector.tensor_tensor(PV_[:, g_, :], scr_at(1536, SEQ), PV_[:, g_, :], ALU.subtract)
            v.drain().then_inc(b.y, 1)
            for g_ in range(4):
                v.wait_ge(b.mm, g_ + 1)
                nc.vector.tensor_scalar(HT[:, g_, 0:SEQ], bank(g_, SEQ), pcol("pool_scale", g_), None, ALU.mult)
            v.drain().then_inc(b.done, 1)

        def pool_tensor(pe, b):
            pe.wait_ge(b.y, 1)
            for g_ in range(4):
                nc.tensor.matmul(bank(g_, SEQ), scr_at(5120 + P * g_, P), PV_[:, g_, :], start=True, stop=True).then_inc(b.mm, 1)

        def ret_head_decays_scalar(act, r, h):
            act.wait_ge(r.att_free, 12 // 12 * 0 + 1 + h)
            nc.scalar.activation(RDEC[:, 0:896], RD[:, 0:896], ACT.Exp, scale=decay[:, ds(h, 1)])
            nc.scalar.activation(RTMP[:, 0:896], RD[:, 896:1792], ACT.Exp, scale=decay[:, ds(4 + h, 1)]).then_inc(r.e1, 1)
            nc.scalar.activation(RDEC[:, 896:1920], RD[:, 3584:4608], ACT.Exp, scale=decay[:, ds(h, 1)])
            act.wait_ge(r.e1v, h + 1)
            nc.scalar.activation(RTMP[:, 0:1024], RD[:, 4608:5632], ACT.Exp, scale=decay[:, ds(4 + h, 1)]).then_inc(r.e2, 1)

        def ret_vector(v, r):
            v.drain().then_inc(r.att_free, 1)
            v.drain().then_inc(r.af, 2)
            v.drain().then_inc(r.oc, 1)
            for h in range(RET_HEADS):
                v.wait_ge(r.e1, h + 1)
                nc.vector.tensor_tensor(RDEC[:, 0:896], RDEC[:, 0:896], RD[:, 1792:2688], ALU.mult)
                nc.vector.tensor_tensor(RTMP[:, 0:896], RTMP[:, 0:896], RD[:, 2688:3584], ALU.mult)
                v.drain()
                nc.vector.tensor_tensor(RDEC[:, 0:896], RDEC[:, 0:896], RTMP[:, 0:896], ALU.add).then_inc(r.e1v, 1)
                v.wait_ge(r.e2, h + 1)
                nc.vector.tensor_tensor(RDEC[:, 896:1920], RDEC[:, 896:1920], RTMP[:, 0:1024], ALU.add)
                v.drain()
                for t in range(6):
                    n = 6 * h + t
                    dec = RDEC[:, 384 - P * t:384 - P * t + SEQ] if t < 4 else RDEC[:, 896 + SEQ * (t - 4):896 + SEQ * (t - 3)]
                    v.wait_ge(r.s, n + 1)
                    if n >= 2:
                        v.wait_ge(r.pv, n - 1)
                    nc.vector.tensor_tensor(RATT[n % 2], bank(n % 2, SEQ), dec, ALU.mult).then_inc(r.af, 1)
                v.wait_ge(r.o, h + 1)
                nc.vector.tensor_copy(HT[:, 4 + h, 0:SEQ], bank(2, SEQ)).then_inc(r.oc, 1)
                v.drain().then_inc(r.att_free, 1)

        def ret_scalar(act, r):
            for h in range(RET_HEADS):
                ret_head_decays_scalar(act, r, h)

        def ret_tensor(pe, r):
            N = 6 * RET_HEADS

            def score(n):
                h, t = divmod(n, 6)
                pe.wait_ge(r.af, n + 1)
                rr = slice(HD * (h % 2), HD * (h % 2 + 1))
                nc.tensor.matmul(bank(n % 2, SEQ), RK[rr, h // 2, P * t:P * (t + 1)], RQ[rr, h // 2, :], start=True, stop=True).then_inc(r.s, 1)

            pe.wait_ge(r.oc, 1)
            score(0)
            for n in range(N):
                h, t = divmod(n, 6)
                if n + 1 < N:
                    score(n + 1)
                pe.wait_ge(r.af, n + 3)
                if t == 0:
                    pe.wait_ge(r.oc, h + 1)
                mm = nc.tensor.matmul(bank(2, SEQ), RV[:, t, P * h:P * (h + 1)], RATT[n % 2], start=(t == 0), stop=(t == 5))
                mm.then_inc(r.pv, 1)
                if t == 5:
                    pe.drain().then_inc(r.o, 1)

        def l1_gate(act, v_, g, eng):
            pass

        to = sems("tokout", "go tr cp st")
        OUT = big[:, 0:4 * D].rearrange("p (t c) -> p t c", t=4)

        def tokout_tensor(pe):
            pe.wait_ge(to.go, 1)
            for t in range(4):
                for hf in range(2):
                    n = 2 * t + hf
                    if n >= 2:
                        pe.wait_ge(to.cp, n - 1)
                    for c in range(4):
                        m = nc.tensor.transpose(bank(n % 2, P, P * c), XT[:, 4 * hf + c, P * t:P * (t + 1)], cs("ident"))
                    m.then_inc(to.tr, 1)

        def tokout_vector(v):
            v.drain().then_inc(to.go, 1)
            for n in range(8):
                v.wait_ge(to.tr, n + 1)
                nc.vector.tensor_copy(OUT[:, n // 2, 512 * (n % 2):512 * (n % 2) + 512], bank(n % 2, 512)).then_inc(to.cp, 1)

        def tokout_sync(sp):
            for t in range(4):
                sp.wait_ge(to.cp, 2 * t + 2)
                sp.dma_start(out[0][P * t:P * (t + 1), :], OUT[:, t, :]).then_inc(to.st, 16)
            sp.wait_ge(to.st, 64)

        G_T2 = [(0, T2)]
        mt = sems("meta", "x tr")

        def meta_gpsimd(pool, gate_sem):
            pool.wait_ge(gate_sem, 1)
            pool.dma_start(scr_at(3072, D, META), A["meta_tokens_2"]).then_inc(mt.x, 16)

        def meta_tensor(pe):
            pe.wait_ge(mt.x, 16)
            for k in range(KD):
                m = nc.tensor.transpose(bank(0, META, META * k), scr_at(3072 + P * k, P, META), cs("ident", 0, META, META))
            m.then_inc(mt.tr, 1)

        def meta_vector(v):
            v.wait_ge(mt.tr, 1)
            nc.vector.tensor_copy(XT[:, :, SEQ:T2], bank(0, META * KD).rearrange("p (k t) -> p k t", k=KD))
            v.drain()

        FQ = big[:, 0:KD * T2].rearrange("p (j t) -> p j t", j=KD)
        FK = big[:, KD * T2:2 * KD * T2].rearrange("p (j t) -> p j t", j=KD)
        FV = big[:, 2 * KD * T2:2 * KD * T2 + 5 * D].rearrange("p (t c) -> p t c", t=5)
        SEL = big[0:FOX_HEADS, 13568:15616]
        CUM = big[0:FOX_HEADS, 15616:16144]
        CT1 = big[0:FOX_HEADS, 16144:16672]
        CT2 = scr_at(4096, T2, FOX_HEADS)
        CT3 = scr_at(4736, T2, FOX_HEADS)
        WF = big[:, 16672:16800].rearrange("p (k h) -> p k h", k=KD)
        fx = sems("fox", "dma fl fn fe fs fd")
        QC, KC = scr_at(3072, T2), scr_at(3600, T2)
        VC = scr_at(4128, 640).rearrange("p (t c) -> p t c", t=5)
        SELC = scr_at(4768, 256, FOX_HEADS)
        PF = [scr_at(5024, T2), scr_at(5552, T2)]
        PTF = [scr_at(6080, 640), scr_at(6720, 640)]

        def fox_gpsimd(pool):
            pool.dma_start(SEL, K["fox_sel"]).then_inc(fx.dma, 16)
            pool.dma_start(WF, A["fox_w_in_2"][0].rearrange("(k p) c -> p k c", p=P)[:, :, 3 * D:3 * D + FOX_HEADS]).then_inc(fx.dma, 16)

        def proj_sync(sp, w, cols, slots):
            for t, (c0, s) in enumerate(zip(cols, slots)):
                fill(sp, s, w[:, :, c0:c0 + 512], KD)

        FOX_SLOTS = (0, 1, 2, 0, 1, 2)

        def fox_proj_tensor(pe, g):
            for t, s in enumerate(FOX_SLOTS[:4]):
                gemm_tile(pe, g, s, used[s], 4 * t, wview(s, KD, 512), KD, hrhs, T2)
                used[s] += 1
            for t, s in enumerate(FOX_SLOTS[4:]):
                gemm_tokens(pe, g, s, used[s], 16 + 5 * t, wview(s, KD, 512), TOK, par0=t)
                used[s] += 1
            pe.wait_ge(fx.dma, 32)
            for b, (t0, n) in enumerate(SEGS[T2]):
                for k in range(KD):
                    m = nc.tensor.matmul(bank(4 + b, n, parts=FOX_HEADS), WF[:, k, :], HT[:, k, t0:t0 + n], start=(k == 0), stop=(k == KD - 1))
            m.then_inc(fx.fl, 1)

        def fox_proj_vector(v, g):
            v.drain().then_inc(g.free, 2)
            for c in range(16):
                dst = FQ[:, c, :] if c < 8 else FK[:, c - 8, :]
                v.wait_ge(g.rdy, g.r0 + c + 1)
                nc.vector.tensor_copy(tok(dst, T2), pair(c % 2, T2)).then_inc(g.free, 1)
            for c in range(10):
                t, hf = c % 5, c // 5
                m = TOK[t][1]
                v.wait_ge(g.rdy, g.r0 + 16 + c + 1)
                nc.vector.tensor_copy(FV[0:m, t, 512 * hf:512 * hf + 512], bank(2 * (c % 2), 512, parts=m)).then_inc(g.free, 1)
            v.wait_ge(fx.fl, 1)
            src = ps[0:FOX_HEADS, 2048:3072].rearrange("p (a b) -> p a b", a=2)[:, :, 0:HALF]
            nc.vector.tensor_scalar(tok(CT1, T2), src, fbias[0:FOX_HEADS, 0:1], None, ALU.add)
            v.drain()
            nc.vector.tensor_scalar(CT2, CT1, -1.0, None, ALU.mult)
            v.drain()
            nc.vector.tensor_tensor(CT2, CT1, CT2, ALU.min).then_inc(fx.fn, 1)
            nc.vector.tensor_scalar(CT1, CT1, 0.0, None, ALU.min)
            nc.vector.memset(CT3, 0.0)
            v.wait_ge(fx.fe, 1)
            nc.vector.tensor_scalar(CT2, CT2, 1.0, None, ALU.add).then_inc(fx.fs, 1)
            v.wait_ge(fx.fd, 1)
            v.drain()
            nc.vector.tensor_tensor(CT1, CT1, CT2, ALU.subtract)
            v.drain()
            nc.vector.tensor_tensor_scan(CUM[:, SEQ:T2], CT3[:, SEQ:T2], CT1[:, SEQ:T2], 0.0, ALU.add, ALU.add)
            v.drain()
            nc.vector.tensor_tensor_scan(CUM[:, 0:SEQ], CT3[:, 0:SEQ], CT1[:, 0:SEQ], CUM[:, T2 - 1:T2], ALU.add, ALU.add)
            v.drain()

        def fox_proj_scalar(act):
            act.wait_ge(fx.fn, 1)
            nc.scalar.activation(CT2, CT2, ACT.Exp).then_inc(fx.fe, 1)
            act.wait_ge(fx.fs, 1)
            nc.scalar.activation(CT2, CT2, ACT.Ln).then_inc(fx.fd, 1)

        def fox_item(n):
            j, hh = n // 2, n % 2
            q0, nq = TOK[j]
            keys = [(P * b, P * b, P, b) for b in range(j + 1)] + [(P * (j + 1), SEQ, META, 4)] if j < 4 else [(0, SEQ, META, 4)]
            return hh, q0, nq, keys, keys[-1][0] + META

        N_ITEMS = 10

        def fox_scores(pe, a, hp, n):
            hh, q0, nq, keys, nk = fox_item(n)
            pe.wait_ge(a.p, a.b.p + N_ITEMS * hp + n + 1)
            tick(pe, ps[0:1, 1024 * hh:1024 * hh + 1])
            r = slice(HD * hh, HD * (hh + 1))
            base = 1024 * hh
            runs = [(0, 0, nk - META), (nk - META, SEQ, META)] if nk > META else [(0, SEQ, META)]
            q = QC[r, q0:q0 + nq]
            d0 = (n // 2) * P if nk > META else 0
            mms = []
            for c, k0, w in runs:
                mms.append((c, w, q, KC[r, k0:k0 + w]))
            for c, k0, w in runs:
                mms.append((c, w, SELC[:, P * hh:P * hh + nq], CUM[:, k0:k0 + w]))
            mms.append((d0, nq, cs("ident", 0, nq, nq), cs("cmask", 0, nq, nq)))
            seen = set()
            last_of = {c // 512: i for i, (c, w, _, _) in enumerate(mms)}
            for i, (c, w, l, rr) in enumerate(mms):
                b = c // 512
                mm = nc.tensor.matmul(ps[0:nq, base + c:base + c + w], l, rr, start=b not in seen, stop=last_of[b] == i, skip_group_check=True)
                seen.add(b)
            mm.then_inc(a.s, 1)

        def fox_att_tensor(pe, a):
            pe.drain().then_inc(a.pt, 2)
            pe.drain().then_inc(a.o, 2)
            with pe.Fori(0, FOX_HEADS // 2) as hp:
                pe.wait_ge(a.qkv, a.b.qkv + hp + 1)
                fox_scores(pe, a, hp, 0)
                for n in range(N_ITEMS):
                    hh, q0, nq, keys, nk = fox_item(n)
                    m = N_ITEMS * hp + n
                    if n + 1 < N_ITEMS:
                        fox_scores(pe, a, hp, n + 1)
                    pe.wait_ge(a.pd, a.b.pd + m + 1)
                    pe.wait_ge(a.ptc, a.b.ptc + m + 1)
                    tick(pe, ps[0:1, 2048:2049])
                    for b, (c, _, w, _) in enumerate(keys):
                        mm = nc.tensor.transpose(ps[0:w, 2048 + P * b:2048 + P * b + nq], PF[hh][0:nq, c:c + w], cs("ident", 0, nq, nq))
                    mm.then_inc(a.pt, 1)
                    pe.wait_ge(a.ptc, a.b.ptc + m + 2)
                    pe.wait_ge(a.oc, a.b.oc + m + 1)
                    tick(pe, bank(6 + hh, 1, parts=1))
                    for b, (_, _, w, t) in enumerate(keys):
                        mm = nc.tensor.matmul(bank(6 + hh, nq), VC[0:w, t, :], PTF[hh][0:w, P * b:P * b + nq],
                                              start=(b == 0), stop=(b == len(keys) - 1))
                    mm.then_inc(a.o, 1)

        def fox_att_scalar(act, a):
            act.drain().then_inc(a.p, 2)
            act.drain().then_inc(a.ptc, 1)

            def exps(hp, n):
                hh, q0, nq, keys, nk = fox_item(n)
                m = N_ITEMS * hp + n
                act.wait_ge(a.nm, a.b.nm + m + 1)
                act.wait_ge(a.pt, a.b.pt + m + 1)
                nc.scalar.activation(PF[hh][0:nq, 0:nk], ps[0:nq, 1024 * hh:1024 * hh + nk], ACT.Exp,
                                     bias=stats[0:nq, 4 * hh + 1:4 * hh + 2], accum_out=stats[0:nq, 4 * hh + 2:4 * hh + 3]).then_inc(a.p, 1)

            with act.Fori(0, FOX_HEADS // 2) as hp:
                act.wait_ge(a.o, a.b.o + N_ITEMS * hp + 2)
                nc.scalar.copy(QC, FQ[:, hp, :])
                nc.scalar.copy(KC, FK[:, hp, :])
                nc.scalar.copy(VC[:, 0:4, :], FV[:, 0:4, ds(P * hp, P)])
                nc.scalar.copy(VC[0:META, 4, :], FV[0:META, 4, ds(P * hp, P)])
                nc.scalar.copy(SELC, SEL[:, ds(256 * hp, 256)]).then_inc(a.qkv, 1)
                exps(hp, 0)
                for n in range(N_ITEMS):
                    hh, q0, nq, keys, nk = fox_item(n)
                    m = N_ITEMS * hp + n
                    if n + 1 < N_ITEMS:
                        exps(hp, n + 1)
                    act.wait_ge(a.pt, a.b.pt + m + 3)
                    act.wait_ge(a.o, a.b.o + m + 1)
                    full = [b for b, k in enumerate(keys) if k[2] == P]
                    if full:
                        nc.scalar.copy(PTF[hh][:, 0:P * len(full)], ps[:, 2048:2048 + P * len(full)])
                    c = P * len(full)
                    nc.scalar.copy(PTF[hh][0:META, c:c + nq], ps[0:META, 2048 + c:2048 + c + nq]).then_inc(a.ptc, 1)

        def fox_att_vector(v, a):
            v.drain().then_inc(a.oc, 2)

            def top(hp, n):
                hh, q0, nq, keys, nk = fox_item(n)
                v.wait_ge(a.s, a.b.s + N_ITEMS * hp + n + 1)
                nc.vector.tensor_reduce(stats[0:nq, 4 * hh:4 * hh + 1], ps[0:nq, 1024 * hh:1024 * hh + nk], AX, ALU.max)
                v.drain()
                nc.vector.tensor_scalar(stats[0:nq, 4 * hh + 1:4 * hh + 2], stats[0:nq, 4 * hh:4 * hh + 1], -1.0, None, ALU.mult).then_inc(a.nm, 1)

            def take(hp, n):
                hh, q0, nq, keys, nk = fox_item(n)
                r = slice(HD * hh, HD * (hh + 1))
                v.wait_ge(a.o, a.b.o + N_ITEMS * hp + n + 3)
                nc.vector.tensor_copy(HT[r, hp, q0:q0 + nq], ps[r, 512 * (6 + hh):512 * (6 + hh) + nq]).then_inc(a.oc, 1)

            with v.Fori(0, FOX_HEADS // 2) as hp:
                top(hp, 0)
                for n in range(N_ITEMS):
                    hh, q0, nq, keys, nk = fox_item(n)
                    if n + 1 < N_ITEMS:
                        top(hp, n + 1)
                    v.wait_ge(a.p, a.b.p + N_ITEMS * hp + n + 3)
                    nc.vector.reciprocal(stats[0:nq, 4 * hh + 3:4 * hh + 4], stats[0:nq, 4 * hh + 2:4 * hh + 3])
                    v.drain()
                    nc.vector.tensor_scalar(PF[hh][0:nq, 0:nk], PF[hh][0:nq, 0:nk], stats[0:nq, 4 * hh + 3:4 * hh + 4], None, ALU.mult).then_inc(a.pd, 1)
                    if n:
                        take(hp, n - 1)
                take(hp, N_ITEMS - 1)

        HQ, HF, HV = FQ, FK, FV
        EE = big[:, 13568:13568 + LEVELS * SEQ].rearrange("p (l t) -> p l t", l=LEVELS)
        KE = scr_at(0, 896).rearrange("p (l t) -> p l t", l=LEVELS)
        QE = scr_at(896, 896).rearrange("p (l t) -> p l t", l=LEVELS)
        SMK = scr_at(1792, 1024).rearrange("p (l t) -> p l t", l=8)
        hk, hq, hlf, hb = scr_at(3072, T2), scr_at(3600, T2), scr_at(4128, T2), scr_at(4656, T2)
        HVC = scr_at(5184, 640).rearrange("p (t c) -> p t c", t=5)
        hqb, hkb = scr_at(5824, T2), scr_at(6352, T2)
        hst, hkt = scr_at(6880, P), scr_at(7008, P)
        EM = scr_at(7136, 64).rearrange("p (l t) -> p l t", l=4)
        hend = scr_at(7200, 8)
        MASK = cs("hgmask").rearrange("p (l t) -> p l t", l=8)
        CHUNKS = [TOK[4]] + TOK[:4]
        CT_OF = [4, 0, 1, 2, 3]
        hs = sems("hg", "lb lbe done lf sc eb ex qk s sm o kt ktc dst st oc gated")
        HG_SLOTS = (0, 1, 2, 0, 1, 2, 0, 1)

        def hg_proj_tensor(pe, g):
            for t, s in enumerate(HG_SLOTS[:4]):
                gemm_tile(pe, g, s, used[s], 4 * t, wview(s, KD, 512), KD, hrhs, T2)
                used[s] += 1
            for t, s in enumerate(HG_SLOTS[4:6]):
                gemm_tokens(pe, g, s, used[s], 16 + 5 * t, wview(s, KD, 512), TOK, par0=t)
                used[s] += 1

        def hg_proj_scalar(act, g):
            act.wait_ge(hs.lb, 1)
            nc.scalar.activation(lbc[:, 0:16], lbc[:, 0:16], ACT.Exp).then_inc(hs.lbe, 1)
            for c in range(16):
                act.wait_ge(g.rdy, g.r0 + c + 1)
                if c < 8:
                    nc.scalar.activation(tok(HQ[:, c, :], T2), pair(c % 2, T2), ACT.Silu).then_inc(g.free, 1)
                else:
                    nc.scalar.activation(tok(HF[:, c - 8, :], T2), pair(c % 2, T2), ACT.Exp,
                                         bias=lbc[:, 16 + c - 8:17 + c - 8], scale=-1.0).then_inc(g.free, 1)

        def hg_proj_vector(v, g):
            v.drain().then_inc(g.free, 2)
            nc.vector.tensor_tensor(lbc[:, 24:32], pcol("hg_lb", 0, 8), pcol("hg_lb", 8, 8), ALU.max)
            nc.vector.tensor_scalar(lbc[:, 16:24], pcol("hg_b", 0, 8), -1.0, None, ALU.mult)
            v.drain()
            for n in range(2):
                nc.vector.tensor_tensor(lbc[:, 8 * n:8 * n + 8], pcol("hg_lb", 8 * n, 8), lbc[:, 24:32], ALU.subtract)
            v.drain().then_inc(hs.lb, 1)
            v.wait_ge(hs.lbe, 1)
            nc.vector.tensor_tensor(lbc[:, 24:32], lbc[:, 0:8], lbc[:, 8:16], ALU.add)
            v.drain()
            nc.vector.reciprocal(lbc[:, 24:32], lbc[:, 24:32])
            v.drain()
            nc.vector.tensor_tensor(lbc[:, 0:8], lbc[:, 8:16], lbc[:, 24:32], ALU.mult)
            v.drain()
            nc.vector.tensor_scalar(lbc[:, 8:16], lbc[:, 0:8], -1.0, 1.0, ALU.mult, ALU.add)
            v.drain()
            for c in range(8):
                v.wait_ge(g.free, g.f0 + 2 + 8 + c + 1)
                nc.vector.tensor_scalar(HF[:, c, :], HF[:, c, :], 1.0, None, ALU.add)
                v.drain()
                nc.vector.reciprocal(HF[:, c, :], HF[:, c, :])
                v.drain()
                nc.vector.tensor_scalar(HF[:, c, :], HF[:, c, :], lbc[:, 8 + c:9 + c], lbc[:, c:c + 1], ALU.mult, ALU.add)
            for c in range(10):
                t, hf = c % 5, c // 5
                m = TOK[t][1]
                v.wait_ge(g.rdy, g.r0 + 16 + c + 1)
                nc.vector.tensor_copy(HV[0:m, t, 512 * hf:512 * hf + 512], bank(2 * (c % 2), 512, parts=m)).then_inc(g.free, 1)
            v.drain()

        def hg_scalar(act):
            with act.Fori(0, HG_HEADS) as h:
                act.wait_ge(hs.done, h + 1)
                nc.scalar.copy(hq, HQ[:, h, :])
                nc.scalar.copy(HVC[:, 0:4, :], HV[:, 0:4, ds(P * h, P)])
                nc.scalar.copy(HVC[0:META, 4, :], HV[0:META, 4, ds(P * h, P)])
                nc.scalar.activation(hlf, HF[:, h, :], ACT.Ln).then_inc(hs.lf, 1)
                act.wait_ge(hs.sc, h + 1)
                nc.scalar.activation(hqb, hb, ACT.Exp)
                for ci, (t0, n) in enumerate(CHUNKS):
                    nc.scalar.activation(hkb[:, t0:t0 + n], hb[:, t0:t0 + n], ACT.Exp, bias=hb[:, t0 + n - 1:t0 + n], scale=-1.0)
                    nc.scalar.activation(hend[:, ci:ci + 1], hb[:, t0 + n - 1:t0 + n], ACT.Exp)
                act.drain().then_inc(hs.eb, 1)
                nc.scalar.activation(EM, EM, ACT.Exp)
                nc.scalar.activation(EE, EE, ACT.Exp).then_inc(hs.ex, 1)
                for ci in range(4):
                    act.wait_ge(hs.kt, 4 * h + ci + 1)
                    act.wait_ge(hs.dst, 4 * h + ci + 1)
                    n = CHUNKS[ci][1]
                    nc.scalar.copy(hkt[0:n, :], bank(3, P, parts=n)).then_inc(hs.ktc, 1)

        def hg_vector(v):
            nc.vector.memset(scr_at(2816, P), 0.0)
            v.drain().then_inc(hs.done, 1)
            with v.Fori(0, HG_HEADS) as h:
                v.wait_ge(hs.lf, h + 1)
                nc.vector.tensor_scalar(hk, HF[:, h, :], -1.0, 1.0, ALU.mult, ALU.add)
                for t0, n in CHUNKS:
                    nc.vector.tensor_tensor_scan(hb[:, t0:t0 + n], scr_at(2816, n), hlf[:, t0:t0 + n], 0.0, ALU.add, ALU.add)
                v.drain()
                for lv in range(LEVELS):
                    L = P >> lv
                    views = [(hb[:, 0:SEQ], EE[:, lv, :])] + ([(hb[:, SEQ:T2], EM[:, lv - 3, :])] if lv >= 3 else [])
                    for b_, e_ in views:
                        b3 = b_.rearrange("p (n l) -> p n l", l=L)
                        e3 = e_.rearrange("p (n l) -> p n l", l=L)
                        nb, half = b3.shape[1], L // 2
                        ref = b3[:, :, half - 1:half].to_broadcast([P, nb, half])
                        nc.vector.tensor_tensor(e3[:, :, 0:half], ref, b3[:, :, 0:half], ALU.subtract)
                        nc.vector.tensor_tensor(e3[:, :, half:L], b3[:, :, half:L], ref, ALU.subtract)
                v.drain().then_inc(hs.sc, 1)
                v.wait_ge(hs.eb, h + 1)
                nc.vector.tensor_tensor(hqb, hqb, hq, ALU.mult)
                nc.vector.tensor_tensor(hkb, hkb, hk, ALU.mult)
                v.wait_ge(hs.ex, h + 1)
                for ci, (t0, n) in enumerate(CHUNKS):
                    m = 5 * h + ci
                    lv = LEVELS if ci else 4
                    e = EE[:, :, t0:t0 + n] if ci else EM
                    l0 = LEVELS - lv
                    nc.vector.tensor_tensor(KE[:, l0:, 0:n], e, hk[:, t0:t0 + n].unsqueeze(1).to_broadcast([P, lv, n]), ALU.mult)
                    nc.vector.tensor_tensor(QE[:, l0:, 0:n], e, hq[:, t0:t0 + n].unsqueeze(1).to_broadcast([P, lv, n]), ALU.mult).then_inc(hs.qk, 1)
                    v.wait_ge(hs.s, m + 1)
                    nc.vector.tensor_tensor(SMK[0:n, l0:, 0:n], ps[0:n, 0:1024].rearrange("p (l t) -> p l t", l=8)[:, l0:, 0:n],
                                            MASK[0:n, l0:, 0:n], ALU.mult).then_inc(hs.sm, 1)
                    if ci < 4:
                        v.wait_ge(hs.st, 4 * h + ci + 1)
                        if ci:
                            v.wait_ge(hs.o, m + 1)
                            nc.vector.scalar_tensor_tensor(hst, hst, hend[:, ci:ci + 1], bank(4, P), ALU.mult, ALU.add)
                        else:
                            nc.vector.tensor_copy(hst, bank(4, P))
                        v.drain().then_inc(hs.dst, 1)
                    v.wait_ge(hs.o, m + 1)
                    nc.vector.tensor_copy(HQ[:, h, t0:t0 + n], bank(2, n)).then_inc(hs.oc, 1)
                v.drain().then_inc(hs.done, 1)

        def hg_tensor(pe):
            pe.drain().then_inc(hs.dst, 1)
            pe.drain().then_inc(hs.oc, 1)
            with pe.Fori(0, HG_HEADS) as h:
                for ci, (t0, n) in enumerate(CHUNKS):
                    m = 5 * h + ci
                    l0 = 0 if ci else 3
                    t = CT_OF[ci]
                    pe.wait_ge(hs.qk, m + 1)
                    tick(pe, bank(0, 1, P * l0, 1))
                    for lv in range(l0, LEVELS):
                        nc.tensor.matmul(ps[0:n, P * lv:P * lv + n], KE[:, lv, 0:n], QE[:, lv, 0:n], start=True, stop=True)
                    nc.tensor.matmul(ps[0:n, P * LEVELS:P * LEVELS + n], hk[:, t0:t0 + n], hq[:, t0:t0 + n], start=True, stop=True).then_inc(hs.s, 1)
                    if ci < 4:
                        nc.tensor.transpose(bank(3, P, parts=n), hkb[:, t0:t0 + n], cs("ident")).then_inc(hs.kt, 1)
                        pe.wait_ge(hs.ktc, 4 * h + ci + 1)
                        tick(pe, bank(4, 1, parts=1))
                        nc.tensor.matmul(bank(4, P), hkt[0:n, :], HVC[0:n, t, :], start=True, stop=True).then_inc(hs.st, 1)
                    pe.wait_ge(hs.sm, m + 1)
                    pe.wait_ge(hs.oc, m + 1)
                    tick(pe, bank(2, 1, parts=1))
                    for lv in range(l0, 8):
                        mm = nc.tensor.matmul(bank(2, n), HVC[0:n, t, :], SMK[0:n, lv, 0:n], start=(lv == l0), stop=(lv == 7 and not ci))
                    if ci:
                        mm = nc.tensor.matmul(bank(2, n), hst, hqb[:, t0:t0 + n], start=False, stop=True)
                    mm.then_inc(hs.o, 1)
                    if ci < 4:
                        pe.wait_ge(hs.dst, 4 * h + ci + 2)

        def hg_gate_tensor(pe, g):
            for t, s in enumerate(HG_SLOTS[6:]):
                gemm_tile(pe, g, s, used[s], 4 * t, wview(s, KD, 512), KD, hrhs, T2)
                used[s] += 1

        def hg_gate_scalar(act, g):
            for c in range(8):
                act.wait_ge(g.rdy, g.r0 + c + 1)
                act.wait_ge(g.free, g.f0 + c + 1)
                nc.scalar.activation(tok(SQ[c % 2][:, 0:T2], T2), pair(c % 2, T2), ACT.Silu).then_inc(hs.gated, 1)

        def hg_gate_vector(v, g):
            v.drain().then_inc(g.free, 2)
            for c in range(8):
                v.wait_ge(hs.gated, c + 1)
                nc.vector.tensor_tensor(HQ[:, c, :], HQ[:, c, :], SQ[c % 2][:, 0:T2], ALU.mult).then_inc(g.free, 1)

        BT = 12288
        bt_at = [BT]

        def bt(n, parts=P):
            at_ = bt_at[0]
            bt_at[0] += n
            assert bt_at[0] <= 17152
            return big[0:parts, at_:at_ + n]

        LG = bt(180).rearrange("p (t c) -> p t c", t=5)
        G8 = bt(40).rearrange("p (t c) -> p t c", t=5)
        GM8 = bt(40).rearrange("p (t c) -> p t c", t=5)
        GI8 = bt(40).bitcast(U32).rearrange("p (t c) -> p t c", t=5)
        EM8 = bt(40).rearrange("p (t c) -> p t c", t=5)
        EI8 = bt(40).bitcast(U32).rearrange("p (t c) -> p t c", t=5)
        GX = bt(20).rearrange("p (t c) -> p t c", t=5)
        GIF = bt(5)
        IF2 = bt(10).rearrange("p (t s) -> p t s", s=2)
        GG, DV = bt(5), bt(5)
        MK = bt(160).rearrange("p (t c) -> p t c", t=5)
        ME = bt(160).rearrange("p (t c) -> p t c", t=5)
        OH = [bt(160).rearrange("p (t c) -> p t c", t=5) for _ in range(2)]
        AA = bt(160).rearrange("p (t c) -> p t c", t=5)
        RK_ = bt(160).rearrange("p (t c) -> p t c", t=5)
        CN, OV, INC, BS, ZB = bt(32), bt(32), bt(32), bt(32), bt(32)
        DF = bt(10).rearrange("p (t s) -> p t s", s=2)
        OX = bt(32 * MAX_OVER, 1).rearrange("p (j e) -> p j e", j=MAX_OVER)
        CF = bt(MAX_OVER + 1, 1)
        WR = scr_at(7296, 288).rearrange("p (k c) -> p k c", k=KD)
        BR = scr_at(7584, 36)
        XG = [scr_at(0, D, CAP), scr_at(D, D, CAP)]
        XE = [scr_at(2048 + 512 * b, KD * CAP).rearrange("p (k s) -> p k s", k=KD) for b in range(2)]
        SA = [scr_at(3072 + 256 * b, 4 * CAP) for b in range(2)]
        HE = [scr_at(3584 + 256 * b, 4 * CAP).rearrange("p (k s) -> p k s", k=4) for b in range(2)]
        YE = [scr_at(4096, D, CAP), scr_at(4096 + D, D, CAP)]
        IDX = scr_at(6144, N_EXP + MAX_OVER, CAP).bitcast(I32)
        IC = [scr_at(6200 + b, 1, CAP).bitcast(U32) for b in range(2)]
        TR = [scr_at(4096, D), scr_at(4096 + D, D)]
        YG = [[big[:, BT + D * (2 * b + s):BT + D * (2 * b + s + 1)] for s in range(2)] for b in range(2)]
        rows_d, res_d = scratch["rows"], scratch["results"]
        zi = sem("slots_cleared")
        zr = sem("overflow_results_cleared")

        MOE_ADDS = dict(big=1, wr=64, lg=1, gx=1, gxe=1, dv=1, dve=1, oh=1, rk=1, dest=1, trp=10, trc=10, trs=48, trs1=32,
                        scd=160, idx=16, xg0=8 * N_EXP, xg1=8 * N_EXP, xt=N_EXP + 2, xe=N_EXP, up=N_EXP, sa=N_EXP, he=N_EXP,
                        y=N_EXP, yc=N_EXP + 2, st0=8 * N_EXP + 16, st1=8 * N_EXP + 16, ctl=1, cg0=96, cg1=64, w=5, t=10, c=10)
        moe_s = sems("moe", " ".join(MOE_ADDS))._asdict()

        def moe_use(l):
            over = sems(f"over{l}", "ow og ope oact odve ost odone")._asdict()
            return named(o=named(**{n: l * c for n, c in MOE_ADDS.items()}), **moe_s, **over)

        def moe_sync(sp, l, m):
            up = A["moe_w_up_2"][l].rearrange("e (k p) c -> e p k c", p=P)
            dn = A["moe_w_down_2"][l].rearrange("e (k p) c -> e p k c", p=P)

            def load(e, s, nth):
                src = dn[e] if s % 3 == 2 else up[e][:, :, 512 * (s % 3):512 * (s % 3) + 512]
                fill(sp, s, src, 4 if s % 3 == 2 else KD, nth)

            for s in range(3):
                load(0, s, filled[s])
            sp.wait_ge(m.big, m.o.big + 1)
            for s in range(3, 6):
                load(1, s, filled[s])
            with sp.Fori(1, N_EXP // 2) as i:
                for s in range(6):
                    load(2 * i + s // 3, s, filled[s] + i)
            for s in range(6):
                filled[s] += N_EXP // 2
            sp.wait_ge(m.ctl, m.o.ctl + 1)
            n_over = sp.value_load(ctl[0:1, 0:1], min_val=0, max_val=MAX_OVER)
            for s in range(3):
                sp.wait_ge(w_free[s], filled[s] + 1)
            with sp.Fori(0, MAX_OVER) as j:
                with sp.If(n_over > j):
                    e = sp.value_load(ctl[0:1, ds(1 + j, 1)], min_val=0, max_val=N_EXP - 1)
                    sp.wait_ge(m.odone, j + 1)
                    for s in range(3):
                        src = dn[e] if s == 2 else up[e][:, :, 512 * s:512 * s + 512]
                        k = 4 if s == 2 else KD
                        sp.dma_start(ring[s].rearrange("p (k c) -> p k c", k=k), src).then_inc(m.ow, 16)
                sp.drain()

        def moe_gpsimd(pool, l, m):
            pool.wait_ge(m.big, m.o.big + 1)
            pool.dma_start(WR[:, :, 0:4], A["moe_w_grp_2"][l].rearrange("(k p) c -> p k c", p=P)).then_inc(m.wr, 16)
            pool.dma_start(WR[:, :, 4:36], A["moe_w_rt_2"][l].rearrange("(k p) c -> p k c", p=P)).then_inc(m.wr, 16)
            pool.dma_start(BR[:, 0:4], A["moe_b_grp_2"][l].partition_broadcast(P)).then_inc(m.wr, 16)
            pool.dma_start(BR[:, 4:36], A["moe_b_rt_2"][l].partition_broadcast(P)).then_inc(m.wr, 16)
            for t, (t0, n) in enumerate(TOK):
                pool.wait_ge(m.trc, m.o.trc + 2 * t + 2)
                pool.dma_start(rows_d[t0:t0 + n, :], TR[t % 2][0:n, :]).then_inc(m.trs if t % 2 == 0 else m.trs1, 16)
            pool.wait_ge(m.dest, m.o.dest + 1)
            pool.wait_ge(zi, 64)
            pool.wait_ge(zr, 16 * MAX_OVER)
            for t, (t0, n) in enumerate(TOK):
                for s in range(2):
                    pool.indirect_dma_start(out=scratch["slots"][l], out_offset=bass.IndirectOffsetOnAxis(ap=dest[0:n, 2 * t + s:2 * t + s + 1], axis=0),
                                            in_=tokid[0:n, t:t + 1], in_offset=None).then_inc(m.scd, 16)
            pool.wait_ge(m.scd, m.o.scd + 160)
            pool.dma_start(IDX, scratch["slots"][l].rearrange("(b s) a -> s (b a)", s=CAP), allow_slow_non_contiguous=True).then_inc(m.idx, 16)
            pool.wait_ge(m.idx, m.o.idx + 16)
            pool.wait_ge(m.trs, m.o.trs + 48)
            pool.wait_ge(m.trs1, m.o.trs1 + 32)
            with pool.Fori(0, N_EXP // 2) as i:
                for b in range(2):
                    pool.wait_ge(m.xt, m.o.xt + 2 * i + b + 1)
                    tick(pool)
                    nc.gpsimd.tensor_copy(IC[b].bitcast(I32), IDX[:, ds(2 * i + b, 1)])
                    pool.drain()
                    pool.indirect_dma_start(out=XG[b], out_offset=None, in_=rows_d[:, :],
                                            in_offset=bass.IndirectOffsetOnAxis(ap=IC[b], axis=0)).then_inc((m.xg0, m.xg1)[b], 16)
            pool.wait_ge(m.ctl, m.o.ctl + 1)
            n_over = pool.value_load(ctl[0:1, 0:1], min_val=0, max_val=MAX_OVER)
            pool.wait_ge(m.xt, m.o.xt + N_EXP + 2)
            with pool.Fori(0, MAX_OVER) as j:
                with pool.If(n_over > j):
                    nc.gpsimd.tensor_copy(IC[0].bitcast(I32), IDX[:, ds(N_EXP + j, 1)])
                    pool.drain()
                    pool.indirect_dma_start(out=XG[0], out_offset=None, in_=rows_d[:, :],
                                            in_offset=bass.IndirectOffsetOnAxis(ap=IC[0], axis=0)).then_inc(m.og, 16)
                    pool.wait_ge(m.ost, 16 * (j + 1))
                    tick(pool)
                pool.drain()
            pool.wait_ge(m.st0, m.o.st0 + 16 * (N_EXP // 2 + 1))
            pool.wait_ge(m.st1, m.o.st1 + 16 * (N_EXP // 2 + 1))
            for t, (t0, n) in enumerate(TOK):
                if t >= 2:
                    pool.wait_ge(m.w, m.o.w + t - 1)
                    pool.wait_ge(m.t, m.o.t + 2 * (t - 1))
                for s in range(2):
                    pool.indirect_dma_start(out=YG[t % 2][s][0:n, :], out_offset=None, in_=res_d[:, :],
                                            in_offset=bass.IndirectOffsetOnAxis(ap=dest[0:n, 2 * t + s:2 * t + s + 1], axis=0)).then_inc((m.cg0, m.cg1)[t % 2], 16)

        def moe_tensor(pe, l, m):
            pe.wait_ge(m.wr, m.o.wr + 64)
            for t, (t0, n) in enumerate(TOK):
                for k in range(KD):
                    mm = nc.tensor.matmul(bank(0, 36, 36 * t, n), HT[:, k, t0:t0 + n], WR[:, k, :], start=(k == 0), stop=(k == KD - 1))
            mm.then_inc(m.lg, 1)
            for t, (t0, n) in enumerate(TOK):
                for hf in range(2):
                    q = 2 * t + hf
                    if q >= 2:
                        pe.wait_ge(m.trc, m.o.trc + q - 1)
                    for c in range(4):
                        mm = nc.tensor.transpose(bank(2 + q % 2, P, P * c, n), HT[:, 4 * hf + c, t0:t0 + n], cs("ident"))
                    mm.then_inc(m.trp, 1)
            pe.wait_ge(m.oh, m.o.oh + 1)
            for t in range(5):
                for u in range(t + 1):
                    nc.tensor.matmul(bank(1, 32, 32 * t), cs("upper") if u == t else cs("ones"), AA[:, u, :], start=(u == 0), stop=(u == t))
            for u in range(5):
                mm = nc.tensor.matmul(bank(1, 32, 160), cs("ones"), AA[:, u, :], start=(u == 0), stop=(u == 4))
            mm.then_inc(m.rk, 1)
            pe.wait_ge(m.dest, m.o.dest + 1)
            pe.drain().then_inc(m.xt, 2)

            def transposed(b, xt):
                for k in range(KD):
                    mm = nc.tensor.transpose(bank(b, CAP, CAP * k), XG[b][:, P * k:P * (k + 1)], cs("ident", 0, CAP, CAP))
                mm.then_inc(xt, 1)

            def up_half(b, w, hf):
                for c in range(4):
                    for k in range(KD):
                        mm = nc.tensor.matmul(bank(2 + b, CAP, 256 * hf + CAP * c), w[:, k, P * c:P * (c + 1)], XE[b][:, k, :],
                                              start=(k == 0), stop=(k == KD - 1))
                return mm

            def down(b, w):
                for hf in range(2):
                    for k in range(4):
                        mm = nc.tensor.matmul(bank(4 + 2 * b + hf, 512, parts=CAP), HE[b][:, k, :], w[:, k, 512 * hf:512 * hf + 512],
                                              start=(k == 0), stop=(k == 3))
                return mm

            with pe.Fori(0, N_EXP // 2) as i:
                for b in range(2):
                    e = 2 * i + b
                    pe.wait_ge((m.xg0, m.xg1)[b], m.o.xg0 + 16 * (i + 1))
                    tick(pe, bank(b, 1, parts=1))
                    transposed(b, m.xt)
                    pe.wait_ge(m.xe, m.o.xe + e + 1)
                    for hf in range(2):
                        s = 3 * b + hf
                        await_tile(pe, s, used[s] + i)
                        mm = up_half(b, wview(s, KD, 512), hf)
                        if hf:
                            mm.then_inc(m.up, 1)
                        leave_tile(pe, s)
                    s = 3 * b + 2
                    await_tile(pe, s, used[s] + i)
                    pe.wait_ge(m.he, m.o.he + e + 1)
                    pe.wait_ge(m.yc, m.o.yc + e + 1)
                    tick(pe, bank(4 + 2 * b, 1, parts=1))
                    down(b, wview(s, 4, D)).then_inc(m.y, 1)
                    leave_tile(pe, s)
            for s in range(6):
                used[s] += N_EXP // 2
            n_over = pe.value_load(ctl[0:1, 0:1], min_val=0, max_val=MAX_OVER)
            pe.wait_ge(m.yc, m.o.yc + N_EXP + 2)
            pe.drain().then_inc(m.odone, 1)
            with pe.Fori(0, MAX_OVER) as j:
                with pe.If(n_over > j):
                    pe.wait_ge(m.og, 16 * (j + 1))
                    tick(pe, bank(0, 1, parts=1))
                    transposed(0, m.ope)
                    pe.wait_ge(m.oact, 2 * j + 1)
                    pe.wait_ge(m.ow, 48 * (j + 1))
                    for hf in range(2):
                        mm = up_half(0, wview(hf, KD, 512), hf)
                    mm.then_inc(m.ope, 1)
                    pe.wait_ge(m.odve, 2 * j + 1)
                    tick(pe, bank(4, 1, parts=1))
                    down(0, wview(2, 4, D)).then_inc(m.ope, 1)
                    pe.wait_ge(m.odve, 2 * j + 2)
                    tick(pe, bank(4, 1, parts=1)).then_inc(m.odone, 1)
                pe.drain()
            for t, (t0, n) in enumerate(TOK):
                pe.wait_ge(m.w, m.o.w + t + 1)
                for hf in range(2):
                    q = 2 * t + hf
                    if q >= 2:
                        pe.wait_ge(m.c, m.o.c + q - 1)
                    for c in range(4):
                        mm = nc.tensor.transpose(bank(q % 2, n, n * c), YG[t % 2][0][0:n, 512 * hf + P * c:512 * hf + P * (c + 1)], cs("ident", 0, n, n))
                    mm.then_inc(m.t, 1)

        def moe_scalar(act, l, m):
            act.wait_ge(m.gx, m.o.gx + 1)
            nc.scalar.activation(GX, GX, ACT.Exp).then_inc(m.gxe, 1)
            act.wait_ge(m.dv, m.o.dv + 1)
            nc.scalar.activation(DV, DV, ACT.Exp).then_inc(m.dve, 1)
            sts = (m.st0, m.st1)
            with act.Fori(0, N_EXP // 2) as i:
                for b in range(2):
                    e = 2 * i + b
                    act.wait_ge(m.xt, m.o.xt + e + 3)
                    nc.scalar.copy(XE[b].rearrange("p k s -> p (k s)"), bank(b, KD * CAP)).then_inc(m.xe, 1)
                    act.wait_ge(m.up, m.o.up + e + 1)
                    nc.scalar.activation(SA[b], bank(2 + b, 4 * CAP), ACT.Silu).then_inc(m.sa, 1)
                    act.wait_ge(m.yc, m.o.yc + e + 3)
                    act.dma_start(res_d[ds(CAP * e, CAP), :], YE[b]).then_inc(sts[b], 16)
            n_over = act.value_load(ctl[0:1, 0:1], min_val=0, max_val=MAX_OVER)
            act.wait_ge(m.st0, m.o.st0 + 16 * (N_EXP // 2 + 1))
            with act.Fori(0, MAX_OVER) as j:
                with act.If(n_over > j):
                    act.wait_ge(m.ope, 3 * j + 1)
                    nc.scalar.copy(XE[0].rearrange("p k s -> p (k s)"), bank(0, KD * CAP)).then_inc(m.oact, 1)
                    act.wait_ge(m.ope, 3 * j + 2)
                    nc.scalar.activation(SA[0], bank(2, 4 * CAP), ACT.Silu).then_inc(m.oact, 1)
                    act.wait_ge(m.odve, 2 * j + 2)
                    act.dma_start(res_d[ds(CAP * (N_EXP + j), CAP), :], YE[0]).then_inc(m.ost, 16)
                    act.wait_ge(m.ost, 16 * (j + 1))
                    tick(act)
                act.drain()

        def moe_vector(v, l, m):
            bc = lambda a, n: a.unsqueeze(1).to_broadcast([P, 5, n])
            bk = lambda a, n: a.to_broadcast([P, 5, n])
            iota = cs("iota")
            nc.vector.memset(LG, 0.0)
            nc.vector.memset(G8, NEG)
            nc.vector.memset(ZB, 0.0)
            v.drain()
            v.wait_ge(m.lg, m.o.lg + 1)
            nc.vector.tensor_tensor(LG[:, 0:4, :], bank(0, 144).rearrange("p (t c) -> p t c", t=4), BR.unsqueeze(1).to_broadcast([P, 4, 36]), ALU.add)
            nc.vector.tensor_tensor(LG[0:META, 4, :], bank(0, 36, 144, META), BR[0:META, :], ALU.add)
            v.drain()
            nc.vector.tensor_copy(G8[:, :, 0:4], LG[:, :, 0:4])
            v.drain()
            for t in range(5):
                nc.vector.max(GM8[:, t, :], G8[:, t, :])
            v.drain()
            for t in range(5):
                nc.vector.max_index(GI8[:, t, :], GM8[:, t, :], G8[:, t, :])
            nc.vector.tensor_tensor(GX, LG[:, :, 0:4], bk(GM8[:, :, 0:1], 4), ALU.subtract).then_inc(m.gx, 1)
            v.drain()
            nc.vector.tensor_copy(GIF, GI8[:, :, 0])
            v.drain()
            nc.vector.tensor_tensor(MK, bc(cs("iotag"), 32), bk(GIF.unsqueeze(2), 32), ALU.is_equal)
            v.drain()
            nc.vector.tensor_tensor(ME, LG[:, :, 4:36], MK, ALU.mult)
            nc.vector.tensor_scalar(MK, MK, -NEG, NEG, ALU.mult, ALU.add)
            v.drain()
            nc.vector.tensor_tensor(ME, ME, MK, ALU.add)
            v.drain()
            for t in range(5):
                nc.vector.max(EM8[:, t, :], ME[:, t, :])
            v.drain()
            for t in range(5):
                nc.vector.max_index(EI8[:, t, :], EM8[:, t, :], ME[:, t, :])
            nc.vector.tensor_tensor(DV.unsqueeze(2), EM8[:, :, 1:2], EM8[:, :, 0:1], ALU.subtract).then_inc(m.dv, 1)
            v.drain()
            nc.vector.tensor_copy(IF2, EI8[:, :, 0:2])
            v.drain()
            for s in range(2):
                nc.vector.tensor_tensor(OH[s], bc(iota, 32), bk(IF2[:, :, s:s + 1], 32), ALU.is_equal)
            v.drain()
            for s in range(2):
                nc.vector.tensor_tensor(OH[s], OH[s], bk(cs("valid").unsqueeze(2), 32), ALU.mult)
            v.drain()
            nc.vector.tensor_tensor(AA, OH[0], OH[1], ALU.add).then_inc(m.oh, 1)
            for q in range(10):
                t, hf = q // 2, q % 2
                n = TOK[t][1]
                v.wait_ge(m.trp, m.o.trp + q + 1)
                if t >= 2 and hf == 0:
                    v.wait_ge((m.trs, m.trs1)[t % 2], (m.o.trs, m.o.trs1)[t % 2] + 16 * (t // 2))
                nc.vector.tensor_copy(TR[t % 2][0:n, 512 * hf:512 * hf + 512], bank(2 + q % 2, 512, parts=n)).then_inc(m.trc, 1)
            v.wait_ge(m.gxe, m.o.gxe + 1)
            nc.vector.tensor_reduce(GG, GX, AX, ALU.add)
            v.wait_ge(m.dve, m.o.dve + 1)
            nc.vector.tensor_scalar(GIF, DV, 1.0, None, ALU.add)
            v.drain()
            nc.vector.tensor_tensor(GG, GG, GIF, ALU.mult)
            v.drain()
            nc.vector.reciprocal(gate[:, :, 0], GG)
            v.drain()
            nc.vector.tensor_tensor(gate[:, :, 1], gate[:, :, 0], DV, ALU.mult)
            v.wait_ge(m.rk, m.o.rk + 1)
            nc.vector.tensor_copy(RK_, bank(1, 160).rearrange("p (t c) -> p t c", t=5))
            nc.vector.tensor_copy(CN, bank(1, 32, 160))
            nc.vector.memset(OV, 0.0)
            for j in range(1, OVER_STEPS + 1):
                v.drain()
                nc.vector.scalar_tensor_tensor(OV, CN, float(CAP * j), OV, ALU.is_gt, ALU.add)
            v.drain()
            nc.vector.tensor_tensor_scan(INC, ZB, OV, 0.0, ALU.add, ALU.add)
            v.drain()
            nc.vector.tensor_tensor(BS, INC, OV, ALU.subtract)
            v.drain()
            nc.vector.tensor_tensor(BS, BS, iota, ALU.subtract)
            v.drain()
            nc.vector.tensor_scalar(BS, BS, float(CAP), float(CAP * (N_EXP - 1)), ALU.mult, ALU.add)
            nc.vector.tensor_scalar(MK, RK_, float(CAP), None, ALU.is_ge)
            v.drain()
            nc.vector.tensor_tensor(MK, MK, bc(BS, 32), ALU.mult)
            nc.vector.tensor_scalar(OV, iota, float(CAP), None, ALU.mult)
            v.drain()
            nc.vector.tensor_tensor(RK_, RK_, MK, ALU.add)
            v.drain()
            nc.vector.tensor_tensor(RK_, RK_, bc(OV, 32), ALU.add)
            v.drain()
            for s in range(2):
                nc.vector.tensor_tensor(OH[s], OH[s], RK_, ALU.mult)
            v.drain()
            for s in range(2):
                nc.vector.tensor_reduce(DF[:, :, s], OH[s], AX, ALU.add)
            nc.vector.tensor_tensor(OX, INC[0:1, :].unsqueeze(1).to_broadcast([1, MAX_OVER, 32]),
                                    cs("iota", 0, MAX_OVER, 1).unsqueeze(2).to_broadcast([1, MAX_OVER, 32]), ALU.is_le)
            nc.vector.tensor_copy(CF[:, 0:1], INC[0:1, 31:32])
            v.drain()
            nc.vector.tensor_copy(dest[:, :], DF.rearrange("p t s -> p (t s)"))
            nc.vector.tensor_reduce(CF[:, 1:], OX, AX, ALU.add)
            v.drain()
            nc.vector.tensor_scalar(CF[:, 1:], CF[:, 1:], float(N_EXP - 1), None, ALU.min)
            v.drain()
            nc.vector.tensor_copy(ctl[:, :], CF)
            v.drain().then_inc(m.ctl, 1)
            v.drain().then_inc(m.dest, 1)
            v.drain().then_inc(m.yc, 2)
            sts = (m.st0, m.st1)
            v.wait_ge(m.trs, m.o.trs + 48)
            v.wait_ge(m.trs1, m.o.trs1 + 32)
            for b in range(2):
                v.drain().then_inc(sts[b], 16)
            with v.Fori(0, N_EXP // 2) as i:
                for b in range(2):
                    e = 2 * i + b
                    v.wait_ge(m.sa, m.o.sa + e + 1)
                    nc.vector.tensor_tensor(HE[b].rearrange("p k s -> p (k s)"), SA[b], bank(2 + b, 4 * CAP, 256), ALU.mult).then_inc(m.he, 1)
                    v.wait_ge(m.y, m.o.y + e + 1)
                    v.wait_ge(sts[b], m.o.st0 + 16 * (i + 1))
                    nc.vector.tensor_copy(YE[b], ps[0:CAP, 512 * (4 + 2 * b):512 * (6 + 2 * b)]).then_inc(m.yc, 1)
            n_over = v.value_load(ctl[0:1, 0:1], min_val=0, max_val=MAX_OVER)
            v.wait_ge(m.st0, m.o.st0 + 16 * (N_EXP // 2 + 1))
            with v.Fori(0, MAX_OVER) as j:
                with v.If(n_over > j):
                    v.wait_ge(m.oact, 2 * j + 2)
                    nc.vector.tensor_tensor(HE[0].rearrange("p k s -> p (k s)"), SA[0], bank(2, 4 * CAP, 256), ALU.mult).then_inc(m.odve, 1)
                    v.wait_ge(m.ope, 3 * j + 3)
                    nc.vector.tensor_copy(YE[0], ps[0:CAP, 2048:3072]).then_inc(m.odve, 1)
                    v.wait_ge(m.ost, 16 * (j + 1))
                    tick(v)
                v.drain()
            for t, (t0, n) in enumerate(TOK):
                v.wait_ge((m.cg0, m.cg1)[t % 2], (m.o.cg0, m.o.cg1)[t % 2] + 32 * (t // 2 + 1))
                Y = YG[t % 2]
                nc.vector.tensor_scalar(Y[0][0:n, :], Y[0][0:n, :], gate[0:n, t, 0:1], None, ALU.mult)
                v.drain()
                nc.vector.scalar_tensor_tensor(Y[0][0:n, :], Y[1][0:n, :], gate[0:n, t, 1:2], Y[0][0:n, :], ALU.mult, ALU.add).then_inc(m.w, 1)
                for hf in range(2):
                    q = 2 * t + hf
                    v.wait_ge(m.t, m.o.t + q + 1)
                    nc.vector.tensor_tensor(XT[:, 4 * hf:4 * hf + 4, t0:t0 + n], XT[:, 4 * hf:4 * hf + 4, t0:t0 + n],
                                            bank(q % 2, 4 * n).rearrange("p (c t) -> p c t", c=4), ALU.add).then_inc(m.c, 1)
            v.drain()

        nb = [norm_use(q) for q in range(4, 8)]
        gate2 = sem("big_free2")
        ff_ = att_use(1)
        mo = [moe_use(l) for l in range(2)]
        fruns = [(8, lambda i: FQ[:, i, :], lambda i: FQ[:, i, :], gains[:, 1:2], True, False),
                 (8, lambda i: FK[:, i, :], lambda i: FK[:, i, :], pcol("fk_g"), True, False)]
        hruns = [(8, lambda i: HQ[:, i, :], lambda i: HQ[:, i, :], pcol("hg_o"), True, False)]

        def gain_of(name, l):
            return lambda k, gi: pcol(name, 8 * l + k)

        def block2_sync(sp):
            w = A["fox_w_in_2"][0].rearrange("(k p) c -> p k c", p=P)
            proj_sync(sp, w, range(0, 3 * D, 512), FOX_SLOTS)
            outproj_sync(sp, A["fox_w_out_2"][0])
            moe_sync(sp, 0, mo[0])
            if last > 4:
                w = A["hg_w_in_2"][0].rearrange("(k p) c -> p k c", p=P)
                proj_sync(sp, w, range(0, 4 * D, 512), HG_SLOTS)
                outproj_sync(sp, A["hg_w_out_2"][0])
            if last > 5:
                moe_sync(sp, 1, mo[1])

        def block2_gpsimd(pool):
            meta_gpsimd(pool, gate2)
            fox_gpsimd(pool)
            moe_gpsimd(pool, 0, mo[0])
            if last > 5:
                moe_gpsimd(pool, 1, mo[1])

        def block2_scalar(act):
            norm_scalar(act, nb[0], T2, G_T2, gain_of("fox_norm", 0), None)
            fox_proj_scalar(act)
            heads_scalar(act, hf_, fruns, T2)
            fox_att_scalar(act, ff_)
            norm_scalar(act, nb[1], T2, G_T2, gain_of("moe_norm", 0), None)
            moe_scalar(act, 0, mo[0])
            if last > 4:
                norm_scalar(act, nb[2], T2, G_T2, gain_of("hg_norm", 0), None)
                hg_proj_scalar(act, gh)
                hg_scalar(act)
                heads_scalar(act, hh_, hruns, T2)
                hg_gate_scalar(act, ghg)
            if last > 5:
                norm_scalar(act, nb[3], T2, G_T2, gain_of("moe_norm", 1), None)
                moe_scalar(act, 1, mo[1])

        def block2_tensor(pe):
            meta_tensor(pe)
            norm_tensor(pe, nb[0], T2)
            fox_proj_tensor(pe, gf)
            heads_tensor(pe, hf_, fruns, T2, cs("blk"))
            fox_att_tensor(pe, ff_)
            outproj_tensor(pe, gof, T2, hrhs)
            norm_tensor(pe, nb[1], T2)
            moe_tensor(pe, 0, mo[0])
            if last > 4:
                norm_tensor(pe, nb[2], T2)
                hg_proj_tensor(pe, gh)
                hg_tensor(pe)
                heads_tensor(pe, hh_, hruns, T2, cs("ones"))
                hg_gate_tensor(pe, ghg)
                outproj_tensor(pe, goh, T2, lambda k: HQ[:, k, :])
            if last > 5:
                norm_tensor(pe, nb[3], T2)
                moe_tensor(pe, 1, mo[1])

        def block2_vector(v):
            v.drain().then_inc(gate2, 1)
            meta_vector(v)
            norm_vector(v, nb[0], T2)
            fox_proj_vector(v, gf)
            heads_vector(v, hf_, fruns, T2, HD)
            fox_att_vector(v, ff_)
            outproj_vector(v, gof, T2, G_T2, None)
            v.drain().then_inc(mo[0].big, 1)
            norm_vector(v, nb[1], T2)
            moe_vector(v, 0, mo[0])
            if last > 4:
                norm_vector(v, nb[2], T2)
                hg_proj_vector(v, gh)
                hg_vector(v)
                heads_vector(v, hh_, hruns, T2, P)
                hg_gate_vector(v, ghg)
                outproj_vector(v, goh, T2, G_T2, None)
            if last > 5:
                v.drain().then_inc(mo[1].big, 1)
                norm_vector(v, nb[3], T2)
                moe_vector(v, 1, mo[1])

        n1, n2, n3, n4 = (norm_use(q) for q in range(4))
        g0, go0, dn0, g1, go1, dn1, gf, gof, gh, ghg, goh = (proj_use(n, o) for n, o in (
            (26, 0), (8, 1), (8, 0), (18, 0), (8, 1), (8, 0), (26, 0), (8, 1), (26, 0), (8, 0), (8, 1)))
        at0 = att_use(0)
        f0, f1 = ffn_use(0), ffn_use(1)
        gate1 = sem("big_free1")
        pl = sems("pool", "y mm done")
        rt = sems("ret", "att_free e1 e1v e2 s pv af o oc gate gated")
        zq = with_dst(l0_runs(), [lambda i: Z[:, 4 + i, :], lambda i: Z[:, 8 + i, :]])
        zo = [(4, lambda i: HT[:, 4 + i, :], lambda i: HT[:, 4 + i, :], gains[:, 2:3], True, False)]
        rq = [(2, lambda i: RQ[:, i, :], lambda i: RQ[:, i, :], gains[:, 3:4], False, True)]
        rk = [(2, lambda i: RK[:, i, :], lambda i: RK[:, i, :], 1.0, False, True)]
        ro = [(4, lambda i: HT[:, 4 + i, 0:SEQ], lambda i: HT[:, 4 + i, 0:SEQ], pcol("ret_gn"), True, False)]
        hd0, hd1, hdr, hdk, hdo, hf_, hh_ = (heads_use(r) for r in (zq, zo, rq, rk, ro, fruns, hruns))

        def y0(k):
            return Z[:, k, :] if k < 4 else HT[:, k, :]

        def scale_of(G, l):
            return lambda k, gi: G[:, l, k, gi:gi + 1]

        def shift_of(l, part):
            return lambda k, gi: modT[:, l, 8 * part + k, gi:gi + 1]

        def gate_of(l, part):
            return lambda m, gi: modT[:, l, 8 * part + m, gi:gi + 1]

        block = ctx.enter_context(nc.Block())

        @block.sync
        def _(sp):
            mod_sync(sp)
            l0_sync(sp)
            outproj_sync(sp, A["ev_w_out"][0])
            ffn_sync(sp, 0)
            down_sync(sp, 0)
            if last > 1:
                l1_sync(sp)
                outproj_sync(sp, A["od_w_out"][0])
                ffn_sync(sp, 1)
                down_sync(sp, 1)
            if last > 2:
                block2_sync(sp)
            tokout_sync(sp)

        @block.gpsimd
        def _(pool):
            prep_gpsimd(pool)
            tokin_gpsimd(pool)
            if last > 2:
                pool.dma_start(tokid[:, :], K["tokid"]).then_inc(zi, 16)
                for l in range(DEPTH):
                    pool.dma_start(scratch["slots"][l].rearrange("(b s) a -> s (b a)", s=CAP), K["zeros_i"], allow_slow_non_contiguous=True).then_inc(zi, 16)
                for j in range(MAX_OVER):
                    pool.dma_start(scratch["results"][CAP * (N_EXP + j):CAP * (N_EXP + j + 1), :], K["zero_rows"]).then_inc(zr, 16)
                pool.dma_start(fbias[0:FOX_HEADS, 1:2], A["fox_b_f_2"].rearrange("a h -> h a")).then_inc(zi, 16)
            if last > 1:
                l1_gpsimd(pool, gate1)
            if last > 2:
                block2_gpsimd(pool)

        @block.scalar
        def _(act):
            prep_scalar(act)
            norm_scalar(act, n1, TC, G_ALL, scale_of(G1, 0), shift_of(0, 0))
            heads_scalar(act, hd0, zq, TC)
            l0_att_scalar(act, at0)
            heads_scalar(act, hd1, zo, TC)
            norm_scalar(act, n2, TC, G_ALL, scale_of(G2, 0), shift_of(0, 3))
            ffn_scalar(act, f0, 0, TC)
            if last > 1:
                norm_scalar(act, n3, TC, G_ALL, scale_of(G1, 1), shift_of(1, 0))
                ret_scalar(act, rt)
                heads_scalar(act, hdo, ro, SEQ)
                act.wait_ge(rt.gate, 1)
                nc.scalar.activation(RG, RG, ACT.Silu).then_inc(rt.gated, 1)
                norm_scalar(act, n4, SEQ, G_LAT, scale_of(G2, 1), shift_of(1, 3))
                ffn_scalar(act, f1, 1, SEQ)
            if last > 2:
                block2_scalar(act)

        @block.tensor
        def _(pe):
            prep_tensor(pe)
            tokin_tensor(pe)
            mod_tensor(pe)
            norm_tensor(pe, n1, TC)
            l0_tensor(pe, g0)
            heads_tensor(pe, hd0, zq, TC, cs("blk"))
            l0_att_tensor(pe, at0)
            heads_tensor(pe, hd1, zo, TC, cs("ones"))
            outproj_tensor(pe, go0, TC, y0)
            norm_tensor(pe, n2, TC)
            ffn_tensor(pe, f0, TC)
            down_tensor(pe, f0, dn0, TC)
            if last > 1:
                norm_tensor(pe, n3, TC)
                l1_tensor(pe, g1)
                pool_tensor(pe, pl)
                heads_tensor(pe, hdr, rq, SEQ, None)
                heads_tensor(pe, hdk, rk, TC, None)
                ret_tensor(pe, rt)
                heads_tensor(pe, hdo, ro, SEQ, cs("ones"))
                outproj_tensor(pe, go1, SEQ, hrhs)
                norm_tensor(pe, n4, SEQ)
                ffn_tensor(pe, f1, SEQ)
                down_tensor(pe, f1, dn1, SEQ)
            if last > 2:
                block2_tensor(pe)
            tokout_tensor(pe)

        @block.vector
        def _(v):
            prep_vector(v)
            tokin_vector(v)
            mod_vector(v)
            norm_vector(v, n1, TC)
            l0_vector(v, g0)
            heads_vector(v, hd0, zq, TC, HD)
            l0_att_vector(v, at0)
            heads_vector(v, hd1, zo, TC, P)
            outproj_vector(v, go0, TC, G_ALL, gate_of(0, 2))
            norm_vector(v, n2, TC)
            ffn_vector(v, f0, 0, TC, G_ALL)
            down_vector(v, dn0, 0, TC, G_ALL)
            if last > 1:
                v.drain().then_inc(gate1, 1)
                norm_vector(v, n3, TC)
                l1_vector(v, g1)
                pool_vector(v, pl)
                heads_vector(v, hdr, rq, SEQ, HD)
                heads_vector(v, hdk, rk, TC, HD)
                ret_vector(v, rt)
                heads_vector(v, hdo, ro, SEQ, P)
                v.drain().then_inc(rt.gate, 1)
                v.wait_ge(rt.gated, 1)
                nc.vector.tensor_tensor(HT[:, 4:8, 0:SEQ], HT[:, 4:8, 0:SEQ], RG, ALU.mult)
                outproj_vector(v, go1, SEQ, G_LAT, gate_of(1, 2))
                norm_vector(v, n4, SEQ)
                ffn_vector(v, f1, 1, SEQ, G_LAT)
                down_vector(v, dn1, 1, SEQ, G_LAT)
            if last > 2:
                block2_vector(v)
            tokout_vector(v)


def kernel(**inputs):
    import concourse.bacc as bacc
    from concourse.bass_utils import run_bass_kernel_spmd

    nc = bacc.Bacc("TRN2", target_bir_lowering=False, num_devices=1)
    arrays, A, K = {}, {}, {}
    for name, value in inputs.items():
        a = np.ascontiguousarray(value)
        arrays[f"in_{name}"] = a
        A[name] = nc.dram_tensor(f"in_{name}", a.shape, mybir.dt.from_np(a.dtype), kind="ExternalInput").ap()
    for name, a in shape_constants().items():
        arrays[f"const_{name}"] = a
        K[name] = nc.dram_tensor(f"const_{name}", a.shape, mybir.dt.from_np(a.dtype), kind="ExternalInput").ap()
    out = nc.dram_tensor("out_0", (1, SEQ, D), F32, kind="ExternalOutput").ap()
    scratch = {
        "rows": nc.dram_tensor("expert_in", (T2, D), F32).ap(),
        "results": nc.dram_tensor("expert_out", ((N_EXP + MAX_OVER) * CAP, D), F32).ap(),
        "slots": [nc.dram_tensor(f"slot_token{l}", ((N_EXP + MAX_OVER) * CAP, 1), I32).ap() for l in range(DEPTH)],
    }
    build(nc, A, K, out, scratch, STOP)
    got = run_bass_kernel_spmd(nc, [arrays], core_ids=[0])
    return got.results[0]["out_0"]
```

```python
import math
from contextlib import ExitStack
from collections import namedtuple

import numpy as np

import concourse.bass as bass
from concourse import mybir


def named(**fields):
    return namedtuple("Named", fields)(**fields)


ALU = mybir.AluOpType
ACT = mybir.ActivationFunctionType
F32 = mybir.dt.float32
I32 = mybir.dt.int32
U32 = mybir.dt.uint32
AX = mybir.AxisListType.X
ds = bass.ds

P = 128
D = 1024
KD = D // P
SEQ = 512
CTX = 256
TC = SEQ + CTX
META = 16
T2 = SEQ + META
HALF = T2 // 2
EPS = 1e-6
FFN = 2816
KF = FFN // P
DEPTH = 2
LAM_INIT = 0.8 - 0.6 * math.exp(0.0)
NEG = -1e30
HEADS_DA = 4
HD = 64
RET_HEADS = 4
POOL_RADII = (1, 2, 4, 8)
FOX_HEADS = 16
HG_HEADS = 8
LEVELS = 7
N_GROUPS, PER_GROUP = 4, 8
N_EXP = N_GROUPS * PER_GROUP
D_EXP = 512
CAP = 64
N_ASG = 2 * T2
MAX_OVER = (N_ASG - 1) // CAP
OVER_STEPS = (T2 - 1) // CAP
TOK = [(128 * t, 128) for t in range(4)] + [(512, META)]

RING = 4096

CST = {}
_at = 0
for _n, _w in (("ident", 128), ("ones", 128), ("blk", 128), ("rot", 128), ("cmask", 128), ("upper", 128),
               ("cos", 512), ("sin", 512), ("hgmask", 1024), ("iota", 32), ("iotag", 32), ("valid", 5), ("eps", 1)):
    CST[_n] = (_at, _w)
    _at += _w
CST_W = _at

PRM = {}
PRM_ROWS = [[], [], []]


def shape_constants():
    p = np.arange(P)
    c = np.zeros((P, CST_W), np.float32)

    def put(name, a):
        at, w = CST[name]
        c[:, at:at + w] = a.reshape(P, w)

    put("ident", np.eye(P))
    put("ones", np.ones((P, P)))
    put("blk", (p[:, None] // HD == p[None, :] // HD).astype(float))
    rot = np.zeros((P, P))
    for m in range(P):
        if (m // 16) % 2 == 0:
            rot[m + 16, m] = -1.0
        else:
            rot[m - 16, m] = 1.0
    put("rot", rot)
    put("cmask", np.where(p[None, :] > p[:, None], NEG, 0.0))
    put("upper", (p[:, None] < p[None, :]).astype(float))
    d = p % HD
    inv = np.float32(10000.0) ** (-np.arange(16, dtype=np.float32) / np.float32(16))
    t = np.arange(SEQ)
    pos = np.where((d // 32 == 0)[:, None], (t // 64)[None, :], (t % 64)[None, :]).astype(np.float32)
    ang = pos * inv[d % 16][:, None]
    put("cos", np.cos(ang))
    put("sin", np.sin(ang))
    hg = np.zeros((P, 8, P))
    for lv in range(LEVELS):
        L = P >> lv
        hg[:, lv, :] = ((p[:, None] // L == p[None, :] // L) & (p[:, None] % L < L // 2) & (p[None, :] % L >= L // 2))
    hg[:, 7, :] = np.eye(P)
    put("hgmask", hg)
    put("iota", np.tile(np.arange(32), (P, 1)))
    put("iotag", np.tile(np.arange(32) // 8, (P, 1)))
    put("eps", np.full((P, 1), EPS))
    put("valid", np.stack([(p < w).astype(float) for _, w in TOK], axis=1))
    u = np.arange(896)[None, :] - 384 - p[:, None]
    i = np.arange(SEQ)[None, None, :]
    tt = np.arange(2)[None, :, None]
    pp = p[:, None, None]
    ret = np.concatenate([
        np.maximum(u, 0).reshape(P, -1), np.maximum(-u, 0).reshape(P, -1), (u >= 0).reshape(P, -1), (u <= 0).reshape(P, -1),
        (i + CTX - 128 * tt - pp).reshape(P, -1), (SEQ + 128 * tt + pp - i).reshape(P, -1)], axis=1).astype(np.float32)
    cnt = np.zeros((4, SEQ), np.float32)
    for g, r in enumerate(POOL_RADII):
        cnt[g] = 1.0 / (np.minimum(t + r + 1, SEQ) - np.maximum(t - r, 0))
    sel = np.zeros((FOX_HEADS, FOX_HEADS, P), np.float32)
    for h in range(FOX_HEADS):
        sel[h, h, :] = -1.0
    tokid = np.zeros((P, 5), np.int32)
    for n, (t0, w) in enumerate(TOK):
        tokid[:w, n] = t0 + np.arange(w)
    return {"cst": c, "ret_dist": ret, "pool_inv": np.ascontiguousarray(np.tile(cnt.reshape(1, -1), (P, 1))),
            "fox_sel": sel.reshape(FOX_HEADS, -1), "tokid": tokid, "zeros_i": np.zeros((CAP, N_EXP + MAX_OVER), np.int32),
            "zero_rows": np.zeros((CAP, D), np.float32)}


def param_rows(A):
    rows, at = [], [0, 0, 0]

    def add(stack, name, ap, n, width=P, col=0):
        if col == 0:
            PRM[name] = (stack, at[stack])
        rows.append((stack, at[stack], n, col, width, ap))
        if col + width == P:
            at[stack] += n

    add(0, "mod_b", A["mod_b"].rearrange("l (r p) -> (l r) p", p=P), 96)
    add(0, "norm1_g", A["norm1_g"].rearrange("l (r p) -> (l r) p", p=P), 16)
    add(0, "norm2_g", A["norm2_g"].rearrange("l (r p) -> (l r) p", p=P), 16)
    add(1, "conv_w0", A["ffn_conv_w"][0].rearrange("t (r p) -> (t r) p", p=P), 66)
    add(1, "conv_b", A["ffn_conv_b"].rearrange("l (r p) -> (l r) p", p=P), 44)
    add(1, "sc_w", A["sc_conv_w"][0].rearrange("t (r p) -> (t r) p", p=P), 12)
    add(1, "pool_scale", A["pool_scale"].rearrange("l (r p) -> (l r) p", p=P), 4)
    add(1, "ret_gn", A["ret_gn_g"], 1)
    add(1, "subln", A["da_subln_g"], 1)
    add(2, "conv_w1", A["ffn_conv_w"][1].rearrange("t (r p) -> (t r) p", p=P), 66)
    for name, key, n in (("fox_norm", "fox_norm_2", 8), ("hg_norm", "hg_norm_2", 8), ("hg_b", "hg_b_f_2", 8),
                         ("hg_lb", "hg_lb_logits_2", 16), ("moe_norm", "moe_norm_2", 16)):
        add(2, name, A[key].rearrange("l (r p) -> (l r) p", p=P), n)
    for name, key in (("q_g", "da_q_norm"), ("k_g", "da_k_norm"), ("fq_g", "fox_q_norm_2"), ("fk_g", "fox_k_norm_2")):
        add(2, name, A[key], 1, HD, 0)
        add(2, name, A[key], 1, HD, HD)
    add(2, "hg_o", A["hg_o_norm_2"], 1)
    add(2, "spare", A["hg_o_norm_2"], 1)
    assert at == [P, P, P], at
    return rows




def build(nc, A, K, out, scratch):
    rows = param_rows(A)
    ctx = ExitStack()
    with ctx:
        def sb(name, cols, dt=F32, parts=P):
            return ctx.enter_context(nc.sbuf_tensor(name, [parts, cols], dt))

        def sem(name):
            return ctx.enter_context(nc.semaphore(name))

        def sems(prefix, names):
            return named(**{n: sem(f"{prefix}_{n}") for n in names.split()})

        ring_sb = sb("ring_sb", 3 * RING)
        x_sb = sb("x_sb", KD * TC)
        h_sb = sb("h_sb", KD * TC)
        big = sb("big", 17152)
        cst = sb("cst", CST_W)
        prm = sb("prm", 3 * P)
        small = sb("small", 380)
        dest = sb("dest", 10, U32)
        tokid = sb("tokid", 5, I32)
        ctl = sb("ctl", MAX_OVER + 1, I32, 1)
        scr = sb("scr", 7680)
        ps = ctx.enter_context(nc.psum_tensor("ps", [P, 8 * 512], F32))

        XT = x_sb[:, :].rearrange("p (k t) -> p k t", k=KD)
        HT = h_sb[:, :].rearrange("p (k t) -> p k t", k=KD)

        def cs(name, lo=0, n=None, parts=P):
            at, w = CST[name]
            return cst[0:parts, at + lo:at + lo + (w if n is None else n)]

        def pcol(name, i=0, n=1):
            stack, at = PRM[name]
            return prm[:, ds(P * stack + at + i, n)]

        def bank(b, n, lo=0, parts=P):
            return ps[0:parts, 512 * b + lo:512 * b + lo + n]


        def tick(eng, dst=None):
            one = cs("ident", 0, 1)
            if dst is not None:
                return nc.tensor.matmul(dst, one, one, start=True, stop=True)
            if eng.engine == mybir.EngineType.Activation:
                return nc.scalar.copy(ticks[:, 0:1], one)
            if eng.engine == mybir.EngineType.Pool:
                return nc.gpsimd.tensor_tensor(ticks[:, 1:2], one, one, ALU.mult)
            return nc.vector.tensor_tensor(ticks[:, 2:3], one, one, ALU.mult)

        def scr_at(lo, n, parts=P):
            return scr[0:parts, lo:lo + n]

        SM = {}
        at = [0]

        def small_at(name, n):
            SM[name] = small[:, at[0]:at[0] + n]
            at[0] += n
            assert at[0] <= 380
            return SM[name]

        ticks = small_at("ticks", 4)
        modT = small_at("mod", 2 * 48 * 2).rearrange("p (l c g) -> p l c g", l=2, g=2)
        cT = small_at("cT", 16).rearrange("p (k g) -> p k g", g=2)
        G1 = small_at("G1", 32).rearrange("p (l k g) -> p l k g", l=2, g=2)
        G2 = small_at("G2", 32).rearrange("p (l k g) -> p l k g", l=2, g=2)
        lam = small_at("lam", 4)
        gains = small_at("gains", 4)
        stats = small_at("stats", 16)
        decay = small_at("decay", 8)
        lbc = small_at("lbc", 32)
        fbias = small_at("fbias", 1)
        gate = small_at("gate", 10).rearrange("p (t s) -> p t s", s=2)

        ring = [ring_sb[:, RING * s:RING * (s + 1)] for s in range(3)] + [big[:, RING * s:RING * (s + 1)] for s in range(3)]
        w_full = [sem(f"w_full{s}") for s in range(6)]
        w_free = [sem(f"w_free{s}") for s in range(6)]
        filled, used = [0] * 6, [0] * 6

        def fill(sp, s, src, k, nth=None):
            n = filled[s] if nth is None else nth
            sp.wait_ge(w_free[s], n + 1)
            w = src.shape[-1]
            sp.dma_start(ring[s][:, 0:k * w].rearrange("p (k c) -> p k c", k=k), src).then_inc(w_full[s], 16)
            if nth is None:
                filled[s] += 1

        def await_tile(pe, s, nth):
            pe.wait_ge(w_full[s], 16 * (nth + 1))

        def leave_tile(pe, s):
            pe.drain().then_inc(w_free[s], 1)

        def in_turns(eng, n, slots, counts, step):
            with eng.Fori(0, n // 2) as i:
                for s in (0, 1):
                    step(slots[s], counts[slots[s]] + i, 2 * i + s, s)
            for s in (0, 1):
                counts[slots[s]] += n // 2
            if n % 2:
                step(slots[0], counts[slots[0]], n - 1, 0)
                counts[slots[0]] += 1

        def wview(s, k, c):
            return ring[s][:, 0:k * c].rearrange("p (k c) -> p k c", k=k)

        SEGS = {TC: [(0, 512), (512, 256)], SEQ: [(0, 512)], T2: [(0, HALF), (HALF, HALF)]}

        def pair(p, T):
            if T == T2:
                return ps[:, 1024 * p:1024 * p + 1024].rearrange("p (a b) -> p a b", a=2)[:, :, 0:HALF]
            return ps[:, 1024 * p:1024 * p + T]

        def tok(ap, T):
            return ap.rearrange("p (a b) -> p a b", a=2) if T == T2 else ap

        proj_s = sems("proj", "rdy free src")._asdict()
        proj_at = [0, 0, 0]

        def proj_use(chunks, out=False):
            use = named(r0=proj_at[0], f0=proj_at[0] + 2 * proj_at[1], src0=proj_at[2], **proj_s)
            proj_at[0] += chunks
            proj_at[1] += 1
            proj_at[2] += out
            return use

        def gemm_tile(pe, g, s, nth, n0, w, kt, rhs, T, chunks=4, col=0, par0=0, leave=True):
            await_tile(pe, s, nth)
            for c in range(chunks):
                p = (par0 + c) % 2
                pe.wait_ge(g.free, g.f0 + n0 + c + 1)
                for k in range(kt):
                    for b, (t0, n) in enumerate(SEGS[T]):
                        m = nc.tensor.matmul(bank(2 * p + b, n), w[:, k, col + P * c:col + P * (c + 1)],
                                             rhs(k)[:, t0:t0 + n], start=(k == 0), stop=(k == kt - 1))
                m.then_inc(g.rdy, 1)
            if leave:
                leave_tile(pe, s)

        def gemm_tokens(pe, g, s, nth, n0, w, tiles, par0=0):
            await_tile(pe, s, nth)
            for c, (t0, m) in enumerate(tiles):
                p = (par0 + c) % 2
                pe.wait_ge(g.free, g.f0 + n0 + c + 1)
                for k in range(KD):
                    mm = nc.tensor.matmul(bank(2 * p, 512, parts=m), HT[:, k, t0:t0 + m], w[:, k, :],
                                          start=(k == 0), stop=(k == KD - 1))
                mm.then_inc(g.rdy, 1)
            leave_tile(pe, s)

        def hrhs(k):
            return HT[:, k, :]

        SQ = [scr_at(0, 768), scr_at(768, 768)]
        RR = scr_at(1536, 768)

        def norm_scalar(act, n, T, groups, scale, shift):
            act.wait_ge(n.go, n.q + 1)
            for k in range(KD):
                if k >= 2:
                    act.wait_ge(n.ssk, KD * n.q + k - 1)
                nc.scalar.activation(SQ[k % 2][:, 0:T], XT[:, k, 0:T], ACT.Square).then_inc(n.sq, 1)
            act.wait_ge(n.ssk, KD * (n.q + 1))
            nc.scalar.activation(tok(RR[:, 0:T], T), pair(3, T), ACT.Ln, bias=cs("eps"), scale=1.0 / D)
            act.drain()
            nc.scalar.activation(RR[:, 0:T], RR[:, 0:T], ACT.Exp, scale=-0.5).then_inc(n.root, 1)
            for k in range(KD):
                act.wait_ge(n.mul, KD * n.q + k + 1)
                for gi, (t0, t1) in enumerate(groups):
                    bias = 0.0 if shift is None else shift(k, gi)
                    a = nc.scalar.activation(HT[:, k, t0:t1], HT[:, k, t0:t1], ACT.Identity, bias=bias, scale=scale(k, gi))
                a.then_inc(n.h, 1)

        def norm_tensor(pe, n, T):
            for k in range(KD):
                pe.wait_ge(n.sq, KD * n.q + k + 1)
                for b, (t0, w) in enumerate(SEGS[T]):
                    m = nc.tensor.matmul(bank(6 + b, w), cs("ones"), SQ[k % 2][:, t0:t0 + w], start=(k == 0), stop=(k == KD - 1))
                m.then_inc(n.ssk, 1)
            pe.wait_ge(n.h, KD * (n.q + 1))

        def norm_vector(v, n, T):
            v.drain().then_inc(n.go, 1)
            v.wait_ge(n.root, n.q + 1)
            for k in range(KD):
                nc.vector.tensor_tensor(HT[:, k, 0:T], XT[:, k, 0:T], RR[:, 0:T], ALU.mult).then_inc(n.mul, 1)

        norm_s = sems("norm", "go sq ssk root mul h")._asdict()

        def norm_use(q):
            return named(q=q, **norm_s)

        HSQ, HQN, HTT = scr_at(0, 768), scr_at(1536, 768), scr_at(2304, 768)
        HRR = [scr_at(768, 768), scr_at(3072, 768)]

        def heads_gpsimd(pool, h, runs, T):
            n0 = h.norm0
            pool.wait_ge(h.fin, h.fin0 + 2)
            for cnt, src, _, _, normed, _ in runs:
                if normed:
                    with pool.Fori(0, cnt) as i:
                        pool.wait_ge(h.ss, n0 + i + 1)
                        nc.gpsimd.tensor_tensor(HSQ[:, 0:T], src(i), src(i), ALU.mult).then_inc(h.sq, 1)
                    n0 += cnt

        def heads_scalar(act, h, runs, T, width):
            n0, f0 = h.norm0, h.fin0
            if not n0:
                act.drain().then_inc(h.ms, 2)
            for cnt, src, _, _, normed, _ in runs:
                if normed:
                    with act.Fori(0, cnt // 2) as i:
                        for b in range(2):
                            act.wait_ge(h.ss, n0 + 2 * i + b + 2)
                            act.wait_ge(h.fin, f0 + 2 * i + b + 1)
                            nc.scalar.activation(tok(HRR[b][:, 0:T], T), pair(1 + b, T), ACT.Ln, bias=cs("eps"), scale=1.0 / width).then_inc(h.ms, 1)
                        act.drain()
                        for b in range(2):
                            nc.scalar.activation(HRR[b][:, 0:T], HRR[b][:, 0:T], ACT.Exp, scale=-0.5).then_inc(h.root, 1)
                    n0 += cnt
                f0 += cnt
            act.wait_ge(h.fin, f0 + 2)

        def heads_tensor(pe, h, runs, T, mat):
            n0, r0 = h.norm0, h.rot0
            if not n0:
                pe.drain().then_inc(h.ss, 1)
            for cnt, src, _, _, normed, rotated in runs:
                with pe.Fori(0, cnt // 2) as i:
                    if normed:
                        for par in range(2):
                            pe.wait_ge(h.sq, n0 + 2 * i + par + 1)
                            pe.wait_ge(h.ms, n0 + 2 * i + par + 1)
                            for b, (t0, w) in enumerate(SEGS[T]):
                                m = nc.tensor.matmul(bank(2 + 2 * par + b, w), mat, HSQ[:, t0:t0 + w], start=True, stop=True)
                            m.then_inc(h.ss, 1)
                    if rotated:
                        for par in range(2):
                            pe.wait_ge(h.qn, r0 + 2 * i + par + 1)
                            nc.tensor.matmul(bank(6, SEQ), cs("rot"), HQN[:, 0:SEQ], start=True, stop=True).then_inc(h.rot, 1)
                if normed:
                    n0 += cnt
                if rotated:
                    r0 += cnt

        def heads_vector(v, h, runs, T, width):
            n0, r0 = h.norm0, h.rot0
            v.drain().then_inc(h.fin, 2)
            for cnt, src, dst, gain, normed, rotated in runs:
                def chunk(i, par):
                    out_ap = HQN[:, 0:T] if rotated else dst(i)
                    if normed:
                        v.wait_ge(h.root, n0 + i + 1)
                        a = nc.vector.scalar_tensor_tensor(out_ap, src(i), gain, HRR[par][:, 0:T], ALU.mult, ALU.mult)
                    else:
                        a = nc.vector.tensor_scalar(out_ap, src(i), gain, None, ALU.mult)
                    if rotated:
                        a.then_inc(h.qn, 1)
                        v.drain()
                        q = dst(i)
                        nc.vector.tensor_tensor(q[:, 0:SEQ], HQN[:, 0:SEQ], cs("cos"), ALU.mult)
                        if T > SEQ:
                            nc.vector.tensor_copy(q[:, SEQ:T], HQN[:, SEQ:T])
                        v.wait_ge(h.rot, r0 + i + 1)
                        nc.vector.tensor_tensor(HTT[:, 0:SEQ], bank(6, SEQ), cs("sin"), ALU.mult)
                        v.drain()
                        nc.vector.tensor_tensor(q[:, 0:SEQ], q[:, 0:SEQ], HTT[:, 0:SEQ], ALU.add)
                    v.drain().then_inc(h.fin, 1)

                with v.Fori(0, cnt // 2) as ip:
                    for par in range(2):
                        chunk(2 * ip + par, par)
                if normed:
                    n0 += cnt
                if rotated:
                    r0 += cnt

        heads_s = sems("heads", "fin sq ss ms root qn rot")._asdict()
        heads_at = [0, 0, 0]

        def heads_use(runs):
            use = named(fin0=heads_at[0], norm0=heads_at[1], rot0=heads_at[2], **heads_s)
            heads_at[0] += 2 + sum(r[0] for r in runs)
            heads_at[1] += sum(r[0] for r in runs if r[4])
            heads_at[2] += sum(r[0] for r in runs if r[5])
            return use

        def outproj_sync(sp, w):
            for t, s in enumerate((1, 2)):
                fill(sp, s, w.rearrange("(k p) c -> p k c", p=P)[:, :, 512 * t:512 * t + 512], KD)

        def outproj_tensor(pe, g, T, rhs):
            pe.wait_ge(g.src, g.src0 + 1)
            for t, s in enumerate((1, 2)):
                gemm_tile(pe, g, s, used[s], 4 * t, wview(s, KD, 512), KD, rhs, T)
                used[s] += 1

        def add_vector(v, p, T, m, groups, gate):
            if gate is None:
                return nc.vector.tensor_tensor(tok(XT[:, m, 0:T], T), tok(XT[:, m, 0:T], T), pair(p, T), ALU.add)
            for gi, (t0, t1) in enumerate(groups):
                a = nc.vector.scalar_tensor_tensor(XT[:, m, t0:t1], ps[:, 1024 * p + t0:1024 * p + t1], gate(m, gi),
                                                   XT[:, m, t0:t1], ALU.mult, ALU.add)
            return a

        def outproj_vector(v, g, T, groups, gate):
            v.drain().then_inc(g.src, 1)
            v.drain().then_inc(g.free, 2)
            for m in range(KD):
                v.wait_ge(g.rdy, g.r0 + m + 1)
                add_vector(v, m % 2, T, m, groups, gate).then_inc(g.free, 1)

        pr = sems("prep", "row tr col c lamd lame misc cdma")
        md = sems("mod", "rdy free rows tr")

        def prep_gpsimd(pool):
            pool.dma_start(cst[:, :], K["cst"]).then_inc(pr.row, 16)
            for stack, at_, n, col, width, ap in rows:
                pool.dma_start(scr[at_:at_ + n, P * stack + col:P * stack + col + width], ap).then_inc(pr.row, 16)

        def prep_scalar(act):
            act.dma_start(scr[0:8, 512:640], A["c"].rearrange("a (k p) -> (a k) p", p=P)).then_inc(pr.cdma, 16)
            act.dma_start(scr[8:16, 512:640], A["c_ctx"].rearrange("(k p) -> k p", p=P)).then_inc(pr.cdma, 16)
            for n, key in enumerate(("da_lq1", "da_lk1", "da_lq2", "da_lk2")):
                act.dma_start(scr[:, 640 + HD * n:640 + HD * (n + 1)], A[key].partition_broadcast(P).rearrange("p a b -> p (a b)") if len(A[key].partition_broadcast(P).shape) == 3 else A[key].partition_broadcast(P)).then_inc(pr.misc, 16)
            for n, key in enumerate(("ret_decay_f", "ret_decay_b")):
                b = A[key].partition_broadcast(P)
                act.dma_start(decay[:, 4 * n:4 * n + 4], b.rearrange("p a b -> p (a b)") if len(b.shape) == 3 else b).then_inc(pr.misc, 16)
            act.dma_start(fbias[0:FOX_HEADS, 0:1], A["fox_b_f_2"].rearrange("a h -> h a")).then_inc(pr.misc, 16)
            act.wait_ge(pr.tr, 4)
            for n in range(3):
                nc.scalar.copy(prm[:, P * n:P * (n + 1)], bank(n, P))
            act.drain().then_inc(pr.col, 1)
            nc.scalar.activation(cT, bank(3, 16).rearrange("p (g k) -> p k g", g=2), ACT.Silu).then_inc(pr.c, 1)
            act.wait_ge(pr.lamd, 1)
            nc.scalar.activation(lam[:, 0:2], lam[:, 0:2], ACT.Exp)
            act.wait_ge(pr.misc, 16 * 7)
            nc.scalar.activation(decay[:, :], decay[:, :], ACT.Exp)
            act.drain().then_inc(pr.lame, 1)

        def prep_tensor(pe):
            for s in range(6):
                pe.drain().then_inc(w_free[s], 1)
            pe.wait_ge(pr.row, 16 * (1 + len(rows)))
            for n in range(3):
                nc.tensor.transpose(bank(n, P), scr_at(P * n, P), cs("ident")).then_inc(pr.tr, 1)
            pe.wait_ge(pr.cdma, 32)
            nc.tensor.transpose(bank(3, 16), scr_at(512, P, 16), cs("ident", 0, 16, 16)).then_inc(pr.tr, 1)

        def prep_vector(v):
            v.wait_ge(pr.misc, 16 * 7)
            nc.vector.tensor_tensor(scr_at(896, HD), scr_at(640, HD), scr_at(640 + HD, HD), ALU.mult)
            nc.vector.tensor_tensor(scr_at(896 + HD, HD), scr_at(640 + 2 * HD, HD), scr_at(640 + 3 * HD, HD), ALU.mult)
            v.drain()
            nc.vector.tensor_reduce(lam[:, 0:2], scr_at(896, 2 * HD).rearrange("p (a b) -> p a b", a=2), AX, ALU.add).then_inc(pr.lamd, 1)
            v.wait_ge(pr.lame, 1)
            nc.vector.tensor_tensor(lam[:, 2:3], lam[:, 0:1], lam[:, 1:2], ALU.subtract)
            nc.vector.tensor_scalar(decay[:, :], decay[:, :], -1.0, None, ALU.mult)
            v.drain()
            nc.vector.tensor_scalar(lam[:, 3:4], lam[:, 2:3], LAM_INIT, None, ALU.add)
            v.wait_ge(pr.col, 1)
            for n, (name, f) in enumerate((("q_g", HD ** -0.5), ("fq_g", HD ** -0.5), ("subln", 1.0 - LAM_INIT))):
                nc.vector.tensor_scalar(gains[:, n:n + 1], pcol(name), f, None, ALU.mult)
            nc.vector.memset(gains[:, 3:4], HD ** -0.5)
            v.drain()

        MOD_ROWS = [h_sb[0:2, 0:6 * D], big[0:2, 6 * D:12 * D]]

        def mod_sync(sp):
            for l in range(DEPTH):
                w = A["mod_w"][l].rearrange("(k p) c -> p k c", p=P)
                in_turns(sp, 12, (0, 1), filled, lambda s, nth, t, par: fill(sp, s, w[:, :, ds(512 * t, 512)], KD, nth))

        def mod_tensor(pe):
            pe.wait_ge(pr.c, 1)
            for l in range(DEPTH):
                def step(s, nth, t, par):
                    await_tile(pe, s, nth)
                    pe.wait_ge(md.free, 12 * l + t + 1)
                    for k in range(KD):
                        m = nc.tensor.matmul(bank(par, 512, parts=2), cT[:, k, :], wview(s, KD, 512)[:, k, :],
                                             start=(k == 0), stop=(k == KD - 1))
                    m.then_inc(md.rdy, 1)
                    leave_tile(pe, s)
                in_turns(pe, 12, (0, 1), used, step)
            for l in range(DEPTH):
                pe.wait_ge(md.rows, l + 1)
                for c in range(48):
                    m = nc.tensor.transpose(bank(2 + l, 2, 2 * c), MOD_ROWS[l][:, P * c:P * (c + 1)], cs("ident", 0, 2, 2))
                m.then_inc(md.tr, 1)

        def mod_scalar(act):
            act.drain().then_inc(md.free, 2)
            for l in range(DEPTH):
                def step(s, nth, t, par):
                    act.wait_ge(md.rdy, 12 * l + t + 1)
                    nc.scalar.copy(MOD_ROWS[l][:, ds(512 * t, 512)], bank(par, 512, parts=2)).then_inc(md.free, 1)
                in_turns(act, 12, (0, 1), [0] * 6, step)
                act.drain().then_inc(md.rows, 1)

        def mod_vector(v):
            for l in range(DEPTH):
                v.wait_ge(md.tr, l + 1)
                nc.vector.tensor_tensor(modT[:, l, :, :], bank(2 + l, 96).rearrange("p (c g) -> p c g", g=2),
                                        pcol("mod_b", 48 * l, 48).unsqueeze(2).to_broadcast([P, 48, 2]), ALU.add)
            v.drain()
            for l in range(DEPTH):
                for G, name, part in ((G1, "norm1_g", 1), (G2, "norm2_g", 4)):
                    nc.vector.tensor_scalar(G[:, l, :, :], modT[:, l, 8 * part:8 * part + 8, :], 1.0, None, ALU.add)
                    v.drain()
                    nc.vector.tensor_tensor(G[:, l, :, :], G[:, l, :, :],
                                            pcol(name, 8 * l, 8).unsqueeze(2).to_broadcast([P, 8, 2]), ALU.mult)
            v.drain()

        ti = sems("tokin", "x tr cp")

        def tokin_gpsimd(pool):
            for t in range(6):
                src = A["x"][0][P * t:P * (t + 1), :] if t < 4 else A["ctx"][0][P * (t - 4):P * (t - 3), :]
                pool.dma_start(big[:, D * t:D * (t + 1)], src).then_inc(ti.x, 16)

        def tokin_tensor(pe):
            pe.wait_ge(ti.x, 16 * 6)
            for t in range(6):
                for hf in range(2):
                    n = 2 * t + hf
                    if n >= 2:
                        pe.wait_ge(ti.cp, n - 1)
                    for c in range(4):
                        m = nc.tensor.transpose(bank(4 + n % 2, P, P * c), big[:, D * t + 512 * hf + P * c:D * t + 512 * hf + P * (c + 1)], cs("ident"))
                    m.then_inc(ti.tr, 1)

        def tokin_vector(v):
            for t in range(6):
                for hf in range(2):
                    n = 2 * t + hf
                    v.wait_ge(ti.tr, n + 1)
                    nc.vector.tensor_copy(XT[:, 4 * hf:4 * hf + 4, P * t:P * (t + 1)],
                                          bank(4 + n % 2, 512).rearrange("p (c t) -> p c t", c=4)).then_inc(ti.cp, 1)
            v.drain()

        GU = big[:, 0:KF * TC].rearrange("p (j t) -> p j t", j=KF)
        CA = [scr_at(0, 768), scr_at(768, 768)]
        CS = [scr_at(1536, 768), scr_at(2304, 768)]

        def ffn_sync(sp, l):
            up = A["ffn_w_up"][l].rearrange("(k p) (h c) -> h p k c", p=P, h=2)
            with sp.Fori(0, KF // 2) as i:
                for h in range(2):
                    fill(sp, h, up[h][:, :, ds(256 * i, 256)], KD, filled[h] + i)
            for h in range(2):
                filled[h] += KF // 2

        def conv_ops(v, out_ap, src, w, j, T):
            spans = [(0, SEQ)] + ([(SEQ, TC)] if T == TC else [])
            for tap in (0, 2):
                for t0, t1 in spans:
                    o = out_ap[:, t0 + 1:t1] if tap == 0 else out_ap[:, t0:t1 - 1]
                    i = src[:, t0:t1 - 1] if tap == 0 else src[:, t0 + 1:t1]
                    a = nc.vector.scalar_tensor_tensor(o, i, w(tap, j), o, ALU.mult, ALU.add)
                if tap == 0:
                    v.drain()
            return a

        def ffn_tensor(pe, f, T):
            with pe.Fori(0, KF // 2) as i:
                for jj in range(2):
                    pe.wait_ge(f.free, f.o.free + 2 * i + jj + 1)
                    for h in range(2):
                        w = wview(h, KD, 256)
                        if jj == 0:
                            await_tile(pe, h, used[h] + i)
                        for k in range(KD):
                            for b, (t0, n) in enumerate(SEGS[T]):
                                m = nc.tensor.matmul(bank(4 * jj + 2 * h + b, n), w[:, k, P * jj:P * (jj + 1)],
                                                     HT[:, k, t0:t0 + n], start=(k == 0), stop=(k == KD - 1))
                        if h == 1:
                            m.then_inc(f.rdy, 1)
                        if jj == 1:
                            leave_tile(pe, h)
            for h in range(2):
                used[h] += KF // 2
        def ffn_scalar(act, f, l, T):
            with act.Fori(0, KF // 2) as i:
                for jj in range(2):
                    n = 2 * i + jj
                    act.wait_ge(f.rdy, f.o.rdy + n + 1)
                    nc.scalar.activation(CA[jj][:, 0:T], ps[:, 2048 * jj:2048 * jj + T], ACT.Identity,
                                         bias=pcol("conv_b", KF * l + n), scale=pcol(f"conv_w{l}", KF + n)).then_inc(f.mid, 1)
                    act.wait_ge(f.conv, f.o.conv + n + 1)
                    nc.scalar.activation(CS[jj][:, 0:T], CA[jj][:, 0:T], ACT.Silu).then_inc(f.silu, 1)

        def ffn_vector(v, f, l, T, groups):
            v.drain().then_inc(f.free, 2)

            with v.Fori(0, KF // 2) as i:
                for jj in range(2):
                    n = 2 * i + jj
                    v.wait_ge(f.mid, f.o.mid + n + 1)
                    conv_ops(v, CA[jj], ps[:, 2048 * jj:2048 * jj + T], lambda tap, j: pcol(f"conv_w{l}", KF * tap + j), n, T).then_inc(f.conv, 1)
                    v.wait_ge(f.silu, f.o.silu + n + 1)
                    nc.vector.tensor_tensor(GU[:, n, 0:T], CS[jj][:, 0:T], ps[:, 2048 * jj + 1024:2048 * jj + 1024 + T], ALU.mult).then_inc(f.free, 1)

        def down_sync(sp, l):
            w = A["ffn_w_down"][l].rearrange("(k p) c -> p k c", p=P)
            in_turns(sp, KD, (2, 0), filled, lambda s, nth, t, par: fill(sp, s, w[:, :, ds(P * t, P)], KF, nth))

        def down_tensor(pe, f, g, T):
            pe.wait_ge(f.free, f.o.free + KF + 2)
            in_turns(pe, KD, (2, 0), used, lambda s, nth, t, par: gemm_tile(
                pe, g, s, nth, t, wview(s, KF, P), KF, lambda k: GU[:, k, :], T, chunks=1, par0=par))

        def down_vector(v, g, l, T, groups):
            v.drain().then_inc(g.free, 2)

            def step(s, nth, t, par):
                v.wait_ge(g.rdy, g.r0 + t + 1)
                add_vector(v, par, T, t, groups, lambda m, gi: modT[:, l, ds(40 + m, 1), gi]).then_inc(g.free, 1)
            in_turns(v, KD, (2, 0), [0] * 6, step)
            v.drain()

        ffn_s = sems("ffn", "rdy free mid conv silu")._asdict()

        def ffn_use(q):
            return named(o=named(rdy=KF * q, free=(KF + 2) * q, mid=KF * q, conv=KF * q, silu=KF * q), **ffn_s)

        Z = big[:, 0:12 * TC].rearrange("p (j t) -> p j t", j=12)
        VT = big[:, 12 * TC:12 * TC + 6 * 512].rearrange("p (t c) -> p t c", t=6)
        QH, KH = scr_at(3072, 768), scr_at(3840, 768)
        VH = scr_at(4608, 768).rearrange("p (t c) -> p t c", t=6)
        PR = scr_at(5376, 1536).rearrange("p (m t) -> p m t", m=2)
        PTR = scr_at(6912, 768)
        G_ALL = [(0, SEQ), (SEQ, TC)]
        G_LAT = [(0, SEQ)]
        TILES6 = [(P * t, P) for t in range(6)]

        def l0_sync(sp):
            w = A["ev_w_in"][0].rearrange("(k p) c -> p k c", p=P)
            for t, part in enumerate((1, 2, 0, 3, 4, 5)):
                fill(sp, t % 3, w[:, :, 512 * part:512 * part + 512], KD)

        def l0_tensor(pe, g):
            for t in range(5):
                gemm_tile(pe, g, t % 3, used[t % 3], 4 * t, wview(t % 3, KD, 512), KD, hrhs, TC)
                used[t % 3] += 1
            gemm_tokens(pe, g, 2, used[2], 20, wview(2, KD, 512), TILES6)
            used[2] += 1

        def l0_vector(v, g):
            v.drain().then_inc(g.free, 2)
            for c in range(4):
                v.wait_ge(g.rdy, g.r0 + c + 1)
                nc.vector.tensor_copy(Z[:, c, :], pair(c % 2, TC)).then_inc(g.free, 1)
            v.drain()
            for c in range(4):
                v.wait_ge(g.rdy, g.r0 + 4 + c + 1)
                nc.vector.tensor_tensor(Z[:, c, :], Z[:, c, :], pair(c % 2, TC), ALU.mult).then_inc(g.free, 1)
            v.drain()
            for c in range(4):
                nc.vector.tensor_scalar(HQN, Z[:, c, :], pcol("sc_w", 4 + c), None, ALU.mult)
                v.drain()
                conv_ops(v, HQN, Z[:, c, :], lambda tap, j: pcol("sc_w", 4 * tap + j), c, TC)
                v.drain()
                v.wait_ge(g.rdy, g.r0 + 8 + c + 1)
                nc.vector.tensor_tensor(Z[:, c, :], HQN, pair(c % 2, TC), ALU.mult).then_inc(g.free, 1)
                v.drain()
            for c in range(8):
                v.wait_ge(g.rdy, g.r0 + 12 + c + 1)
                nc.vector.tensor_copy(Z[:, 4 + c, :], pair(c % 2, TC)).then_inc(g.free, 1)
            for t in range(6):
                v.wait_ge(g.rdy, g.r0 + 20 + t + 1)
                nc.vector.tensor_copy(VT[:, t, :], bank(2 * (t % 2), 512)).then_inc(g.free, 1)

        def l0_runs():
            return [(4, lambda i: Z[:, 4 + i, :], None, gains[:, 0:1], True, True),
                    (4, lambda i: Z[:, 8 + i, :], None, pcol("k_g"), True, True)]

        def with_dst(runs, dsts):
            return [(c, s, d, g_, n, r) for (c, s, _, g_, n, r), d in zip(runs, dsts)]

        L0_Q = [(j, 0, 768) for j in range(4)] + [(j, 512, 256) for j in (4, 5)]

        att_s = sems("att", "qkv s nm p pd pt ptc o oc")._asdict()
        ATT_ADDS = dict(qkv=4, s=24, nm=24, p=25, pd=24, pt=25, ptc=24, o=25, oc=25)

        def att_use(q):
            return named(b=named(**{n: q * c for n, c in ATT_ADDS.items()}), **att_s)

        def l0_att_scalar(act, a):
            act.drain().then_inc(a.p, 1)
            with act.Fori(0, HEADS_DA) as h:
                act.wait_ge(a.o, a.b.o + 6 * h + 1)
                nc.scalar.copy(QH, Z[:, 4 + h, :])
                nc.scalar.copy(KH, Z[:, 8 + h, :])
                nc.scalar.copy(VH, VT[:, :, ds(P * h, P)]).then_inc(a.qkv, 1)
                for j, (qt, k0, nk) in enumerate(L0_Q):
                    n = 6 * h + j
                    act.wait_ge(a.nm, a.b.nm + n + 1)
                    act.wait_ge(a.pt, a.b.pt + n + 1)
                    for m in range(2):
                        e = nc.scalar.activation(PR[:, m, 0:nk], ps[:, 1024 * m:1024 * m + nk], ACT.Exp,
                                                 bias=stats[:, 2 + m:3 + m], accum_out=stats[:, 4 + m:5 + m])
                    e.then_inc(a.p, 1)
                    act.wait_ge(a.pt, a.b.pt + n + 2)
                    act.wait_ge(a.o, a.b.o + n + 1)
                    nc.scalar.copy(PTR[:, 0:nk], ps[:, 2048:2048 + nk]).then_inc(a.ptc, 1)

        def l0_att_tensor(pe, a):
            pe.drain().then_inc(a.pt, 1)
            pe.drain().then_inc(a.o, 1)
            with pe.Fori(0, HEADS_DA) as h:
                pe.wait_ge(a.qkv, a.b.qkv + h + 1)
                def scores(j):
                    qt, k0, nk = L0_Q[j]
                    pe.wait_ge(a.p, a.b.p + 6 * h + j + 1)
                    for m in range(2):
                        r = slice(HD * m, HD * (m + 1))
                        for c0 in range(0, nk, 512):
                            w = min(512, nk - c0)
                            mm = nc.tensor.matmul(bank(2 * m + c0 // 512, w), QH[r, P * qt:P * (qt + 1)],
                                                  KH[r, k0 + c0:k0 + c0 + w], start=True, stop=True)
                    mm.then_inc(a.s, 1)

                scores(0)
                for j, (qt, k0, nk) in enumerate(L0_Q):
                    n = 6 * h + j
                    if j + 1 < len(L0_Q):
                        scores(j + 1)
                    pe.wait_ge(a.pd, a.b.pd + n + 1)
                    for b in range(nk // P):
                        mm = nc.tensor.transpose(ps[:, 2048 + P * b:2048 + P * (b + 1)], PR[:, 0, P * b:P * (b + 1)], cs("ident"))
                    mm.then_inc(a.pt, 1)
                    pe.wait_ge(a.ptc, a.b.ptc + n + 1)
                    pe.wait_ge(a.oc, a.b.oc + n + 1)
                    for b in range(nk // P):
                        mm = nc.tensor.matmul(bank(6, P), VH[:, k0 // P + b, :], PTR[:, P * b:P * (b + 1)],
                                              start=(b == 0), stop=(b == nk // P - 1))
                    mm.then_inc(a.o, 1)

        def l0_att_vector(v, a):
            v.drain().then_inc(a.oc, 1)
            with v.Fori(0, HEADS_DA) as h:
                def top(j):
                    nk = L0_Q[j][2]
                    v.wait_ge(a.s, a.b.s + 6 * h + j + 1)
                    for m in range(2):
                        nc.vector.tensor_reduce(stats[:, m:m + 1], ps[:, 1024 * m:1024 * m + nk], AX, ALU.max)
                    v.drain()
                    nc.vector.tensor_scalar(stats[:, 2:4], stats[:, 0:2], -1.0, None, ALU.mult).then_inc(a.nm, 1)

                top(0)
                for j, (qt, k0, nk) in enumerate(L0_Q):
                    n = 6 * h + j
                    v.wait_ge(a.p, a.b.p + n + 2)
                    nc.vector.reciprocal(stats[:, 6:8], stats[:, 4:6])
                    v.drain()
                    nc.vector.tensor_tensor(stats[:, 7:8], stats[:, 7:8], lam[:, 3:4], ALU.mult)
                    v.drain()
                    nc.vector.tensor_scalar(PR[:, 1, 0:nk], PR[:, 1, 0:nk], stats[:, 7:8], None, ALU.mult)
                    v.drain()
                    nc.vector.scalar_tensor_tensor(PR[:, 0, 0:nk], PR[:, 0, 0:nk], stats[:, 6:7], PR[:, 1, 0:nk],
                                                   ALU.mult, ALU.subtract).then_inc(a.pd, 1)
                    if j + 1 < len(L0_Q):
                        top(j + 1)
                    v.wait_ge(a.o, a.b.o + n + 2)
                    nc.vector.tensor_copy(HT[:, 4 + h, P * qt:P * (qt + 1)], bank(6, P)).then_inc(a.oc, 1)

        PV_ = big[:, 0:4 * SEQ].rearrange("p (j t) -> p j t", j=4)
        RQ = big[:, 2048:2048 + 2 * SEQ].rearrange("p (j t) -> p j t", j=2)
        RK = big[:, 3072:3072 + 2 * TC].rearrange("p (j t) -> p j t", j=2)
        RG = big[:, 4608:4608 + 4 * SEQ].rearrange("p (j t) -> p j t", j=4)
        RV = big[:, 6656:6656 + 6 * 512].rearrange("p (t c) -> p t c", t=6)
        RD = big[:, 9728:9728 + 3584 + 2048]
        RDEC = scr_at(3072, 1920)
        RTMP = scr_at(4992, 1024)
        RATT = [scr_at(6016, 512), scr_at(6528, 512)]
        l1s = sems("l1", "dma")

        def l1_gpsimd(pool, gate):
            pool.wait_ge(gate, 1)
            pool.dma_start(RD, K["ret_dist"]).then_inc(l1s.dma, 16)
            pool.dma_start(scr_at(3072, 2048), K["pool_inv"]).then_inc(l1s.dma, 16)
            pool.dma_start(scr_at(5120, 512).rearrange("p (g c) -> p g c", g=4), A["pool_w"][0].rearrange("g p c -> p g c")).then_inc(l1s.dma, 16)

        def l1_sync(sp):
            w = A["od_w_in"][0].rearrange("(k p) c -> p k c", p=P)
            for t in range(4):
                fill(sp, (1, 2, 0, 1)[t], w[:, :, 512 * t:512 * t + 512], KD)

        def l1_tensor(pe, g):
            W = lambda s: wview(s, KD, 512)
            gemm_tile(pe, g, 1, used[1], 0, W(1), KD, hrhs, SEQ)
            used[1] += 1
            gemm_tile(pe, g, 2, used[2], 4, W(2), KD, hrhs, SEQ, chunks=2, leave=False)
            gemm_tile(pe, g, 2, used[2], 6, W(2), KD, hrhs, TC, chunks=2, col=256)
            used[2] += 1
            gemm_tokens(pe, g, 0, used[0], 8, W(0), TILES6)
            used[0] += 1
            gemm_tile(pe, g, 1, used[1], 14, W(1), KD, hrhs, SEQ)
            used[1] += 1

        def l1_vector(v, g):
            v.drain().then_inc(g.free, 2)
            for c in range(18):
                v.wait_ge(g.rdy, g.r0 + c + 1)
                src = ps[:, 1024 * (c % 2):1024 * (c % 2) + SEQ]
                if c < 4:
                    nc.vector.tensor_copy(PV_[:, c, :], src).then_inc(g.free, 1)
                elif c < 6:
                    nc.vector.tensor_copy(RQ[:, c - 4, :], src).then_inc(g.free, 1)
                elif c < 8:
                    nc.vector.tensor_copy(RK[:, c - 6, :], pair(c % 2, TC)).then_inc(g.free, 1)
                elif c < 14:
                    nc.vector.tensor_copy(RV[:, c - 8, :], src).then_inc(g.free, 1)
                else:
                    nc.vector.tensor_copy(RG[:, c - 14, :], src).then_inc(g.free, 1)

        def pool_vector(v, b):
            v.wait_ge(l1s.dma, 48)
            v.drain()
            R = max(POOL_RADII)
            run = scr_at(0, SEQ + 2 * R + 1)
            nc.vector.memset(scr_at(768, SEQ), 0.0)
            nc.vector.memset(run[:, 0:R + 1], 0.0)
            for g_, r in enumerate(POOL_RADII):
                v.drain()
                nc.vector.tensor_tensor_scan(run[:, R + 1:R + 1 + SEQ], scr_at(768, SEQ), PV_[:, g_, :], 0.0, ALU.add, ALU.add)
                v.drain()
                nc.vector.tensor_copy(run[:, R + 1 + SEQ:], run[:, R + SEQ:R + SEQ + 1].to_broadcast([P, R]))
                v.drain()
                nc.vector.tensor_tensor(scr_at(1536, SEQ), run[:, R + 1 + r:R + 1 + r + SEQ], run[:, R - r:R - r + SEQ], ALU.subtract)
                v.drain()
                nc.vector.tensor_tensor(scr_at(1536, SEQ), scr_at(1536, SEQ), scr_at(3072 + SEQ * g_, SEQ), ALU.mult)
                v.drain()
                nc.vector.tensor_tensor(PV_[:, g_, :], scr_at(1536, SEQ), PV_[:, g_, :], ALU.subtract)
            v.drain().then_inc(b.y, 1)
            for g_ in range(4):
                v.wait_ge(b.mm, g_ + 1)
                nc.vector.tensor_scalar(HT[:, g_, 0:SEQ], bank(g_, SEQ), pcol("pool_scale", g_), None, ALU.mult)
            v.drain().then_inc(b.done, 1)

        def pool_tensor(pe, b):
            pe.wait_ge(b.y, 1)
            for g_ in range(4):
                nc.tensor.matmul(bank(g_, SEQ), scr_at(5120 + P * g_, P), PV_[:, g_, :], start=True, stop=True).then_inc(b.mm, 1)

        def ret_head_decays_scalar(act, r, h):
            act.wait_ge(r.att_free, h + 1)
            nc.scalar.activation(RDEC[:, 0:896], RD[:, 0:896], ACT.Exp, scale=decay[:, ds(h, 1)])
            nc.scalar.activation(RTMP[:, 0:896], RD[:, 896:1792], ACT.Exp, scale=decay[:, ds(4 + h, 1)]).then_inc(r.e1, 1)
            nc.scalar.activation(RDEC[:, 896:1920], RD[:, 3584:4608], ACT.Exp, scale=decay[:, ds(h, 1)])
            act.wait_ge(r.e1v, h + 1)
            nc.scalar.activation(RTMP[:, 0:1024], RD[:, 4608:5632], ACT.Exp, scale=decay[:, ds(4 + h, 1)]).then_inc(r.e2, 1)

        def ret_vector(v, r):
            v.drain().then_inc(r.att_free, 1)
            v.drain().then_inc(r.af, 2)
            v.drain().then_inc(r.oc, 1)
            for h in range(RET_HEADS):
                v.wait_ge(r.e1, h + 1)
                nc.vector.tensor_tensor(RDEC[:, 0:896], RDEC[:, 0:896], RD[:, 1792:2688], ALU.mult)
                nc.vector.tensor_tensor(RTMP[:, 0:896], RTMP[:, 0:896], RD[:, 2688:3584], ALU.mult)
                v.drain()
                nc.vector.tensor_tensor(RDEC[:, 0:896], RDEC[:, 0:896], RTMP[:, 0:896], ALU.add).then_inc(r.e1v, 1)
                v.wait_ge(r.e2, h + 1)
                nc.vector.tensor_tensor(RDEC[:, 896:1920], RDEC[:, 896:1920], RTMP[:, 0:1024], ALU.add)
                v.drain()
                for t in range(6):
                    n = 6 * h + t
                    dec = RDEC[:, 384 - P * t:384 - P * t + SEQ] if t < 4 else RDEC[:, 896 + SEQ * (t - 4):896 + SEQ * (t - 3)]
                    v.wait_ge(r.s, n + 1)
                    if n >= 2:
                        v.wait_ge(r.pv, n - 1)
                    nc.vector.tensor_tensor(RATT[n % 2], bank(n % 2, SEQ), dec, ALU.mult).then_inc(r.af, 1)
                v.wait_ge(r.o, h + 1)
                nc.vector.tensor_copy(HT[:, 4 + h, 0:SEQ], bank(2, SEQ)).then_inc(r.oc, 1)
                v.drain().then_inc(r.att_free, 1)

        def ret_scalar(act, r):
            for h in range(RET_HEADS):
                ret_head_decays_scalar(act, r, h)

        def ret_tensor(pe, r):
            N = 6 * RET_HEADS

            def score(n):
                h, t = divmod(n, 6)
                pe.wait_ge(r.af, n + 1)
                rr = slice(HD * (h % 2), HD * (h % 2 + 1))
                nc.tensor.matmul(bank(n % 2, SEQ), RK[rr, h // 2, P * t:P * (t + 1)], RQ[rr, h // 2, :], start=True, stop=True).then_inc(r.s, 1)

            pe.wait_ge(r.oc, 1)
            score(0)
            for n in range(N):
                h, t = divmod(n, 6)
                if n + 1 < N:
                    score(n + 1)
                pe.wait_ge(r.af, n + 3)
                if t == 0:
                    pe.wait_ge(r.oc, h + 1)
                mm = nc.tensor.matmul(bank(2, SEQ), RV[:, t, P * h:P * (h + 1)], RATT[n % 2], start=(t == 0), stop=(t == 5))
                mm.then_inc(r.pv, 1)
                if t == 5:
                    pe.drain().then_inc(r.o, 1)

        to = sems("tokout", "go tr cp st")
        OUT = big[:, 0:4 * D].rearrange("p (t c) -> p t c", t=4)

        def tokout_tensor(pe):
            pe.wait_ge(to.go, 1)
            for t in range(4):
                for hf in range(2):
                    n = 2 * t + hf
                    if n >= 2:
                        pe.wait_ge(to.cp, n - 1)
                    for c in range(4):
                        m = nc.tensor.transpose(bank(n % 2, P, P * c), XT[:, 4 * hf + c, P * t:P * (t + 1)], cs("ident"))
                    m.then_inc(to.tr, 1)

        def tokout_vector(v):
            v.drain().then_inc(to.go, 1)
            for n in range(8):
                v.wait_ge(to.tr, n + 1)
                nc.vector.tensor_copy(OUT[:, n // 2, 512 * (n % 2):512 * (n % 2) + 512], bank(n % 2, 512)).then_inc(to.cp, 1)

        def tokout_sync(sp):
            for t in range(4):
                sp.wait_ge(to.cp, 2 * t + 2)
                sp.dma_start(out[0][P * t:P * (t + 1), :], OUT[:, t, :]).then_inc(to.st, 16)
            sp.wait_ge(to.st, 64)

        G_T2 = [(0, T2)]
        mt = sems("meta", "x tr")

        def meta_gpsimd(pool, gate_sem):
            pool.wait_ge(gate_sem, 1)
            pool.dma_start(scr_at(3072, D, META), A["meta_tokens_2"]).then_inc(mt.x, 16)

        def meta_tensor(pe):
            pe.wait_ge(mt.x, 16)
            for k in range(KD):
                m = nc.tensor.transpose(bank(0, META, META * k), scr_at(3072 + P * k, P, META), cs("ident", 0, META, META))
            m.then_inc(mt.tr, 1)

        def meta_vector(v):
            v.wait_ge(mt.tr, 1)
            nc.vector.tensor_copy(XT[:, :, SEQ:T2], bank(0, META * KD).rearrange("p (k t) -> p k t", k=KD))
            v.drain()

        FQ = big[:, 0:KD * T2].rearrange("p (j t) -> p j t", j=KD)
        FK = big[:, KD * T2:2 * KD * T2].rearrange("p (j t) -> p j t", j=KD)
        FV = big[:, 2 * KD * T2:2 * KD * T2 + 5 * D].rearrange("p (t c) -> p t c", t=5)
        SEL = big[0:FOX_HEADS, 13568:15616]
        CUM = big[0:FOX_HEADS, 15616:16144]
        CT1 = big[0:FOX_HEADS, 16144:16672]
        CT2 = scr_at(4096, T2, FOX_HEADS)
        CT3 = scr_at(4736, T2, FOX_HEADS)
        WF = big[:, 16672:16800].rearrange("p (k h) -> p k h", k=KD)
        fx = sems("fox", "dma fl fn fe fs fd")
        QC, KC = scr_at(3072, T2), scr_at(3600, T2)
        VC = scr_at(4128, 640).rearrange("p (t c) -> p t c", t=5)
        SELC = scr_at(4768, 256, FOX_HEADS)
        PF = [scr_at(5024, T2), scr_at(5552, T2)]
        PTF = [scr_at(6080, 640), scr_at(6720, 640)]

        def fox_gpsimd(pool):
            pool.dma_start(SEL, K["fox_sel"]).then_inc(fx.dma, 16)
            pool.dma_start(WF, A["fox_w_in_2"][0].rearrange("(k p) c -> p k c", p=P)[:, :, 3 * D:3 * D + FOX_HEADS]).then_inc(fx.dma, 16)

        def proj_sync(sp, w, cols, slots):
            for t, (c0, s) in enumerate(zip(cols, slots)):
                fill(sp, s, w[:, :, c0:c0 + 512], KD)

        FOX_SLOTS = (0, 1, 2, 0, 1, 2)

        def fox_proj_tensor(pe, g):
            for t, s in enumerate(FOX_SLOTS[:4]):
                gemm_tile(pe, g, s, used[s], 4 * t, wview(s, KD, 512), KD, hrhs, T2)
                used[s] += 1
            for t, s in enumerate(FOX_SLOTS[4:]):
                gemm_tokens(pe, g, s, used[s], 16 + 5 * t, wview(s, KD, 512), TOK, par0=t)
                used[s] += 1
            pe.wait_ge(fx.dma, 32)
            for b, (t0, n) in enumerate(SEGS[T2]):
                for k in range(KD):
                    m = nc.tensor.matmul(bank(4 + b, n, parts=FOX_HEADS), WF[:, k, :], HT[:, k, t0:t0 + n], start=(k == 0), stop=(k == KD - 1))
            m.then_inc(fx.fl, 1)

        def fox_proj_vector(v, g):
            v.drain().then_inc(g.free, 2)
            for c in range(16):
                dst = FQ[:, c, :] if c < 8 else FK[:, c - 8, :]
                v.wait_ge(g.rdy, g.r0 + c + 1)
                nc.vector.tensor_copy(tok(dst, T2), pair(c % 2, T2)).then_inc(g.free, 1)
            for c in range(10):
                t, hf = c % 5, c // 5
                m = TOK[t][1]
                v.wait_ge(g.rdy, g.r0 + 16 + c + 1)
                nc.vector.tensor_copy(FV[0:m, t, 512 * hf:512 * hf + 512], bank(2 * (c % 2), 512, parts=m)).then_inc(g.free, 1)
            v.wait_ge(fx.fl, 1)
            src = ps[0:FOX_HEADS, 2048:3072].rearrange("p (a b) -> p a b", a=2)[:, :, 0:HALF]
            nc.vector.tensor_scalar(tok(CT1, T2), src, fbias[0:FOX_HEADS, 0:1], None, ALU.add)
            v.drain()
            nc.vector.tensor_scalar(CT2, CT1, -1.0, None, ALU.mult)
            v.drain()
            nc.vector.tensor_tensor(CT2, CT1, CT2, ALU.min).then_inc(fx.fn, 1)
            nc.vector.tensor_scalar(CT1, CT1, 0.0, None, ALU.min)
            nc.vector.memset(CT3, 0.0)
            v.wait_ge(fx.fe, 1)
            nc.vector.tensor_scalar(CT2, CT2, 1.0, None, ALU.add).then_inc(fx.fs, 1)
            v.wait_ge(fx.fd, 1)
            v.drain()
            nc.vector.tensor_tensor(CT1, CT1, CT2, ALU.subtract)
            v.drain()
            nc.vector.tensor_tensor_scan(CUM[:, SEQ:T2], CT3[:, SEQ:T2], CT1[:, SEQ:T2], 0.0, ALU.add, ALU.add)
            v.drain()
            nc.vector.tensor_tensor_scan(CUM[:, 0:SEQ], CT3[:, 0:SEQ], CT1[:, 0:SEQ], CUM[:, T2 - 1:T2], ALU.add, ALU.add)
            v.drain()

        def fox_proj_scalar(act):
            act.wait_ge(fx.fn, 1)
            nc.scalar.activation(CT2, CT2, ACT.Exp).then_inc(fx.fe, 1)
            act.wait_ge(fx.fs, 1)
            nc.scalar.activation(CT2, CT2, ACT.Ln).then_inc(fx.fd, 1)

        def fox_item(n):
            j, hh = n // 2, n % 2
            q0, nq = TOK[j]
            keys = [(P * b, P * b, P, b) for b in range(j + 1)] + [(P * (j + 1), SEQ, META, 4)] if j < 4 else [(0, SEQ, META, 4)]
            return hh, q0, nq, keys, keys[-1][0] + META

        N_ITEMS = 10

        def fox_scores(pe, a, hp, n):
            hh, q0, nq, keys, nk = fox_item(n)
            pe.wait_ge(a.p, a.b.p + N_ITEMS * hp + n + 1)
            tick(pe, ps[0:1, 1024 * hh:1024 * hh + 1])
            r = slice(HD * hh, HD * (hh + 1))
            base = 1024 * hh
            runs = [(0, 0, nk - META), (nk - META, SEQ, META)] if nk > META else [(0, SEQ, META)]
            q = QC[r, q0:q0 + nq]
            d0 = (n // 2) * P if nk > META else 0
            mms = []
            for c, k0, w in runs:
                mms.append((c, w, q, KC[r, k0:k0 + w]))
            for c, k0, w in runs:
                mms.append((c, w, SELC[:, P * hh:P * hh + nq], CUM[:, k0:k0 + w]))
            mms.append((d0, nq, cs("ident", 0, nq, nq), cs("cmask", 0, nq, nq)))
            seen = set()
            last_of = {c // 512: i for i, (c, w, _, _) in enumerate(mms)}
            for i, (c, w, l, rr) in enumerate(mms):
                b = c // 512
                mm = nc.tensor.matmul(ps[0:nq, base + c:base + c + w], l, rr, start=b not in seen, stop=last_of[b] == i, skip_group_check=True)
                seen.add(b)
            mm.then_inc(a.s, 1)

        def fox_att_tensor(pe, a):
            pe.drain().then_inc(a.pt, 2)
            pe.drain().then_inc(a.o, 2)
            with pe.Fori(0, FOX_HEADS // 2) as hp:
                pe.wait_ge(a.qkv, a.b.qkv + hp + 1)
                fox_scores(pe, a, hp, 0)
                fox_scores(pe, a, hp, 1)
                for n in range(N_ITEMS):
                    hh, q0, nq, keys, nk = fox_item(n)
                    m = N_ITEMS * hp + n
                    pe.wait_ge(a.pd, a.b.pd + m + 1)
                    pe.wait_ge(a.ptc, a.b.ptc + m + 1)
                    tick(pe, ps[0:1, 2048:2049])
                    for b, (c, _, w, _) in enumerate(keys):
                        mm = nc.tensor.transpose(ps[0:w, 2048 + P * b:2048 + P * b + nq], PF[hh][0:nq, c:c + w], cs("ident", 0, nq, nq))
                    mm.then_inc(a.pt, 1)
                    if n + 2 < N_ITEMS:
                        fox_scores(pe, a, hp, n + 2)
                    pe.wait_ge(a.ptc, a.b.ptc + m + 2)
                    pe.wait_ge(a.oc, a.b.oc + m + 1)
                    tick(pe, bank(6 + hh, 1, parts=1))
                    for b, (_, _, w, t) in enumerate(keys):
                        mm = nc.tensor.matmul(bank(6 + hh, nq), VC[0:w, t, :], PTF[hh][0:w, P * b:P * b + nq],
                                              start=(b == 0), stop=(b == len(keys) - 1))
                    mm.then_inc(a.o, 1)

        def fox_att_scalar(act, a):
            act.drain().then_inc(a.p, 2)
            act.drain().then_inc(a.ptc, 1)

            def exps(hp, n):
                hh, q0, nq, keys, nk = fox_item(n)
                m = N_ITEMS * hp + n
                act.wait_ge(a.nm, a.b.nm + m + 1)
                act.wait_ge(a.pt, a.b.pt + m + 1)
                nc.scalar.activation(PF[hh][0:nq, 0:nk], ps[0:nq, 1024 * hh:1024 * hh + nk], ACT.Exp,
                                     bias=stats[0:nq, 4 * hh + 1:4 * hh + 2], accum_out=stats[0:nq, 4 * hh + 2:4 * hh + 3]).then_inc(a.p, 1)

            with act.Fori(0, FOX_HEADS // 2) as hp:
                act.wait_ge(a.o, a.b.o + N_ITEMS * hp + 2)
                nc.scalar.copy(QC, FQ[:, hp, :])
                nc.scalar.copy(KC, FK[:, hp, :])
                nc.scalar.copy(VC[:, 0:4, :], FV[:, 0:4, ds(P * hp, P)])
                nc.scalar.copy(VC[0:META, 4, :], FV[0:META, 4, ds(P * hp, P)])
                nc.scalar.copy(SELC, SEL[:, ds(256 * hp, 256)]).then_inc(a.qkv, 1)
                exps(hp, 0)
                for n in range(N_ITEMS):
                    hh, q0, nq, keys, nk = fox_item(n)
                    m = N_ITEMS * hp + n
                    if n + 1 < N_ITEMS:
                        exps(hp, n + 1)
                    act.wait_ge(a.pt, a.b.pt + m + 3)
                    act.wait_ge(a.o, a.b.o + m + 1)
                    full = [b for b, k in enumerate(keys) if k[2] == P]
                    if full:
                        nc.scalar.copy(PTF[hh][:, 0:P * len(full)], ps[:, 2048:2048 + P * len(full)])
                    c = P * len(full)
                    nc.scalar.copy(PTF[hh][0:META, c:c + nq], ps[0:META, 2048 + c:2048 + c + nq]).then_inc(a.ptc, 1)

        def fox_att_vector(v, a):
            v.drain().then_inc(a.oc, 2)

            def top(hp, n):
                hh, q0, nq, keys, nk = fox_item(n)
                v.wait_ge(a.s, a.b.s + N_ITEMS * hp + n + 1)
                nc.vector.tensor_reduce(stats[0:nq, 4 * hh:4 * hh + 1], ps[0:nq, 1024 * hh:1024 * hh + nk], AX, ALU.max)
                v.drain()
                nc.vector.tensor_scalar(stats[0:nq, 4 * hh + 1:4 * hh + 2], stats[0:nq, 4 * hh:4 * hh + 1], -1.0, None, ALU.mult).then_inc(a.nm, 1)

            def take(hp, n):
                hh, q0, nq, keys, nk = fox_item(n)
                r = slice(HD * hh, HD * (hh + 1))
                v.wait_ge(a.o, a.b.o + N_ITEMS * hp + n + 3)
                nc.vector.tensor_copy(HT[r, hp, q0:q0 + nq], ps[r, 512 * (6 + hh):512 * (6 + hh) + nq]).then_inc(a.oc, 1)

            with v.Fori(0, FOX_HEADS // 2) as hp:
                top(hp, 0)
                for n in range(N_ITEMS):
                    hh, q0, nq, keys, nk = fox_item(n)
                    v.wait_ge(a.p, a.b.p + N_ITEMS * hp + n + 3)
                    nc.vector.reciprocal(stats[0:nq, 4 * hh + 3:4 * hh + 4], stats[0:nq, 4 * hh + 2:4 * hh + 3])
                    v.drain()
                    nc.vector.tensor_scalar(PF[hh][0:nq, 0:nk], PF[hh][0:nq, 0:nk], stats[0:nq, 4 * hh + 3:4 * hh + 4], None, ALU.mult).then_inc(a.pd, 1)
                    if n + 1 < N_ITEMS:
                        top(hp, n + 1)
                    if n:
                        take(hp, n - 1)
                take(hp, N_ITEMS - 1)

        HQ, HF, HV = FQ, FK, FV
        EE = big[:, 13568:13568 + LEVELS * SEQ].rearrange("p (l t) -> p l t", l=LEVELS)
        KE = [scr_at(0, 896).rearrange("p (l t) -> p l t", l=LEVELS), HT[:, 0:LEVELS, T2:T2 + P]]
        QE = [scr_at(896, 896).rearrange("p (l t) -> p l t", l=LEVELS), XT[:, 0:LEVELS, T2:T2 + P]]
        SMK = scr_at(1792, 1024).rearrange("p (l t) -> p l t", l=8)
        hk, hq, hlf, hb = scr_at(3072, T2), scr_at(3600, T2), scr_at(4128, T2), scr_at(4656, T2)
        HVC = scr_at(5184, 640).rearrange("p (t c) -> p t c", t=5)
        hqb, hkb = scr_at(5824, T2), scr_at(6352, T2)
        hst, hkt = scr_at(6880, P), scr_at(7008, P)
        EM = scr_at(7136, 64).rearrange("p (l t) -> p l t", l=4)
        hend = scr_at(7200, 8)
        MASK = cs("hgmask").rearrange("p (l t) -> p l t", l=8)
        CHUNKS = [TOK[4]] + TOK[:4]
        CT_OF = [4, 0, 1, 2, 3]
        hs = sems("hg", "lb lbe done lf sc eb ex qk s sm o kt ktc dst st oc gated")
        HG_SLOTS = (0, 1, 2, 0, 1, 2, 0, 1)

        def hg_proj_tensor(pe, g):
            for t, s in enumerate(HG_SLOTS[:4]):
                gemm_tile(pe, g, s, used[s], 4 * t, wview(s, KD, 512), KD, hrhs, T2)
                used[s] += 1
            for t, s in enumerate(HG_SLOTS[4:6]):
                gemm_tokens(pe, g, s, used[s], 16 + 5 * t, wview(s, KD, 512), TOK, par0=t)
                used[s] += 1

        def hg_proj_scalar(act, g):
            act.wait_ge(hs.lb, 1)
            nc.scalar.activation(lbc[:, 0:16], lbc[:, 0:16], ACT.Exp).then_inc(hs.lbe, 1)
            for c in range(16):
                act.wait_ge(g.rdy, g.r0 + c + 1)
                if c < 8:
                    nc.scalar.activation(tok(HQ[:, c, :], T2), pair(c % 2, T2), ACT.Silu).then_inc(g.free, 1)
                else:
                    nc.scalar.activation(tok(HF[:, c - 8, :], T2), pair(c % 2, T2), ACT.Exp,
                                         bias=lbc[:, 16 + c - 8:17 + c - 8], scale=-1.0).then_inc(g.free, 1)

        def hg_proj_vector(v, g):
            v.drain().then_inc(g.free, 2)
            nc.vector.tensor_tensor(lbc[:, 24:32], pcol("hg_lb", 0, 8), pcol("hg_lb", 8, 8), ALU.max)
            nc.vector.tensor_scalar(lbc[:, 16:24], pcol("hg_b", 0, 8), -1.0, None, ALU.mult)
            v.drain()
            for n in range(2):
                nc.vector.tensor_tensor(lbc[:, 8 * n:8 * n + 8], pcol("hg_lb", 8 * n, 8), lbc[:, 24:32], ALU.subtract)
            v.drain().then_inc(hs.lb, 1)
            v.wait_ge(hs.lbe, 1)
            nc.vector.tensor_tensor(lbc[:, 24:32], lbc[:, 0:8], lbc[:, 8:16], ALU.add)
            v.drain()
            nc.vector.reciprocal(lbc[:, 24:32], lbc[:, 24:32])
            v.drain()
            nc.vector.tensor_tensor(lbc[:, 0:8], lbc[:, 8:16], lbc[:, 24:32], ALU.mult)
            v.drain()
            nc.vector.tensor_scalar(lbc[:, 8:16], lbc[:, 0:8], -1.0, 1.0, ALU.mult, ALU.add)
            v.drain()
            for c in range(8):
                v.wait_ge(g.free, g.f0 + 2 + 8 + c + 1)
                nc.vector.tensor_scalar(HF[:, c, :], HF[:, c, :], 1.0, None, ALU.add)
                v.drain()
                nc.vector.reciprocal(HF[:, c, :], HF[:, c, :])
                v.drain()
                nc.vector.tensor_scalar(HF[:, c, :], HF[:, c, :], lbc[:, 8 + c:9 + c], lbc[:, c:c + 1], ALU.mult, ALU.add)
            for c in range(10):
                t, hf = c % 5, c // 5
                m = TOK[t][1]
                v.wait_ge(g.rdy, g.r0 + 16 + c + 1)
                nc.vector.tensor_copy(HV[0:m, t, 512 * hf:512 * hf + 512], bank(2 * (c % 2), 512, parts=m)).then_inc(g.free, 1)
            v.drain()

        def hg_scalar(act):
            def head(h, following):
                act.wait_ge(hs.done, h + 1)
                nc.scalar.copy(hq, HQ[:, h, :])
                nc.scalar.copy(HVC[:, 0:4, :], HV[:, 0:4, ds(P * h, P)])
                nc.scalar.copy(HVC[0:META, 4, :], HV[0:META, 4, ds(P * h, P)])
                act.wait_ge(hs.sc, h + 1)
                nc.scalar.activation(hqb, hb, ACT.Exp)
                for ci, (t0, n) in enumerate(CHUNKS):
                    nc.scalar.activation(hkb[:, t0:t0 + n], hb[:, t0:t0 + n], ACT.Exp, bias=hb[:, t0 + n - 1:t0 + n], scale=-1.0)
                    nc.scalar.activation(hend[:, ci:ci + 1], hb[:, t0 + n - 1:t0 + n], ACT.Exp)
                act.drain().then_inc(hs.eb, 1)
                nc.scalar.activation(EM, EM, ACT.Exp).then_inc(hs.ex, 1)
                for t0, n in CHUNKS[1:]:
                    nc.scalar.activation(EE[:, :, t0:t0 + n], EE[:, :, t0:t0 + n], ACT.Exp).then_inc(hs.ex, 1)
                if following:
                    nc.scalar.activation(hlf, HF[:, h + 1, :], ACT.Ln).then_inc(hs.lf, 1)
                for ci in range(4):
                    act.wait_ge(hs.kt, 4 * h + ci + 1)
                    act.wait_ge(hs.dst, 4 * h + ci + 1)
                    n = CHUNKS[ci][1]
                    nc.scalar.copy(hkt[0:n, :], bank(3, P, parts=n)).then_inc(hs.ktc, 1)

            act.wait_ge(hs.done, 1)
            nc.scalar.activation(hlf, HF[:, 0, :], ACT.Ln).then_inc(hs.lf, 1)
            with act.Fori(0, HG_HEADS - 1) as h:
                head(h, True)
            head(HG_HEADS - 1, False)

        def hg_vector(v):
            nc.vector.memset(scr_at(2816, P), 0.0)
            v.drain().then_inc(hs.done, 1)
            with v.Fori(0, HG_HEADS) as h:
                v.wait_ge(hs.lf, h + 1)
                nc.vector.tensor_scalar(hk, HF[:, h, :], -1.0, 1.0, ALU.mult, ALU.add)
                for t0, n in CHUNKS:
                    nc.vector.tensor_tensor_scan(hb[:, t0:t0 + n], scr_at(2816, n), hlf[:, t0:t0 + n], 0.0, ALU.add, ALU.add)
                v.drain()
                for lv in range(LEVELS):
                    L = P >> lv
                    views = [(hb[:, 0:SEQ], EE[:, lv, :])] + ([(hb[:, SEQ:T2], EM[:, lv - 3, :])] if lv >= 3 else [])
                    for b_, e_ in views:
                        b3 = b_.rearrange("p (n l) -> p n l", l=L)
                        e3 = e_.rearrange("p (n l) -> p n l", l=L)
                        nb, half = b3.shape[1], L // 2
                        ref = b3[:, :, half - 1:half].to_broadcast([P, nb, half])
                        nc.vector.tensor_tensor(e3[:, :, 0:half], ref, b3[:, :, 0:half], ALU.subtract)
                        nc.vector.tensor_tensor(e3[:, :, half:L], b3[:, :, half:L], ref, ALU.subtract)
                v.drain().then_inc(hs.sc, 1)
                v.wait_ge(hs.eb, h + 1)
                nc.vector.tensor_tensor(hqb, hqb, hq, ALU.mult)
                nc.vector.tensor_tensor(hkb, hkb, hk, ALU.mult)

                def decayed(ci):
                    t0, n = CHUNKS[ci]
                    v.wait_ge(hs.ex, 5 * h + ci + 1)
                    lv = LEVELS if ci else 4
                    e = EE[:, :, t0:t0 + n] if ci else EM
                    l0 = LEVELS - lv
                    nc.vector.tensor_tensor(KE[ci % 2][:, l0:, 0:n], e, hk[:, t0:t0 + n].unsqueeze(1).to_broadcast([P, lv, n]), ALU.mult)
                    nc.vector.tensor_tensor(QE[ci % 2][:, l0:, 0:n], e, hq[:, t0:t0 + n].unsqueeze(1).to_broadcast([P, lv, n]), ALU.mult).then_inc(hs.qk, 1)

                decayed(0)
                for ci, (t0, n) in enumerate(CHUNKS):
                    m = 5 * h + ci
                    l0 = 0 if ci else 3
                    if ci < 4:
                        decayed(ci + 1)
                    v.wait_ge(hs.s, m + 1)
                    nc.vector.tensor_tensor(SMK[0:n, l0:, 0:n], ps[0:n, 3072 * (ci % 2):3072 * (ci % 2) + 1024].rearrange("p (l t) -> p l t", l=8)[:, l0:, 0:n],
                                            MASK[0:n, l0:, 0:n], ALU.mult).then_inc(hs.sm, 1)
                    if ci < 4:
                        v.wait_ge(hs.st, 4 * h + ci + 1)
                        if ci:
                            v.wait_ge(hs.o, m + 1)
                            nc.vector.scalar_tensor_tensor(hst, hst, hend[:, ci:ci + 1], bank(4, P), ALU.mult, ALU.add)
                        else:
                            nc.vector.tensor_copy(hst, bank(4, P))
                        v.drain().then_inc(hs.dst, 1)
                    v.wait_ge(hs.o, m + 1)
                    nc.vector.tensor_copy(HQ[:, h, t0:t0 + n], bank(2, n)).then_inc(hs.oc, 1)
                v.drain().then_inc(hs.done, 1)

        def hg_tensor(pe):
            pe.drain().then_inc(hs.dst, 1)
            pe.drain().then_inc(hs.oc, 1)

            def hg_scores(h, ci):
                t0, n = CHUNKS[ci]
                at_ = 3072 * (ci % 2)
                l0 = 0 if ci else 3
                pe.wait_ge(hs.qk, 5 * h + ci + 1)
                tick(pe, ps[0:1, at_ + P * l0:at_ + P * l0 + 1])
                for lv in range(l0, LEVELS):
                    nc.tensor.matmul(ps[0:n, at_ + P * lv:at_ + P * lv + n], KE[ci % 2][:, lv, 0:n], QE[ci % 2][:, lv, 0:n], start=True, stop=True)
                nc.tensor.matmul(ps[0:n, at_ + P * LEVELS:at_ + P * LEVELS + n], hk[:, t0:t0 + n], hq[:, t0:t0 + n], start=True, stop=True).then_inc(hs.s, 1)

            with pe.Fori(0, HG_HEADS) as h:
                hg_scores(h, 0)
                for ci, (t0, n) in enumerate(CHUNKS):
                    m = 5 * h + ci
                    l0 = 0 if ci else 3
                    t = CT_OF[ci]
                    if ci < 4:
                        nc.tensor.transpose(bank(3, P, parts=n), hkb[:, t0:t0 + n], cs("ident")).then_inc(hs.kt, 1)
                        hg_scores(h, ci + 1)
                        pe.wait_ge(hs.ktc, 4 * h + ci + 1)
                    pe.wait_ge(hs.dst, 4 * h + ci + 1)
                    tick(pe, bank(4, 1, parts=1))
                    if ci < 4:
                        nc.tensor.matmul(bank(4, P), hkt[0:n, :], HVC[0:n, t, :], start=True, stop=True).then_inc(hs.st, 1)
                    pe.wait_ge(hs.sm, m + 1)
                    pe.wait_ge(hs.oc, m + 1)
                    tick(pe, bank(2, 1, parts=1))
                    for lv in range(l0, 8):
                        mm = nc.tensor.matmul(bank(2, n), HVC[0:n, t, :], SMK[0:n, lv, 0:n], start=(lv == l0), stop=(lv == 7 and not ci))
                    if ci:
                        mm = nc.tensor.matmul(bank(2, n), hst, hqb[:, t0:t0 + n], start=False, stop=True)
                    mm.then_inc(hs.o, 1)

        def hg_gate_tensor(pe, g):
            for t, s in enumerate(HG_SLOTS[6:]):
                gemm_tile(pe, g, s, used[s], 4 * t, wview(s, KD, 512), KD, hrhs, T2)
                used[s] += 1

        def hg_gate_scalar(act, g):
            for c in range(8):
                act.wait_ge(g.rdy, g.r0 + c + 1)
                act.wait_ge(g.free, g.f0 + c + 1)
                nc.scalar.activation(tok(SQ[c % 2][:, 0:T2], T2), pair(c % 2, T2), ACT.Silu).then_inc(hs.gated, 1)

        def hg_gate_vector(v, g):
            v.drain().then_inc(g.free, 2)
            for c in range(8):
                v.wait_ge(hs.gated, c + 1)
                nc.vector.tensor_tensor(HQ[:, c, :], HQ[:, c, :], SQ[c % 2][:, 0:T2], ALU.mult).then_inc(g.free, 1)

        BT = 12288
        bt_at = [BT]

        def bt(n, parts=P):
            at_ = bt_at[0]
            bt_at[0] += n
            assert bt_at[0] <= 17152
            return big[0:parts, at_:at_ + n]

        LG = bt(180).rearrange("p (t c) -> p t c", t=5)
        G8 = bt(40).rearrange("p (t c) -> p t c", t=5)
        GM8 = bt(40).rearrange("p (t c) -> p t c", t=5)
        GI8 = bt(40).bitcast(U32).rearrange("p (t c) -> p t c", t=5)
        EM8 = bt(40).rearrange("p (t c) -> p t c", t=5)
        EI8 = bt(40).bitcast(U32).rearrange("p (t c) -> p t c", t=5)
        GX = bt(20).rearrange("p (t c) -> p t c", t=5)
        GIF = bt(5)
        IF2 = bt(10).rearrange("p (t s) -> p t s", s=2)
        GG, DV = bt(5), bt(5)
        MK = bt(160).rearrange("p (t c) -> p t c", t=5)
        ME = bt(160).rearrange("p (t c) -> p t c", t=5)
        OH = [bt(160).rearrange("p (t c) -> p t c", t=5) for _ in range(2)]
        AA = bt(160).rearrange("p (t c) -> p t c", t=5)
        RK_ = bt(160).rearrange("p (t c) -> p t c", t=5)
        CN, OV, INC, BS, ZB = bt(32), bt(32), bt(32), bt(32), bt(32)
        DF = bt(10).rearrange("p (t s) -> p t s", s=2)
        OX = bt(32 * MAX_OVER, 1).rearrange("p (j e) -> p j e", j=MAX_OVER)
        CF = bt(MAX_OVER + 1, 1)
        WR = scr_at(7296, 288).rearrange("p (k c) -> p k c", k=KD)
        BR = scr_at(7584, 36)
        XG = [scr_at(0, D), scr_at(D, D)]
        XE = [scr_at(2048 + D * u, D).rearrange("p (k s) -> p k s", k=KD) for u in range(2)]
        SA = [scr_at(6300 + 256 * b, 4 * CAP) for b in range(2)]
        HE = [h_sb[:, 4 * D + 256 * b:4 * D + 256 * (b + 1)].rearrange("p (k s) -> p k s", k=4) for b in range(2)]
        YE = [h_sb[0:CAP, D * q:D * (q + 1)] for q in range(4)]
        IDX = scr_at(6144, N_EXP // 2).bitcast(I32)
        IDXO = scr_at(6164, MAX_OVER, CAP).bitcast(I32)
        IC = [scr_at(6200 + b, 1).bitcast(U32) for b in range(2)]
        XO = scr_at(2048, KD * CAP).rearrange("p (k s) -> p k s", k=KD)
        TR = [scr_at(4096, D), scr_at(4096 + D, D)]
        YG = [[big[:, BT + D * (2 * b + s):BT + D * (2 * b + s + 1)] for s in range(2)] for b in range(2)]
        rows_d, res_d = scratch["rows"], scratch["results"]
        zi = sem("slots_cleared")
        zr = sem("overflow_results_cleared")

        QUADS = N_EXP // 4

        MOE_ADDS = dict(big=1, wr=64, lg=1, gx=1, gxe=1, dv=1, dve=1, oh=1, rk=1, dest=1, trp=10, trc=10, trs=48, trs1=32,
                        scd=160, idx=32, xg0=16 * QUADS, xg1=16 * QUADS, xt=2 * QUADS, xe=2 * QUADS, up=N_EXP, sa=N_EXP,
                        he=N_EXP, y=N_EXP, yc=N_EXP + 2, st0=16 * (QUADS + 1), st1=16 * (QUADS + 1), st2=16 * (QUADS + 1),
                        st3=16 * (QUADS + 1), ctl=1, cg0=96, cg1=64, w=5, t=10, c=10)
        moe_s = sems("moe", " ".join(MOE_ADDS))._asdict()

        def moe_use(l):
            over = sems(f"over{l}", "ow og ope oact odve ost odone")._asdict()
            return named(o=named(**{n: l * c for n, c in MOE_ADDS.items()}), **moe_s, **over)

        def moe_sync(sp, l, m):
            up = A["moe_w_up_2"][l].rearrange("e (k p) c -> e p k c", p=P)
            dn = A["moe_w_down_2"][l].rearrange("e (k p) c -> e p k c", p=P)

            def load(e, s, nth):
                src = dn[e] if s % 3 == 2 else up[e][:, :, 512 * (s % 3):512 * (s % 3) + 512]
                fill(sp, s, src, 4 if s % 3 == 2 else KD, nth)

            for s in range(3):
                load(0, s, filled[s])
            sp.wait_ge(m.big, m.o.big + 1)
            for s in range(3, 6):
                load(1, s, filled[s])
            with sp.Fori(1, N_EXP // 2) as i:
                for s in (0, 1, 3, 4, 2, 5):
                    load(2 * i + s // 3, s, filled[s] + i)
            for s in range(6):
                filled[s] += N_EXP // 2
            sp.wait_ge(m.ctl, m.o.ctl + 1)
            n_over = sp.value_load(ctl[0:1, 0:1], min_val=0, max_val=MAX_OVER)
            for s in range(3):
                sp.wait_ge(w_free[s], filled[s] + 1)
            with sp.Fori(0, MAX_OVER) as j:
                with sp.If(n_over > j):
                    e = sp.value_load(ctl[0:1, ds(1 + j, 1)], min_val=0, max_val=N_EXP - 1)
                    sp.wait_ge(m.odone, j + 1)
                    for s in range(3):
                        src = dn[e] if s == 2 else up[e][:, :, 512 * s:512 * s + 512]
                        k = 4 if s == 2 else KD
                        sp.dma_start(ring[s].rearrange("p (k c) -> p k c", k=k), src).then_inc(m.ow, 16)
                sp.drain()

        def moe_gpsimd(pool, l, m):
            pool.wait_ge(m.big, m.o.big + 1)
            pool.dma_start(WR[:, :, 0:4], A["moe_w_grp_2"][l].rearrange("(k p) c -> p k c", p=P)).then_inc(m.wr, 16)
            pool.dma_start(WR[:, :, 4:36], A["moe_w_rt_2"][l].rearrange("(k p) c -> p k c", p=P)).then_inc(m.wr, 16)
            pool.dma_start(BR[:, 0:4], A["moe_b_grp_2"][l].partition_broadcast(P)).then_inc(m.wr, 16)
            pool.dma_start(BR[:, 4:36], A["moe_b_rt_2"][l].partition_broadcast(P)).then_inc(m.wr, 16)
            for t, (t0, n) in enumerate(TOK):
                pool.wait_ge(m.trc, m.o.trc + 2 * t + 2)
                pool.dma_start(rows_d[t0:t0 + n, :], TR[t % 2][0:n, :]).then_inc(m.trs if t % 2 == 0 else m.trs1, 16)
            pool.wait_ge(m.dest, m.o.dest + 1)
            pool.wait_ge(zi, 48)
            pool.wait_ge(zr, 16 * MAX_OVER)
            for t, (t0, n) in enumerate(TOK):
                for s in range(2):
                    pool.indirect_dma_start(out=scratch["slots"][l], out_offset=bass.IndirectOffsetOnAxis(ap=dest[0:n, 2 * t + s:2 * t + s + 1], axis=0),
                                            in_=tokid[0:n, t:t + 1], in_offset=None).then_inc(m.scd, 16)
            pool.wait_ge(m.scd, m.o.scd + 160)
            pairs, over = N_EXP // 2, N_EXP * CAP
            pool.dma_start(IDX, scratch["slots"][l][0:over].rearrange("(q s) a -> s (q a)", s=2 * CAP), allow_slow_non_contiguous=True).then_inc(m.idx, 16)
            pool.dma_start(IDXO, scratch["slots"][l][over:].rearrange("(b s) a -> s (b a)", s=CAP), allow_slow_non_contiguous=True).then_inc(m.idx, 16)
            pool.wait_ge(m.idx, m.o.idx + 32)
            pool.wait_ge(m.trs, m.o.trs + 48)
            pool.wait_ge(m.trs1, m.o.trs1 + 32)

            def gather(u, pair):
                nc.gpsimd.tensor_copy(IC[u].bitcast(I32), IDX[:, ds(pair, 1)])
                pool.drain()
                pool.indirect_dma_start(out=XG[u], out_offset=None, in_=rows_d[:, :],
                                        in_offset=bass.IndirectOffsetOnAxis(ap=IC[u], axis=0)).then_inc((m.xg0, m.xg1)[u], 16)

            pool.wait_ge(m.dest, m.o.dest + 1)
            gather(0, 0)
            gather(1, 1)
            with pool.Fori(0, QUADS - 1) as i:
                for u in range(2):
                    pool.wait_ge(m.xt, m.o.xt + 2 * i + u + 1)
                    tick(pool)
                    gather(u, 2 * i + u + 2)
            pool.wait_ge(m.ctl, m.o.ctl + 1)
            n_over = pool.value_load(ctl[0:1, 0:1], min_val=0, max_val=MAX_OVER)
            pool.wait_ge(m.xt, m.o.xt + N_EXP // 2)
            with pool.Fori(0, MAX_OVER) as j:
                with pool.If(n_over > j):
                    nc.gpsimd.tensor_copy(IC[0][0:CAP].bitcast(I32), IDXO[:, ds(j, 1)])
                    pool.drain()
                    pool.indirect_dma_start(out=XG[0][0:CAP, :], out_offset=None, in_=rows_d[:, :],
                                            in_offset=bass.IndirectOffsetOnAxis(ap=IC[0][0:CAP], axis=0)).then_inc(m.og, 16)
                    pool.wait_ge(m.ost, 16 * (j + 1))
                    tick(pool)
                pool.drain()
            for st in (m.st0, m.st1, m.st2, m.st3):
                pool.wait_ge(st, m.o.st0 + 16 * (QUADS + 1))
            for t, (t0, n) in enumerate(TOK):
                if t >= 2:
                    pool.wait_ge(m.w, m.o.w + t - 1)
                    pool.wait_ge(m.t, m.o.t + 2 * (t - 1))
                for s in range(2):
                    pool.indirect_dma_start(out=YG[t % 2][s][0:n, :], out_offset=None, in_=res_d[:, :],
                                            in_offset=bass.IndirectOffsetOnAxis(ap=dest[0:n, 2 * t + s:2 * t + s + 1], axis=0)).then_inc((m.cg0, m.cg1)[t % 2], 16)

        def moe_tensor(pe, l, m):
            pe.wait_ge(m.wr, m.o.wr + 64)
            for t, (t0, n) in enumerate(TOK):
                for k in range(KD):
                    mm = nc.tensor.matmul(bank(0, 36, 36 * t, n), HT[:, k, t0:t0 + n], WR[:, k, :], start=(k == 0), stop=(k == KD - 1))
            mm.then_inc(m.lg, 1)
            for t, (t0, n) in enumerate(TOK):
                for hf in range(2):
                    q = 2 * t + hf
                    if q >= 2:
                        pe.wait_ge(m.trc, m.o.trc + q - 1)
                    for c in range(4):
                        mm = nc.tensor.transpose(bank(2 + q % 2, P, P * c, n), HT[:, 4 * hf + c, t0:t0 + n], cs("ident"))
                    mm.then_inc(m.trp, 1)
            pe.wait_ge(m.oh, m.o.oh + 1)
            for t in range(5):
                for u in range(t + 1):
                    nc.tensor.matmul(bank(1, 32, 32 * t), cs("upper") if u == t else cs("ones"), AA[:, u, :], start=(u == 0), stop=(u == t))
            for u in range(5):
                mm = nc.tensor.matmul(bank(1, 32, 160), cs("ones"), AA[:, u, :], start=(u == 0), stop=(u == 4))
            mm.then_inc(m.rk, 1)
            pe.wait_ge(m.dest, m.o.dest + 1)

            def up_half(b, xe, w, hf):
                for c in range(4):
                    for k in range(KD):
                        mm = nc.tensor.matmul(bank(2 + b, CAP, 256 * hf + CAP * c), w[:, k, P * c:P * (c + 1)], xe[:, k, :],
                                              start=(k == 0), stop=(k == KD - 1))
                return mm

            def down(b, w):
                for hf in range(2):
                    for k in range(4):
                        mm = nc.tensor.matmul(bank(4 + 2 * b + hf, 512, parts=CAP), HE[b][:, k, :], w[:, k, 512 * hf:512 * hf + 512],
                                              start=(k == 0), stop=(k == 3))
                return mm

            def pair_of_experts(i, u, following):
                pair = 2 * i + u
                pe.wait_ge(m.xe, m.o.xe + pair + 1)
                for b in range(2):
                    for hf in range(2):
                        s = 3 * b + hf
                        await_tile(pe, s, used[s] + pair)
                        mm = up_half(b, XE[u][:, :, CAP * b:CAP * (b + 1)], wview(s, KD, 512), hf)
                        if hf:
                            mm.then_inc(m.up, 1)
                        leave_tile(pe, s)
                if following:
                    n = 1 - u
                    pe.wait_ge((m.xg0, m.xg1)[n], (m.o.xg0, m.o.xg1)[n] + 16 * (i + 1 + u))
                    tick(pe, bank(0, 1, parts=1))
                    for k in range(KD):
                        mm = nc.tensor.transpose(bank(0, P, P * k), XG[n][:, P * k:P * (k + 1)], cs("ident"))
                    mm.then_inc(m.xt, 1)
                for b in range(2):
                    s = 3 * b + 2
                    await_tile(pe, s, used[s] + pair)
                    pe.wait_ge(m.he, m.o.he + 2 * pair + b + 1)
                    pe.wait_ge(m.yc, m.o.yc + 2 * pair + b + 1)
                    tick(pe, bank(4 + 2 * b, 1, parts=1))
                    down(b, wview(s, 4, D)).then_inc(m.y, 1)
                    leave_tile(pe, s)

            pe.wait_ge(m.xg0, m.o.xg0 + 16)
            for k in range(KD):
                mm = nc.tensor.transpose(bank(0, P, P * k), XG[0][:, P * k:P * (k + 1)], cs("ident"))
            mm.then_inc(m.xt, 1)
            with pe.Fori(0, QUADS - 1) as i:
                for u in range(2):
                    pair_of_experts(i, u, True)
            pair_of_experts(QUADS - 1, 0, True)
            pair_of_experts(QUADS - 1, 1, False)
            for s in range(6):
                used[s] += N_EXP // 2
            n_over = pe.value_load(ctl[0:1, 0:1], min_val=0, max_val=MAX_OVER)
            pe.wait_ge(m.yc, m.o.yc + N_EXP + 2)
            pe.drain().then_inc(m.odone, 1)
            with pe.Fori(0, MAX_OVER) as j:
                with pe.If(n_over > j):
                    pe.wait_ge(m.og, 16 * (j + 1))
                    tick(pe, bank(0, 1, parts=1))
                    for k in range(KD):
                        mm = nc.tensor.transpose(bank(0, CAP, CAP * k), XG[0][0:CAP, P * k:P * (k + 1)], cs("ident", 0, CAP, CAP))
                    mm.then_inc(m.ope, 1)
                    pe.wait_ge(m.oact, 2 * j + 1)
                    pe.wait_ge(m.ow, 48 * (j + 1))
                    for hf in range(2):
                        mm = up_half(0, XO, wview(hf, KD, 512), hf)
                    mm.then_inc(m.ope, 1)
                    pe.wait_ge(m.odve, 2 * j + 1)
                    tick(pe, bank(4, 1, parts=1))
                    down(0, wview(2, 4, D)).then_inc(m.ope, 1)
                    pe.wait_ge(m.odve, 2 * j + 2)
                    tick(pe, bank(4, 1, parts=1)).then_inc(m.odone, 1)
                pe.drain()
            for t, (t0, n) in enumerate(TOK):
                pe.wait_ge(m.w, m.o.w + t + 1)
                for hf in range(2):
                    q = 2 * t + hf
                    if q >= 2:
                        pe.wait_ge(m.c, m.o.c + q - 1)
                    for c in range(4):
                        mm = nc.tensor.transpose(bank(q % 2, n, n * c), YG[t % 2][0][0:n, 512 * hf + P * c:512 * hf + P * (c + 1)], cs("ident", 0, n, n))
                    mm.then_inc(m.t, 1)

        def moe_scalar(act, l, m):
            act.wait_ge(m.gx, m.o.gx + 1)
            nc.scalar.activation(GX, GX, ACT.Exp).then_inc(m.gxe, 1)
            act.wait_ge(m.dv, m.o.dv + 1)
            nc.scalar.activation(DV, DV, ACT.Exp).then_inc(m.dve, 1)
            sts = (m.st0, m.st1, m.st2, m.st3)

            def copy_rows(u, pair):
                act.wait_ge(m.xt, m.o.xt + pair + 1)
                nc.scalar.copy(XE[u].rearrange("p k s -> p (k s)"), ps[:, 0:D]).then_inc(m.xe, 1)

            def pair_of_experts(i, u, following):
                for b in range(2):
                    act.wait_ge(m.up, m.o.up + 4 * i + 2 * u + b + 1)
                    nc.scalar.activation(SA[b], bank(2 + b, 4 * CAP), ACT.Silu).then_inc(m.sa, 1)
                if following:
                    copy_rows(1 - u, 2 * i + u + 1)
                for b in range(2):
                    e = 4 * i + 2 * u + b
                    act.wait_ge(m.yc, m.o.yc + e + 3)
                    act.dma_start(res_d[ds(CAP * e, CAP), :], YE[2 * u + b]).then_inc(sts[2 * u + b], 16)

            copy_rows(0, 0)
            with act.Fori(0, QUADS - 1) as i:
                for u in range(2):
                    pair_of_experts(i, u, True)
            pair_of_experts(QUADS - 1, 0, True)
            pair_of_experts(QUADS - 1, 1, False)
            n_over = act.value_load(ctl[0:1, 0:1], min_val=0, max_val=MAX_OVER)
            act.wait_ge(m.st0, m.o.st0 + 16 * (QUADS + 1))
            with act.Fori(0, MAX_OVER) as j:
                with act.If(n_over > j):
                    act.wait_ge(m.ope, 3 * j + 1)
                    nc.scalar.copy(XO.rearrange("p k s -> p (k s)"), bank(0, KD * CAP)).then_inc(m.oact, 1)
                    act.wait_ge(m.ope, 3 * j + 2)
                    nc.scalar.activation(SA[0], bank(2, 4 * CAP), ACT.Silu).then_inc(m.oact, 1)
                    act.wait_ge(m.odve, 2 * j + 2)
                    act.dma_start(res_d[ds(CAP * (N_EXP + j), CAP), :], YE[0]).then_inc(m.ost, 16)
                    act.wait_ge(m.ost, 16 * (j + 1))
                    tick(act)
                act.drain()

        def moe_vector(v, l, m):
            bc = lambda a, n: a.unsqueeze(1).to_broadcast([P, 5, n])
            bk = lambda a, n: a.to_broadcast([P, 5, n])
            iota = cs("iota")
            nc.vector.memset(LG, 0.0)
            nc.vector.memset(G8, NEG)
            nc.vector.memset(ZB, 0.0)
            v.drain()
            v.wait_ge(m.lg, m.o.lg + 1)
            nc.vector.tensor_tensor(LG[:, 0:4, :], bank(0, 144).rearrange("p (t c) -> p t c", t=4), BR.unsqueeze(1).to_broadcast([P, 4, 36]), ALU.add)
            nc.vector.tensor_tensor(LG[0:META, 4, :], bank(0, 36, 144, META), BR[0:META, :], ALU.add)
            v.drain()
            nc.vector.tensor_copy(G8[:, :, 0:4], LG[:, :, 0:4])
            v.drain()
            for t in range(5):
                nc.vector.max(GM8[:, t, :], G8[:, t, :])
            v.drain()
            for t in range(5):
                nc.vector.max_index(GI8[:, t, :], GM8[:, t, :], G8[:, t, :])
            nc.vector.tensor_tensor(GX, LG[:, :, 0:4], bk(GM8[:, :, 0:1], 4), ALU.subtract).then_inc(m.gx, 1)
            v.drain()
            nc.vector.tensor_copy(GIF, GI8[:, :, 0])
            v.drain()
            nc.vector.tensor_tensor(MK, bc(cs("iotag"), 32), bk(GIF.unsqueeze(2), 32), ALU.is_equal)
            v.drain()
            nc.vector.tensor_tensor(ME, LG[:, :, 4:36], MK, ALU.mult)
            nc.vector.tensor_scalar(MK, MK, -NEG, NEG, ALU.mult, ALU.add)
            v.drain()
            nc.vector.tensor_tensor(ME, ME, MK, ALU.add)
            v.drain()
            for t in range(5):
                nc.vector.max(EM8[:, t, :], ME[:, t, :])
            v.drain()
            for t in range(5):
                nc.vector.max_index(EI8[:, t, :], EM8[:, t, :], ME[:, t, :])
            nc.vector.tensor_tensor(DV.unsqueeze(2), EM8[:, :, 1:2], EM8[:, :, 0:1], ALU.subtract).then_inc(m.dv, 1)
            v.drain()
            nc.vector.tensor_copy(IF2, EI8[:, :, 0:2])
            v.drain()
            for s in range(2):
                nc.vector.tensor_tensor(OH[s], bc(iota, 32), bk(IF2[:, :, s:s + 1], 32), ALU.is_equal)
            v.drain()
            for s in range(2):
                nc.vector.tensor_tensor(OH[s], OH[s], bk(cs("valid").unsqueeze(2), 32), ALU.mult)
            v.drain()
            nc.vector.tensor_tensor(AA, OH[0], OH[1], ALU.add).then_inc(m.oh, 1)
            for q in range(10):
                t, hf = q // 2, q % 2
                n = TOK[t][1]
                v.wait_ge(m.trp, m.o.trp + q + 1)
                if t >= 2 and hf == 0:
                    v.wait_ge((m.trs, m.trs1)[t % 2], (m.o.trs, m.o.trs1)[t % 2] + 16 * (t // 2))
                nc.vector.tensor_copy(TR[t % 2][0:n, 512 * hf:512 * hf + 512], bank(2 + q % 2, 512, parts=n)).then_inc(m.trc, 1)
            v.wait_ge(m.gxe, m.o.gxe + 1)
            nc.vector.tensor_reduce(GG, GX, AX, ALU.add)
            v.wait_ge(m.dve, m.o.dve + 1)
            nc.vector.tensor_scalar(GIF, DV, 1.0, None, ALU.add)
            v.drain()
            nc.vector.tensor_tensor(GG, GG, GIF, ALU.mult)
            v.drain()
            nc.vector.reciprocal(gate[:, :, 0], GG)
            v.drain()
            nc.vector.tensor_tensor(gate[:, :, 1], gate[:, :, 0], DV, ALU.mult)
            v.wait_ge(m.rk, m.o.rk + 1)
            nc.vector.tensor_copy(RK_, bank(1, 160).rearrange("p (t c) -> p t c", t=5))
            nc.vector.tensor_copy(CN, bank(1, 32, 160))
            nc.vector.memset(OV, 0.0)
            for j in range(1, OVER_STEPS + 1):
                v.drain()
                nc.vector.scalar_tensor_tensor(OV, CN, float(CAP * j), OV, ALU.is_gt, ALU.add)
            v.drain()
            nc.vector.tensor_tensor_scan(INC, ZB, OV, 0.0, ALU.add, ALU.add)
            v.drain()
            nc.vector.tensor_tensor(BS, INC, OV, ALU.subtract)
            v.drain()
            nc.vector.tensor_tensor(BS, BS, iota, ALU.subtract)
            v.drain()
            nc.vector.tensor_scalar(BS, BS, float(CAP), float(CAP * (N_EXP - 1)), ALU.mult, ALU.add)
            nc.vector.tensor_scalar(MK, RK_, float(CAP), None, ALU.is_ge)
            v.drain()
            nc.vector.tensor_tensor(MK, MK, bc(BS, 32), ALU.mult)
            nc.vector.tensor_scalar(OV, iota, float(CAP), None, ALU.mult)
            v.drain()
            nc.vector.tensor_tensor(RK_, RK_, MK, ALU.add)
            v.drain()
            nc.vector.tensor_tensor(RK_, RK_, bc(OV, 32), ALU.add)
            v.drain()
            for s in range(2):
                nc.vector.tensor_tensor(OH[s], OH[s], RK_, ALU.mult)
            v.drain()
            for s in range(2):
                nc.vector.tensor_reduce(DF[:, :, s], OH[s], AX, ALU.add)
            nc.vector.tensor_tensor(OX, INC[0:1, :].unsqueeze(1).to_broadcast([1, MAX_OVER, 32]),
                                    cs("iota", 0, MAX_OVER, 1).unsqueeze(2).to_broadcast([1, MAX_OVER, 32]), ALU.is_le)
            nc.vector.tensor_copy(CF[:, 0:1], INC[0:1, 31:32])
            v.drain()
            nc.vector.tensor_copy(dest[:, :], DF.rearrange("p t s -> p (t s)"))
            nc.vector.tensor_reduce(CF[:, 1:], OX, AX, ALU.add)
            v.drain()
            nc.vector.tensor_scalar(CF[:, 1:], CF[:, 1:], float(N_EXP - 1), None, ALU.min)
            v.drain()
            nc.vector.tensor_copy(ctl[:, :], CF)
            v.drain().then_inc(m.ctl, 1)
            v.drain().then_inc(m.dest, 1)
            v.drain().then_inc(m.yc, 2)
            sts = (m.st0, m.st1, m.st2, m.st3)
            for st in sts:
                v.drain().then_inc(st, 16)

            with v.Fori(0, QUADS) as i:
                for u in range(2):
                    for b in range(2):
                        v.wait_ge(m.sa, m.o.sa + 4 * i + 2 * u + b + 1)
                        nc.vector.tensor_tensor(HE[b].rearrange("p k s -> p (k s)"), SA[b], bank(2 + b, 4 * CAP, 256), ALU.mult).then_inc(m.he, 1)
                    for b in range(2):
                        q = 2 * u + b
                        v.wait_ge(m.y, m.o.y + 4 * i + q + 1)
                        v.wait_ge(sts[q], m.o.st0 + 16 * (i + 1))
                        nc.vector.tensor_copy(YE[q], ps[0:CAP, 512 * (4 + 2 * b):512 * (6 + 2 * b)]).then_inc(m.yc, 1)
            n_over = v.value_load(ctl[0:1, 0:1], min_val=0, max_val=MAX_OVER)
            v.wait_ge(m.st0, m.o.st0 + 16 * (QUADS + 1))
            with v.Fori(0, MAX_OVER) as j:
                with v.If(n_over > j):
                    v.wait_ge(m.oact, 2 * j + 2)
                    nc.vector.tensor_tensor(HE[0].rearrange("p k s -> p (k s)"), SA[0], bank(2, 4 * CAP, 256), ALU.mult).then_inc(m.odve, 1)
                    v.wait_ge(m.ope, 3 * j + 3)
                    nc.vector.tensor_copy(YE[0], ps[0:CAP, 2048:3072]).then_inc(m.odve, 1)
                    v.wait_ge(m.ost, 16 * (j + 1))
                    tick(v)
                v.drain()
            for t, (t0, n) in enumerate(TOK):
                v.wait_ge((m.cg0, m.cg1)[t % 2], (m.o.cg0, m.o.cg1)[t % 2] + 32 * (t // 2 + 1))
                Y = YG[t % 2]
                nc.vector.tensor_scalar(Y[0][0:n, :], Y[0][0:n, :], gate[0:n, t, 0:1], None, ALU.mult)
                v.drain()
                nc.vector.scalar_tensor_tensor(Y[0][0:n, :], Y[1][0:n, :], gate[0:n, t, 1:2], Y[0][0:n, :], ALU.mult, ALU.add).then_inc(m.w, 1)
                for hf in range(2):
                    q = 2 * t + hf
                    v.wait_ge(m.t, m.o.t + q + 1)
                    nc.vector.tensor_tensor(XT[:, 4 * hf:4 * hf + 4, t0:t0 + n], XT[:, 4 * hf:4 * hf + 4, t0:t0 + n],
                                            bank(q % 2, 4 * n).rearrange("p (c t) -> p c t", c=4), ALU.add).then_inc(m.c, 1)
            v.drain()

        nb = [norm_use(q) for q in range(4, 8)]
        gate2 = sem("big_free2")
        ff_ = att_use(1)
        mo = [moe_use(l) for l in range(2)]
        fruns = [(8, lambda i: FQ[:, i, :], lambda i: FQ[:, i, :], gains[:, 1:2], True, False),
                 (8, lambda i: FK[:, i, :], lambda i: FK[:, i, :], pcol("fk_g"), True, False)]
        hruns = [(8, lambda i: HQ[:, i, :], lambda i: HQ[:, i, :], pcol("hg_o"), True, False)]

        def gain_of(name, l):
            return lambda k, gi: pcol(name, 8 * l + k)

        def block2_sync(sp):
            w = A["fox_w_in_2"][0].rearrange("(k p) c -> p k c", p=P)
            proj_sync(sp, w, range(0, 3 * D, 512), FOX_SLOTS)
            outproj_sync(sp, A["fox_w_out_2"][0])
            moe_sync(sp, 0, mo[0])
            w = A["hg_w_in_2"][0].rearrange("(k p) c -> p k c", p=P)
            proj_sync(sp, w, range(0, 4 * D, 512), HG_SLOTS)
            outproj_sync(sp, A["hg_w_out_2"][0])
            moe_sync(sp, 1, mo[1])

        def block2_gpsimd(pool):
            meta_gpsimd(pool, gate2)
            fox_gpsimd(pool)
            heads_gpsimd(pool, hf_, fruns, T2)
            moe_gpsimd(pool, 0, mo[0])
            heads_gpsimd(pool, hh_, hruns, T2)
            moe_gpsimd(pool, 1, mo[1])

        def block2_scalar(act):
            norm_scalar(act, nb[0], T2, G_T2, gain_of("fox_norm", 0), None)
            fox_proj_scalar(act)
            heads_scalar(act, hf_, fruns, T2, HD)
            fox_att_scalar(act, ff_)
            norm_scalar(act, nb[1], T2, G_T2, gain_of("moe_norm", 0), None)
            moe_scalar(act, 0, mo[0])
            norm_scalar(act, nb[2], T2, G_T2, gain_of("hg_norm", 0), None)
            hg_proj_scalar(act, gh)
            hg_scalar(act)
            heads_scalar(act, hh_, hruns, T2, P)
            hg_gate_scalar(act, ghg)
            norm_scalar(act, nb[3], T2, G_T2, gain_of("moe_norm", 1), None)
            moe_scalar(act, 1, mo[1])

        def block2_tensor(pe):
            meta_tensor(pe)
            norm_tensor(pe, nb[0], T2)
            fox_proj_tensor(pe, gf)
            heads_tensor(pe, hf_, fruns, T2, cs("blk"))
            fox_att_tensor(pe, ff_)
            outproj_tensor(pe, gof, T2, hrhs)
            norm_tensor(pe, nb[1], T2)
            moe_tensor(pe, 0, mo[0])
            norm_tensor(pe, nb[2], T2)
            hg_proj_tensor(pe, gh)
            hg_tensor(pe)
            heads_tensor(pe, hh_, hruns, T2, cs("ones"))
            hg_gate_tensor(pe, ghg)
            outproj_tensor(pe, goh, T2, lambda k: HQ[:, k, :])
            norm_tensor(pe, nb[3], T2)
            moe_tensor(pe, 1, mo[1])

        def block2_vector(v):
            v.drain().then_inc(gate2, 1)
            meta_vector(v)
            norm_vector(v, nb[0], T2)
            fox_proj_vector(v, gf)
            heads_vector(v, hf_, fruns, T2, HD)
            fox_att_vector(v, ff_)
            outproj_vector(v, gof, T2, G_T2, None)
            v.drain().then_inc(mo[0].big, 1)
            norm_vector(v, nb[1], T2)
            moe_vector(v, 0, mo[0])
            norm_vector(v, nb[2], T2)
            hg_proj_vector(v, gh)
            hg_vector(v)
            heads_vector(v, hh_, hruns, T2, P)
            hg_gate_vector(v, ghg)
            outproj_vector(v, goh, T2, G_T2, None)
            v.drain().then_inc(mo[1].big, 1)
            norm_vector(v, nb[3], T2)
            moe_vector(v, 1, mo[1])

        n1, n2, n3, n4 = (norm_use(q) for q in range(4))
        g0, go0, dn0, g1, go1, dn1, gf, gof, gh, ghg, goh = (proj_use(n, o) for n, o in (
            (26, 0), (8, 1), (8, 0), (18, 0), (8, 1), (8, 0), (26, 0), (8, 1), (26, 0), (8, 0), (8, 1)))
        at0 = att_use(0)
        f0, f1 = ffn_use(0), ffn_use(1)
        gate1 = sem("big_free1")
        pl = sems("pool", "y mm done")
        rt = sems("ret", "att_free e1 e1v e2 s pv af o oc gate gated")
        zq = with_dst(l0_runs(), [lambda i: Z[:, 4 + i, :], lambda i: Z[:, 8 + i, :]])
        zo = [(4, lambda i: HT[:, 4 + i, :], lambda i: HT[:, 4 + i, :], gains[:, 2:3], True, False)]
        rq = [(2, lambda i: RQ[:, i, :], lambda i: RQ[:, i, :], gains[:, 3:4], False, True)]
        rk = [(2, lambda i: RK[:, i, :], lambda i: RK[:, i, :], 1.0, False, True)]
        ro = [(4, lambda i: HT[:, 4 + i, 0:SEQ], lambda i: HT[:, 4 + i, 0:SEQ], pcol("ret_gn"), True, False)]
        hd0, hd1, hdr, hdk, hdo, hf_, hh_ = (heads_use(r) for r in (zq, zo, rq, rk, ro, fruns, hruns))

        def y0(k):
            return Z[:, k, :] if k < 4 else HT[:, k, :]

        def scale_of(G, l):
            return lambda k, gi: G[:, l, k, gi:gi + 1]

        def shift_of(l, part):
            return lambda k, gi: modT[:, l, 8 * part + k, gi:gi + 1]

        def gate_of(l, part):
            return lambda m, gi: modT[:, l, 8 * part + m, gi:gi + 1]

        block = ctx.enter_context(nc.Block())

        @block.sync
        def _(sp):
            mod_sync(sp)
            l0_sync(sp)
            outproj_sync(sp, A["ev_w_out"][0])
            ffn_sync(sp, 0)
            down_sync(sp, 0)
            l1_sync(sp)
            outproj_sync(sp, A["od_w_out"][0])
            ffn_sync(sp, 1)
            down_sync(sp, 1)
            block2_sync(sp)
            tokout_sync(sp)

        @block.gpsimd
        def _(pool):
            prep_gpsimd(pool)
            tokin_gpsimd(pool)
            pool.dma_start(tokid[:, :], K["tokid"]).then_inc(zi, 16)
            for l in range(DEPTH):
                pool.dma_start(scratch["slots"][l].rearrange("(b s) a -> s (b a)", s=CAP), K["zeros_i"], allow_slow_non_contiguous=True).then_inc(zi, 16)
            for j in range(MAX_OVER):
                pool.dma_start(scratch["results"][CAP * (N_EXP + j):CAP * (N_EXP + j + 1), :], K["zero_rows"]).then_inc(zr, 16)
            heads_gpsimd(pool, hd0, zq, TC)
            heads_gpsimd(pool, hd1, zo, TC)
            l1_gpsimd(pool, gate1)
            heads_gpsimd(pool, hdo, ro, SEQ)
            block2_gpsimd(pool)

        @block.scalar
        def _(act):
            prep_scalar(act)
            mod_scalar(act)
            norm_scalar(act, n1, TC, G_ALL, scale_of(G1, 0), shift_of(0, 0))
            heads_scalar(act, hd0, zq, TC, HD)
            l0_att_scalar(act, at0)
            heads_scalar(act, hd1, zo, TC, P)
            norm_scalar(act, n2, TC, G_ALL, scale_of(G2, 0), shift_of(0, 3))
            ffn_scalar(act, f0, 0, TC)
            norm_scalar(act, n3, TC, G_ALL, scale_of(G1, 1), shift_of(1, 0))
            ret_scalar(act, rt)
            heads_scalar(act, hdo, ro, SEQ, P)
            act.wait_ge(rt.gate, 1)
            nc.scalar.activation(RG, RG, ACT.Silu).then_inc(rt.gated, 1)
            norm_scalar(act, n4, SEQ, G_LAT, scale_of(G2, 1), shift_of(1, 3))
            ffn_scalar(act, f1, 1, SEQ)
            block2_scalar(act)

        @block.tensor
        def _(pe):
            prep_tensor(pe)
            tokin_tensor(pe)
            mod_tensor(pe)
            norm_tensor(pe, n1, TC)
            l0_tensor(pe, g0)
            heads_tensor(pe, hd0, zq, TC, cs("blk"))
            l0_att_tensor(pe, at0)
            heads_tensor(pe, hd1, zo, TC, cs("ones"))
            outproj_tensor(pe, go0, TC, y0)
            norm_tensor(pe, n2, TC)
            ffn_tensor(pe, f0, TC)
            down_tensor(pe, f0, dn0, TC)
            norm_tensor(pe, n3, TC)
            l1_tensor(pe, g1)
            pool_tensor(pe, pl)
            heads_tensor(pe, hdr, rq, SEQ, None)
            heads_tensor(pe, hdk, rk, TC, None)
            ret_tensor(pe, rt)
            heads_tensor(pe, hdo, ro, SEQ, cs("ones"))
            outproj_tensor(pe, go1, SEQ, hrhs)
            norm_tensor(pe, n4, SEQ)
            ffn_tensor(pe, f1, SEQ)
            down_tensor(pe, f1, dn1, SEQ)
            block2_tensor(pe)
            tokout_tensor(pe)

        @block.vector
        def _(v):
            prep_vector(v)
            tokin_vector(v)
            mod_vector(v)
            norm_vector(v, n1, TC)
            l0_vector(v, g0)
            heads_vector(v, hd0, zq, TC, HD)
            l0_att_vector(v, at0)
            heads_vector(v, hd1, zo, TC, P)
            outproj_vector(v, go0, TC, G_ALL, gate_of(0, 2))
            norm_vector(v, n2, TC)
            ffn_vector(v, f0, 0, TC, G_ALL)
            down_vector(v, dn0, 0, TC, G_ALL)
            v.drain().then_inc(gate1, 1)
            norm_vector(v, n3, TC)
            l1_vector(v, g1)
            pool_vector(v, pl)
            heads_vector(v, hdr, rq, SEQ, HD)
            heads_vector(v, hdk, rk, TC, HD)
            ret_vector(v, rt)
            heads_vector(v, hdo, ro, SEQ, P)
            v.drain().then_inc(rt.gate, 1)
            v.wait_ge(rt.gated, 1)
            nc.vector.tensor_tensor(HT[:, 4:8, 0:SEQ], HT[:, 4:8, 0:SEQ], RG, ALU.mult)
            outproj_vector(v, go1, SEQ, G_LAT, gate_of(1, 2))
            norm_vector(v, n4, SEQ)
            ffn_vector(v, f1, 1, SEQ, G_LAT)
            down_vector(v, dn1, 1, SEQ, G_LAT)
            block2_vector(v)
            tokout_vector(v)


def kernel(**inputs):
    import concourse.bacc as bacc
    from concourse.bass_utils import run_bass_kernel_spmd

    nc = bacc.Bacc("TRN2", target_bir_lowering=False, num_devices=1)
    arrays, A, K = {}, {}, {}
    for name, value in inputs.items():
        a = np.ascontiguousarray(value)
        arrays[f"in_{name}"] = a
        A[name] = nc.dram_tensor(f"in_{name}", a.shape, mybir.dt.from_np(a.dtype), kind="ExternalInput").ap()
    for name, a in shape_constants().items():
        arrays[f"const_{name}"] = a
        K[name] = nc.dram_tensor(f"const_{name}", a.shape, mybir.dt.from_np(a.dtype), kind="ExternalInput").ap()
    out = nc.dram_tensor("out_0", (1, SEQ, D), F32, kind="ExternalOutput").ap()
    scratch = {
        "rows": nc.dram_tensor("expert_in", (T2, D), F32).ap(),
        "results": nc.dram_tensor("expert_out", ((N_EXP + MAX_OVER) * CAP, D), F32).ap(),
        "slots": [nc.dram_tensor(f"slot_token{l}", ((N_EXP + MAX_OVER) * CAP, 1), I32).ap() for l in range(DEPTH)],
    }
    build(nc, A, K, out, scratch)
    got = run_bass_kernel_spmd(nc, [arrays], core_ids=[0])
    return got.results[0]["out_0"]
```
